# Optimizing a Trainium2 kernel written in Bass

```python
import math
import jax, jax.numpy as jnp
from jax import lax
import numpy as np

D_MODEL = 1024
BATCH = 1
SEQ = 256
DEPTH = 2

N_MIXERS = 3
Q_BLOCK = 128
ROPE_THETA = 10000.0
EPS = 1e-6
MAX_POS_OFFSET = 1024

SB_HEADS = 16
SB_HEAD_DIM = D_MODEL // SB_HEADS

MLA_HEADS = 16
MLA_Q_RANK = 384
MLA_KV_RANK = 256
MLA_NOPE = 64
MLA_ROPE = 32
MLA_V = 64

DIFF_HEADS = 8
DIFF_HEAD_DIM = D_MODEL // (2 * DIFF_HEADS)

N_GROUPS = 4
EXPERTS_PER_GROUP = 4
N_EXPERTS = N_GROUPS * EXPERTS_PER_GROUP
EXPERT_TOPK = 2
EXPERT_FF = 512

kernel_name = 'hybrid_sb_mla_diff_hmoe_adaln'

def rmsnorm(x, g):
    xf = x.astype(jnp.float32)
    y = xf * lax.rsqrt(jnp.mean(xf * xf, axis=-1, keepdims=True) + EPS)
    return (y * g.astype(jnp.float32)).astype(x.dtype)

def rope_tables(positions, dim):
    inv_freq = ROPE_THETA ** (-jnp.arange(0, dim, 2, dtype=jnp.float32) / dim)
    ang = positions.astype(jnp.float32)[..., None] * inv_freq
    return jnp.cos(ang), jnp.sin(ang)

def apply_rope(t, cos, sin):
    c = cos[:, None].astype(t.dtype)
    s = sin[:, None].astype(t.dtype)
    t1, t2 = jnp.split(t, 2, axis=-1)
    return jnp.concatenate([t1 * c - t2 * s, t2 * c + t1 * s], axis=-1)

def split_heads(t, n):
    b, s, _ = t.shape
    return t.reshape(b, s, n, -1).transpose(0, 2, 1, 3)

def merge_heads(t):
    b, h, s, d = t.shape
    return t.transpose(0, 2, 1, 3).reshape(b, s, h * d)

def block_mask(start, seq, strict):
    q_pos = start + jnp.arange(Q_BLOCK, dtype=jnp.int32)
    k_pos = jnp.arange(seq, dtype=jnp.int32)
    if strict:
        return k_pos[None, :] < q_pos[:, None]
    return k_pos[None, :] <= q_pos[:, None]

def sweep_query_blocks(fn, qs):
    b, _, s, _ = qs[0].shape
    nb = s // Q_BLOCK
    blocks = tuple(q.reshape(q.shape[0], q.shape[1], nb, Q_BLOCK, q.shape[3]).transpose(2, 0, 1, 3, 4) for q in qs)
    starts = jnp.arange(nb, dtype=jnp.int32) * Q_BLOCK
    out = lax.map(lambda a: fn(a[0], *a[1]), (starts, blocks))
    return out.transpose(1, 2, 0, 3, 4).reshape(b, out.shape[2], s, out.shape[-1])

def stick_breaking_attention(h, w_qkv, w_o):
    q, k, v = jnp.split(h @ w_qkv, 3, axis=-1)
    q, k, v = (split_heads(t, SB_HEADS) for t in (q, k, v))
    seq = k.shape[2]
    scale = SB_HEAD_DIM ** -0.5

    def blk(start, qb):
        z = jnp.einsum('bhqd,bhkd->bhqk', qb, k).astype(jnp.float32) * scale
        mask = block_mask(start, seq, True)
        log_beta = jax.nn.log_sigmoid(z)
        log_one_minus = jnp.where(mask, jax.nn.log_sigmoid(-z), 0.0)
        log_stick = lax.cumsum(log_one_minus, axis=3, reverse=True) - log_one_minus
        a = jnp.where(mask, jnp.exp(log_beta + log_stick), 0.0)
        return jnp.einsum('bhqk,bhkd->bhqd', a.astype(v.dtype), v)

    return merge_heads(sweep_query_blocks(blk, (q,))) @ w_o

def latent_attention(h, cos, sin, w_in, g_q, g_kv, w_q_up, w_kv_up, w_o):
    lat = h @ w_in
    c_q = rmsnorm(lat[..., :MLA_Q_RANK], g_q)
    c_kv = rmsnorm(lat[..., MLA_Q_RANK:MLA_Q_RANK + MLA_KV_RANK], g_kv)
    k_rope = apply_rope(lat[:, None, :, MLA_Q_RANK + MLA_KV_RANK:], cos, sin)[:, 0]
    q = split_heads(c_q @ w_q_up, MLA_HEADS)
    q_nope = q[..., :MLA_NOPE]
    q_rope = apply_rope(q[..., MLA_NOPE:], cos, sin)
    kv = split_heads(c_kv @ w_kv_up, MLA_HEADS)
    k_nope, v = kv[..., :MLA_NOPE], kv[..., MLA_NOPE:]
    seq = k_nope.shape[2]
    scale = (MLA_NOPE + MLA_ROPE) ** -0.5

    def blk(start, qn, qr):
        s = (jnp.einsum('bhqd,bhkd->bhqk', qn, k_nope)
             + jnp.einsum('bhqr,bkr->bhqk', qr, k_rope)).astype(jnp.float32) * scale
        s = jnp.where(block_mask(start, seq, False), s, -jnp.inf)
        p = jax.nn.softmax(s, axis=-1)
        return jnp.einsum('bhqk,bhkd->bhqd', p.astype(v.dtype), v)

    return merge_heads(sweep_query_blocks(blk, (q_nope, q_rope))) @ w_o

def differential_attention(h, cos, sin, w_qkv, lam_q1, lam_k1, lam_q2, lam_k2, g_sub, w_o, lambda_init):
    q, k, v = jnp.split(h @ w_qkv, 3, axis=-1)
    q = apply_rope(split_heads(q, 2 * DIFF_HEADS), cos, sin)
    k = apply_rope(split_heads(k, 2 * DIFF_HEADS), cos, sin)
    v = split_heads(v, DIFF_HEADS)
    f32 = jnp.float32
    lam = (jnp.exp(jnp.sum(lam_q1.astype(f32) * lam_k1.astype(f32)))
           - jnp.exp(jnp.sum(lam_q2.astype(f32) * lam_k2.astype(f32))) + lambda_init)
    b, seq = k.shape[0], k.shape[2]
    scale = DIFF_HEAD_DIM ** -0.5

    def blk(start, qb):
        s = jnp.einsum('bhqd,bhkd->bhqk', qb, k).astype(f32) * scale
        s = jnp.where(block_mask(start, seq, False), s, -jnp.inf)
        p = jax.nn.softmax(s, axis=-1).reshape(b, DIFF_HEADS, 2, Q_BLOCK, seq)
        a = p[:, :, 0] - lam * p[:, :, 1]
        return jnp.einsum('bhqk,bhkd->bhqd', a.astype(v.dtype), v)

    o = sweep_query_blocks(blk, (q,))
    o = rmsnorm(o, g_sub) * (1.0 - lambda_init)
    return merge_heads(o) @ w_o

def hierarchical_moe(h, w_group, b_group, w_router, b_router, w_gate_up, w_down):
    f32 = jnp.float32
    g_logits = (h @ w_group).astype(f32) + b_group.astype(f32)
    g_prob = jax.nn.softmax(g_logits, axis=-1)
    g_w, g_idx = lax.top_k(g_prob, 1)
    e_logits = ((h @ w_router).astype(f32) + b_router.astype(f32)).reshape(
        h.shape[0], h.shape[1], N_GROUPS, EXPERTS_PER_GROUP)
    g_onehot = jax.nn.one_hot(g_idx[..., 0], N_GROUPS, dtype=f32)
    e_in_group = jnp.sum(e_logits * g_onehot[..., None], axis=-2)
    top_logit, top_local = lax.top_k(e_in_group, EXPERT_TOPK)
    top_w = jax.nn.softmax(top_logit, axis=-1) * g_w
    expert_id = g_idx * EXPERTS_PER_GROUP + top_local
    gates = jnp.sum(jax.nn.one_hot(expert_id, N_EXPERTS, dtype=f32) * top_w[..., None], axis=-2)
    out = jnp.zeros_like(h)
    for e in range(N_EXPERTS):
        gt, up = jnp.split(h @ w_gate_up[e], 2, axis=-1)
        out = out + gates[..., e:e + 1].astype(h.dtype) * ((jax.nn.silu(gt) * up) @ w_down[e])
    return out

def diff_lambda_init(layer):
    return 0.8 - 0.6 * math.exp(-0.3 * layer)

def setup_inputs(seed: int = 0) -> dict:
    key = jax.random.key(seed)
    ks = iter(jax.random.split(key, 40))

    def nrm(shape, scale):
        return jax.random.normal(next(ks), shape, jnp.float32) * scale

    D = D_MODEL
    n_sb = len(range(0, DEPTH, N_MIXERS))
    n_mla = len(range(1, DEPTH, N_MIXERS))
    n_diff = len(range(2, DEPTH, N_MIXERS))
    x = nrm((BATCH, SEQ, D), 1.0)
    c = nrm((BATCH, D), 1.0)
    positions = jnp.arange(SEQ, dtype=jnp.int32)[None, :] + jax.random.randint(
        next(ks), (BATCH, 1), 0, MAX_POS_OFFSET, dtype=jnp.int32)
    gate_offset = jnp.zeros((6 * D,), jnp.float32).at[2 * D:3 * D].set(1.0).at[5 * D:].set(1.0)
    lat_w = MLA_Q_RANK + MLA_KV_RANK + MLA_ROPE
    return {
        'x': x,
        'c': c,
        'positions': positions,
        'norm_mix_g': 1.0 + nrm((DEPTH, D), 0.1),
        'norm_ffn_g': 1.0 + nrm((DEPTH, D), 0.1),
        'ada_w': nrm((DEPTH, D, 6 * D), 0.1 * D ** -0.5),
        'ada_b': nrm((DEPTH, 6 * D), 0.02) + gate_offset,
        'sb_w_qkv': nrm((n_sb, D, 3 * D), D ** -0.5),
        'sb_w_o': nrm((n_sb, D, D), D ** -0.5),
        'mla_w_in': nrm((n_mla, D, lat_w), D ** -0.5),
        'mla_g_q': 1.0 + nrm((n_mla, MLA_Q_RANK), 0.1),
        'mla_g_kv': 1.0 + nrm((n_mla, MLA_KV_RANK), 0.1),
        'mla_w_q_up': nrm((n_mla, MLA_Q_RANK, MLA_HEADS * (MLA_NOPE + MLA_ROPE)), MLA_Q_RANK ** -0.5),
        'mla_w_kv_up': nrm((n_mla, MLA_KV_RANK, MLA_HEADS * (MLA_NOPE + MLA_V)), MLA_KV_RANK ** -0.5),
        'mla_w_o': nrm((n_mla, MLA_HEADS * MLA_V, D), (MLA_HEADS * MLA_V) ** -0.5),
        'diff_w_qkv': nrm((n_diff, D, 3 * D), D ** -0.5),
        'diff_lam_q1': nrm((n_diff, DIFF_HEAD_DIM), 0.1),
        'diff_lam_k1': nrm((n_diff, DIFF_HEAD_DIM), 0.1),
        'diff_lam_q2': nrm((n_diff, DIFF_HEAD_DIM), 0.1),
        'diff_lam_k2': nrm((n_diff, DIFF_HEAD_DIM), 0.1),
        'diff_g_sub': 1.0 + nrm((n_diff, 2 * DIFF_HEAD_DIM), 0.1),
        'diff_w_o': nrm((n_diff, D, D), D ** -0.5),
        'moe_w_group': nrm((DEPTH, D, N_GROUPS), D ** -0.5),
        'moe_b_group': nrm((DEPTH, N_GROUPS), 0.01),
        'moe_w_router': nrm((DEPTH, D, N_EXPERTS), D ** -0.5),
        'moe_b_router': nrm((DEPTH, N_EXPERTS), 0.01),
        'moe_w_gate_up': nrm((DEPTH, N_EXPERTS, D, 2 * EXPERT_FF), D ** -0.5),
        'moe_w_down': nrm((DEPTH, N_EXPERTS, EXPERT_FF, D), EXPERT_FF ** -0.5),
        'final_g': 1.0 + nrm((D,), 0.1),
    }

def reference(x, c, positions, norm_mix_g, norm_ffn_g, ada_w, ada_b,
              sb_w_qkv, sb_w_o,
              mla_w_in, mla_g_q, mla_g_kv, mla_w_q_up, mla_w_kv_up, mla_w_o,
              diff_w_qkv, diff_lam_q1, diff_lam_k1, diff_lam_q2, diff_lam_k2, diff_g_sub, diff_w_o,
              moe_w_group, moe_b_group, moe_w_router, moe_b_router, moe_w_gate_up, moe_w_down,
              final_g):
    cos_mla, sin_mla = rope_tables(positions, MLA_ROPE)
    cos_diff, sin_diff = rope_tables(positions, DIFF_HEAD_DIM)
    c_act = jax.nn.silu(c)
    for i in range(DEPTH):
        mod = (c_act @ ada_w[i] + ada_b[i])[:, None, :]
        sh_m, sc_m, gt_m, sh_f, sc_f, gt_f = jnp.split(mod, 6, axis=-1)
        h = rmsnorm(x, norm_mix_g[i]) * (1.0 + sc_m) + sh_m
        kind, j = i % N_MIXERS, i // N_MIXERS
        if kind == 0:
            y = stick_breaking_attention(h, sb_w_qkv[j], sb_w_o[j])
        elif kind == 1:
            y = latent_attention(h, cos_mla, sin_mla, mla_w_in[j], mla_g_q[j], mla_g_kv[j],
                                 mla_w_q_up[j], mla_w_kv_up[j], mla_w_o[j])
        else:
            y = differential_attention(h, cos_diff, sin_diff, diff_w_qkv[j], diff_lam_q1[j], diff_lam_k1[j],
                                       diff_lam_q2[j], diff_lam_k2[j], diff_g_sub[j], diff_w_o[j],
                                       diff_lambda_init(i))
        x = x + gt_m * y
        h = rmsnorm(x, norm_ffn_g[i]) * (1.0 + sc_f) + sh_f
        x = x + gt_f * hierarchical_moe(h, moe_w_group[i], moe_b_group[i], moe_w_router[i], moe_b_router[i],
                                        moe_w_gate_up[i], moe_w_down[i])
    return rmsnorm(x, final_g)


_drawn_inputs = setup_inputs


def setup_inputs(seed=0):
    import zlib

    import numpy as np

    out = dict(_drawn_inputs(seed))
    spreads = {}
    factors = {'moe_b_router': 12.466}
    for name, (base, spread) in spreads.items():
        noise = np.random.default_rng([zlib.crc32(name.encode()), seed]).standard_normal(out[name].shape)
        drawn = base * np.exp(spread * noise) if base else spread * noise
        out[name] = __import__('jax').numpy.asarray(drawn.astype(out[name].dtype))
    for name, factor in factors.items():
        out[name] = (out[name] * factor).astype(out[name].dtype)
    return out
```

```python
from contextlib import ExitStack

import concourse.bass as bass
import numpy as np
from concourse import mybir

F32 = mybir.dt.float32
I32 = mybir.dt.int32
ALU = mybir.AluOpType
ACT = mybir.ActivationFunctionType
AX = mybir.AxisListType

P = 128
D = 1024
T = 256
KD = D // P
TT = T // P
HEADS = 16
DH = 64
QR, KVR, ROPE = 384, 256, 32
QK = DH + ROPE
NE, NG, EPG = 16, 4, 4
FF = 512
MOD = 6 * D // P
EPS = 1e-6
THETA = 10000.0
NEG = -1.0e30
SLOTS = 8
SLOT = 4096
TQKV = 0
TWO0 = 20
TLAT = TWO0 + 8
TUP = TLAT + 6
TROT = TUP + 12
TKV = TROT + 5
TWO1 = TKV + 12
TEND = TWO1 + 8


def build(nc, x, c, positions, norm_mix_g, norm_ffn_g, ada_w, ada_b, sb_w_qkv, sb_w_o,
          mla_w_in, mla_g_q, mla_g_kv, mla_w_q_up, mla_w_kv_up, mla_w_o,
          moe_w_group, moe_b_group, moe_w_router, moe_b_router, moe_w_gate_up, moe_w_down,
          final_g, inv_freq, out):
    owner = []
    for j in range(TEND):
        alone = TWO0 <= j < TLAT or TUP + 8 <= j < TKV or j >= TWO1
        owner.append("v" if alone or j % 2 == 0 else "a")
    nth = [owner[:j + 1].count(owner[j]) for j in range(TEND)]

    stream = []
    uses = [0] * SLOTS
    where = {}

    def chunk(name, slot, src, k, n):
        uses[slot] += 1
        where[name] = (slot, uses[slot], k, n)
        stream.append((name, slot, src, k, n))

    def cols(w, a, b):
        return w[:, a:b].rearrange("(k p) n -> p k n", p=P)

    qkv_order = [("k", 0), ("q", 0), ("v", 0), ("k", 1), ("q", 1), ("v", 1)]
    ada_rest = [("ada0", i) for i in range(4, 12)] + [("ada1", i) for i in range(12)]
    ada_at = [[] for _ in range(HEADS)]
    for n, a in enumerate(ada_rest):
        ada_at[(n * HEADS) // len(ada_rest)].append(a)
    for n, (kind, i) in enumerate([("ada0", i) for i in range(4)] + qkv_order + ada_rest):
        if kind in ("q", "k", "v"):
            at = D * "qkv".index(kind) + 512 * i
            src = cols(sb_w_qkv[0], at, at + 512)
        else:
            src = cols(ada_w[int(kind[3])], 512 * i, 512 * i + 512)
        chunk((kind, i), n % 6, src, KD, 512)
    for i in range(2):
        chunk(("wo0", i), 6 + i, cols(sb_w_o[0], 512 * i, 512 * i + 512), KD, 512)
    first = [len(stream), 0]
    base = [list(uses), 0]
    for s in range(6):
        uses[s] += NE // 2
    for i in range(2):
        chunk(("win", i), 6 + i, mla_w_in[0][512 * i:512 * i + 512].rearrange("(k p) n -> p k n", p=P), 4,
              QR + KVR + ROPE)
    for i in range(2):
        chunk(("qup", i), i, cols(mla_w_q_up[0], 768 * i, 768 * i + 768), QR // P, 768)
    chunk(("kvup", 0), 2, cols(mla_w_kv_up[0], 0, 2048), KVR // P, 2048)
    for i in range(2):
        chunk(("wo1", i), 6 + i, cols(mla_w_o[0], 512 * i, 512 * i + 512), KD, 512)
    first[1] = len(stream)
    base[1] = list(uses)

    with ExitStack() as ctx:
        def sb(name, shape, dt=F32):
            return ctx.enter_context(nc.sbuf_tensor(name, shape, dt))

        def sem(name):
            return ctx.enter_context(nc.semaphore(name))

        ring = [sb(f"ring{s}", [P, SLOT]) for s in range(SLOTS)]
        xT = sb("xT", [P, KD, T])
        hT = sb("hT", [P, KD, T])
        QT = sb("QT", [P, 8, T])
        KT = sb("KT", [P, 8, T])
        V = sb("V", [P, TT, D])
        OT = sb("OT", [P, 8, T])
        ident = sb("ident", [P, P])
        ones = sb("ones", [P, P])
        neg_ones = sb("neg_ones", [P, P])
        neg_tri = sb("neg_tri", [P, P])
        strict = sb("strict", [P, P])
        bias_strict = sb("bias_strict", [P, 384])
        bias_causal = sb("bias_causal", [P, 384])
        rot = sb("rot", [P, P])
        zeros = sb("zeros", [P, P])
        prio = sb("prio", [P, 4])
        rowsA = sb("rowsA", [P, P])
        rowsB = sb("rowsB", [P, P])
        colA = sb("colA", [P, P])
        colB = sb("colB", [P, P])
        c_act = sb("c_act", [P, KD])
        mod = sb("mod", [P, 2, MOD])
        gs = sb("gs", [P, 4, KD])
        freq = sb("freq", [P, 1])
        cosT = sb("cosT", [P, T])
        sinT = sb("sinT", [P, T])
        rstd = sb("rstd", [P, 2, T])
        sc = [[sb(f"sc{i}_{b}", [P, 384]) for b in range(2)] for i in range(5)]
        st = [sb(f"st{b}", [P, 8]) for b in range(2)]
        wr = sb("wr", [P, 2, KD, NG + NE])
        br = sb("br", [P, 2, NG + NE])
        lg = sb("lg", [P, TT, NG + NE])
        rt = sb("rt", [P, 12, 16])
        gates = sb("gates", [P, TT, NE])
        k_rope = sb("k_rope", [P, T])

        x_nat = V
        sq = V[:, :, :].rearrange("p t (k n) -> p (t k) n", n=T)
        lat = OT
        q_rope = [hT[:, 5, :], hT[:, 6, :], hT[:, 7, :], bias_strict[:, 0:T]]
        pos_i = sc[4][0][:, 0:T].bitcast(I32)
        raw_rope = [OT[:, 0, :], OT[:, 1, :], OT[:, 2, :], OT[:, 3, :], OT[:, 5, :]]
        ang, turns, sin_part = sc[3][0][:, 0:T], sc[3][1][:, 0:T], OT[:, 6, :]
        hg = [QT[:, 0:4, :], QT[:, 4:8, :]]
        silu = [sc[0][b][:, 0:T] for b in range(2)]
        gate_row = [sc[1][b][:, 0:T] for b in range(2)]
        diag = sc[2][0][:, 0:T].rearrange("p (t n) -> p t n", t=TT)
        GU = [[ring[3 * b + i][:, :].rearrange("p (k n) -> p k n", k=4) for i in range(2)] for b in range(2)]
        q_nope_w = ring[3][:, 0:3 * D].rearrange("p (k n) -> p k n", k=3)
        q_rope_w = KT[:, 0:6, :].rearrange("p (k a) t -> p k (a t)", k=3)
        k_nope_w = ring[4][:, 0:2 * D].rearrange("p (k n) -> p k n", k=2)
        k_rope_w = ring[4][:, 2 * D:2 * D + KD * P].rearrange("p (k n) -> p k n", k=KD)
        DN = [ring[3 * b + 2][:, :].rearrange("p (k n) -> p k n", k=4) for b in range(2)]

        banks = [ctx.enter_context(nc.psum_tensor(f"bank{b}", [P, 512], F32)) for b in range(8)]

        consts = sem("consts")
        pool_chain = sem("pool_chain")
        packed = sem("packed")
        dve_chain = sem("dve_chain")
        act_chain = sem("act_chain")
        x_loaded = sem("x_loaded")
        rows_loaded = sem("rows_loaded")
        small_loaded = sem("small_loaded")
        loaded = [sem(f"loaded{s}") for s in range(SLOTS)]
        x_turned = sem("x_turned")
        x_ready = sem("x_ready")
        rows_turned = sem("rows_turned")
        cols_ready = sem("cols_ready")
        c_ready = sem("c_ready")
        mod_done = sem("mod_done")
        sq_ready = sem("sq_ready")
        ss_done = sem("ss_done")
        ms_ready = sem("ms_ready")
        std_ready = sem("std_ready")
        h_ready = sem("h_ready")
        tile_done = sem("tile_done")
        tile_kept = {"v": sem("tile_kept_vector"), "a": sem("tile_kept_scalar")}
        trig_in = sem("trig_in")
        trig_ready = sem("trig_ready")
        z_done = sem("z_done")
        soft_ready = sem("soft_ready")
        sp_ready = sem("sp_ready")
        spm_ready = sem("spm_ready")
        sticks_done = sem("sticks_done")
        log_ready = sem("log_ready")
        a_ready = sem("a_ready")
        o_done = sem("o_done")
        o_ready = sem("o_ready")
        s_done = sem("s_done")
        masked_ready = sem("masked_ready")
        neg_ready = sem("neg_ready")
        p_ready = sem("p_ready")
        pn_ready = sem("pn_ready")
        pt_done = sem("pt_done")
        aT_ready = sem("aT_ready")
        rope_ready = sem("rope_ready")
        logit_done = sem("logit_done")
        route_in = sem("route_in")
        route_out = sem("route_out")
        diag_ready = sem("diag_ready")
        gate_done = sem("gate_done")
        gate_ready = sem("gate_ready")
        gu_done = sem("gu_done")
        silu_ready = sem("silu_ready")
        gu_read = sem("gu_read")
        hg_ready = sem("hg_ready")
        down_done = sem("down_done")
        y_turned = sem("y_turned")
        y_ready = sem("y_ready")
        stored = sem("stored")

        used_up = {}
        for n in range(4):
            used_up[("ada0", n)] = (mod_done, n + 1)
        for n, a in enumerate(ada_rest):
            used_up[a] = (mod_done, 5 + n)
        for half in range(2):
            used_up[("k", half)] = (tile_done, 10 * half + 4)
            used_up[("q", half)] = (tile_done, 10 * half + 8)
            used_up[("v", half)] = (tile_done, 10 * half + 10)
            used_up[("wo0", half)] = (tile_done, TWO0 + 4 * half + 4)
            used_up[("win", half)] = (tile_done, TUP)
            used_up[("qup", half)] = (packed, 5)
            used_up[("wo1", half)] = (tile_done, TWO1 + 4 * half + 4)
        used_up[("kvup", 0)] = (tile_done, TWO1)

        def weights(name):
            slot, _, k, n = where[name]
            return ring[slot][:, 0:k * n].rearrange("p (k n) -> p k n", k=k)

        def wait_weights(eng, name):
            slot, use, _, _ = where[name]
            eng.wait_ge(loaded[slot], 16 * use)

        def wait_tiles(eng, last):
            for kind in "va":
                count = owner[:last + 1].count(kind)
                if count:
                    eng.wait_ge(tile_kept[kind], count)

        block = ctx.enter_context(nc.Block())

        @block.sync
        def _(sp):
            sp.dma_start(x_nat[:, :, :], x[0].rearrange("(t p) d -> p t d", p=P)).then_inc(x_loaded, 16)
            before = [None] * SLOTS

            def load(entry):
                name, slot, src, k, n = entry
                if before[slot] is not None:
                    sp.wait_ge(*before[slot])
                sp.dma_start(ring[slot][:, 0:k * n].rearrange("p (k n) -> p k n", k=k), src).then_inc(loaded[slot], 16)
                before[slot] = used_up[name]

            def load_expert_part(layer, b, part, e):
                slot = 3 * b + part
                if part < 2:
                    src = moe_w_gate_up[layer][e, 512 * part:512 * part + 512, :]
                else:
                    src = moe_w_down[layer][e, :, :]
                sp.dma_start(ring[slot][:, :].rearrange("p (k n) -> p k n", k=4),
                             src.rearrange("e (k p) n -> p (e k) n", p=P)).then_inc(loaded[slot], 16)

            def experts(layer):
                for b in range(2):
                    for part in range(3):
                        sp.wait_ge(*before[3 * b + part])
                        load_expert_part(layer, b, part, bass.ds(b, 1))
                with sp.Fori(1, NE // 2) as i:
                    for b in range(2):
                        for part in range(3):
                            if part < 2:
                                sp.wait_ge(gu_done, i * 8 + (64 * layer + 4 * b - 4))
                            else:
                                sp.wait_ge(down_done, i * 2 + (17 * layer + b))
                            load_expert_part(layer, b, part, bass.ds(i * 2 + b, 1))
                for b in range(2):
                    before[3 * b] = before[3 * b + 1] = (gu_done, 64 * layer + 4 * (NE - 1 + b))
                    before[3 * b + 2] = (down_done, 17 * layer + NE + b)
                before[3] = (tile_done, TUP + 8)
                before[4] = (tile_done, TKV + 8)

            for entry in stream[:first[0]]:
                load(entry)
            experts(0)
            for entry in stream[first[0]:first[1]]:
                load(entry)
            experts(1)
            sp.wait_ge(y_ready, 4)
            sp.dma_start(out[0].rearrange("(t p) d -> p t d", p=P), V[:, :, :]).then_inc(stored, 16)
            sp.wait_ge(stored, 16)

        @block.gpsimd
        def _(pool):
            rows = [(rowsA, 0, c, 8), (rowsA, 8, ada_b[0:1], 48), (rowsA, 56, norm_mix_g[0:1], 8),
                    (rowsA, 64, norm_ffn_g[0:1], 8), (rowsB, 0, ada_b[1:2], 48), (rowsB, 48, norm_mix_g[1:2], 8),
                    (rowsB, 56, norm_ffn_g[1:2], 8), (rowsB, 72, mla_g_q, 3), (rowsB, 75, mla_g_kv, 2)]
            for tile_, at, src, r in rows:
                pool.dma_start(tile_[at:at + r, :], src.rearrange("o (r p) -> (o r) p", p=P)).then_inc(rows_loaded, 16)
            pool.dma_start(rowsB[64:72, :], final_g.rearrange("(r p) -> r p", p=P)).then_inc(rows_loaded, 16)
            nc.gpsimd.memset(ident[:, :], 0.0).then_inc(pool_chain, 1)
            pool.wait_ge(pool_chain, 1)
            nc.gpsimd.affine_select(out=ident[:, :], in_=ident[:, :], compare_op=ALU.not_equal, fill=1.0, base=0,
                                    pattern=[[-1, P]], channel_multiplier=1).then_inc(consts, 1)
            nc.gpsimd.memset(ones[:, :], 1.0).then_inc(consts, 1)
            pool.dma_start(pos_i, positions.broadcast_to([P, T])).then_inc(small_loaded, 16)
            pool.dma_start(freq[:, :], inv_freq.rearrange("(p o) -> p o", o=1)).then_inc(small_loaded, 16)
            for l in range(2):
                pool.dma_start(wr[:, l, :, 0:NG], moe_w_group[l].rearrange("(k p) n -> p k n", p=P)).then_inc(small_loaded, 16)
                pool.dma_start(wr[:, l, :, NG:], moe_w_router[l].rearrange("(k p) n -> p k n", p=P)).then_inc(small_loaded, 16)
                pool.dma_start(br[:, l, 0:NG], moe_b_group[l:l + 1].broadcast_to([P, NG])).then_inc(small_loaded, 16)
                pool.dma_start(br[:, l, NG:], moe_b_router[l:l + 1].broadcast_to([P, NE])).then_inc(small_loaded, 16)
            nc.gpsimd.memset(zeros[:, :], 0.0)
            nc.gpsimd.memset(neg_ones[:, :], -1.0)
            for j in range(4):
                nc.gpsimd.memset(prio[:, j:j + 1], float(4 - j))
            nc.gpsimd.memset(neg_tri[:, :], -1.0)
            nc.gpsimd.memset(strict[:, :], 1.0)
            nc.gpsimd.memset(bias_strict[:, :], 0.0)
            nc.gpsimd.memset(bias_causal[:, :], 0.0)
            nc.gpsimd.memset(rot[:, :], 0.0).then_inc(pool_chain, 1)
            pool.wait_ge(pool_chain, 2)
            nc.gpsimd.affine_select(out=neg_tri[:, :], in_=neg_tri[:, :], compare_op=ALU.is_ge, fill=0.0, base=0,
                                    pattern=[[-1, P]], channel_multiplier=1)
            nc.gpsimd.affine_select(out=strict[:, :], in_=strict[:, :], compare_op=ALU.is_gt, fill=0.0, base=0,
                                    pattern=[[1, P]], channel_multiplier=-1)
            for part in (0, 256):
                nc.gpsimd.affine_select(out=bias_strict[:, part:part + P], in_=bias_strict[:, part:part + P],
                                        compare_op=ALU.is_gt, fill=NEG, base=0, pattern=[[1, P]],
                                        channel_multiplier=-1)
                nc.gpsimd.affine_select(out=bias_causal[:, part:part + P], in_=bias_causal[:, part:part + P],
                                        compare_op=ALU.is_ge, fill=NEG, base=0, pattern=[[-1, P]],
                                        channel_multiplier=1)
            halves = rot[:, :].rearrange("p (b h j) -> p b h j", b=4, h=2)
            nc.gpsimd.affine_select(out=halves[:, :, 0, :], in_=halves[:, :, 0, :], compare_op=ALU.not_equal,
                                    fill=-1.0, base=-16, pattern=[[-32, 4], [-1, 16]], channel_multiplier=1)
            nc.gpsimd.affine_select(out=halves[:, :, 1, :], in_=halves[:, :, 1, :], compare_op=ALU.not_equal,
                                    fill=1.0, base=0, pattern=[[-32, 4], [-1, 16]],
                                    channel_multiplier=1).then_inc(consts, 1)
            for h in range(HEADS):
                pool.wait_ge(sp_ready, h + 1)
                for at in (0, 256):
                    ins = nc.gpsimd.tensor_tensor(sc[2][h % 2][:, at:at + P], sc[2][h % 2][:, at:at + P],
                                                  strict[:, :], ALU.mult)
                ins.then_inc(spm_ready, 1)
            def gate_experts(layer):
                with pool.Fori(0, NE // 2) as i:
                    for b in range(2):
                        e0 = NE * layer + b
                        pool.wait_ge(gate_ready, i * 2 + (e0 + 1))
                        for f in range(4):
                            pool.wait_ge(gu_read, i * 8 + (65 * layer + 4 * b + f + 2))
                            nc.gpsimd.tensor_tensor(hg[b][:, f, :], hg[b][:, f, :], gate_row[b],
                                                    ALU.mult).then_inc(hg_ready, 1)

            def pack_mixer1():
                pool.wait_ge(gu_done, 4 * NE)
                for i in range(2):
                    wait_weights(pool, ("win", i))
                    nc.gpsimd.tensor_copy(
                        k_rope_w[:, 4 * i:4 * i + 4, :].rearrange("p k (c r) -> p k c r", c=4),
                        weights(("win", i))[:, :, QR + KVR:].unsqueeze(2).broadcast_to([P, 4, 4, ROPE])).then_inc(packed, 1)
                for i in range(2):
                    wait_weights(pool, ("qup", i))
                    w = weights(("qup", i)).rearrange("p k (h d) -> p k h d", d=QK)
                    nc.gpsimd.tensor_copy(q_nope_w[:, :, 512 * i:512 * i + 512].rearrange("p k (h d) -> p k h d", d=DH),
                                          w[:, :, :, 0:DH])
                    ins = nc.gpsimd.tensor_copy(
                        q_rope_w[:, :, 256 * i:256 * i + 256].rearrange("p k (h d) -> p k h d", d=ROPE),
                        w[:, :, :, DH:QK])
                    ins.then_inc(packed, 1 + i)
                wait_weights(pool, ("kvup", 0))
                nc.gpsimd.tensor_copy(k_nope_w.rearrange("p k (h d) -> p k h d", d=DH),
                                      weights(("kvup", 0)).rearrange("p k (h d) -> p k h d", d=2 * DH)[:, :, :, 0:DH]) \
                    .then_inc(packed, 1)

            gate_experts(0)
            pack_mixer1()
            gate_experts(1)

        @block.tensor
        def _(pe):
            tile_no = [0]

            def projection(lhs, rhs, ks, n=T):
                j = tile_no[0]
                if j >= 4:
                    pe.wait_ge(tile_kept[owner[j - 4]], nth[j - 4])
                tile_no[0] += 1
                for k in range(ks):
                    mm = pe.matmul(banks[j % 4][:, 0:n], lhs(k), rhs(k), start=(k == 0), stop=(k == ks - 1))
                mm.then_inc(tile_done, 1)

            def sum_squares(tiles, at=0, bank=6):
                for k in tiles:
                    mm = pe.matmul(banks[bank][:, at:at + T], ones[:, :], sq[:, k, :],
                                   start=(k == tiles[0]), stop=(k == tiles[-1]))
                mm.then_inc(ss_done, 1)

            def ada(kind, i, bank):
                wait_weights(pe, (kind, i))
                w = weights((kind, i))
                for j in range(4):
                    col = int(kind[3]) * MOD + 4 * i + j
                    for k in range(KD):
                        mm = pe.matmul(banks[bank][:, col:col + 1], w[:, k, j * P:(j + 1) * P], c_act[:, k:k + 1],
                                       start=(k == 0), stop=(k == KD - 1))
                mm.then_inc(mod_done, 1)

            pe.wait_ge(consts, 2)
            pe.wait_ge(rows_loaded, 160)
            pe.transpose(banks[6][:, 0:72], rowsA[0:72, :], ident[0:72, 0:72])
            pe.transpose(banks[6][:, 128:205], rowsB[0:77, :], ident[0:77, 0:77]).then_inc(rows_turned, 1)
            pe.wait_ge(x_loaded, 16)
            for b in range(4):
                for k in range(2):
                    for t in range(TT):
                        tr = pe.transpose(banks[b][:, k * T + t * P:k * T + (t + 1) * P],
                                          x_nat[:, t, (2 * b + k) * P:(2 * b + k + 1) * P], ident[:, :])
                tr.then_inc(x_turned, 1)
            pe.wait_ge(sq_ready, 1)
            sum_squares(range(KD), bank=7)
            pe.wait_ge(cols_ready, 1)
            pe.wait_ge(c_ready, 1)
            for i in range(4):
                ada("ada0", i, 6)

            pe.wait_ge(h_ready, KD)
            for kind, half in qkv_order:
                wait_weights(pe, (kind, half))
                w = weights((kind, half))
                if kind == "v":
                    for t in range(TT):
                        projection(lambda k: hT[:, k, t * P:(t + 1) * P], lambda k: w[:, k, :], KD, 512)
                else:
                    for j in range(4):
                        projection(lambda k: w[:, k, j * P:(j + 1) * P], lambda k: hT[:, k, :], KD)

            def scores0(h):
                p, r = h // 2, 64 * (h % 2)
                z = banks[h % 4]
                if h >= 4:
                    pe.wait_ge(log_ready, h - 3)
                pe.matmul(z[:, 0:256], KT[r:r + 64, p, 0:P], QT[r:r + 64, p, :], start=True, stop=False,
                          skip_group_check=True)
                pe.matmul(z[:, 256:384], KT[r:r + 64, p, P:T], QT[r:r + 64, p, P:T], start=False, stop=False,
                          skip_group_check=True).then_inc(z_done, 1)

            def sticks(h):
                z, spm = banks[h % 4], sc[2][h % 2]
                pe.wait_ge(spm_ready, h + 1)
                pe.matmul(z[:, 0:256], neg_tri[:, :], spm[:, 0:256], start=False, stop=False, skip_group_check=True)
                pe.matmul(z[:, 128:256], neg_ones[:, :], spm[:, 256:384], start=False, stop=False,
                          skip_group_check=True)
                pe.matmul(z[:, 256:384], neg_tri[:, :], spm[:, 256:384], start=False, stop=True,
                          skip_group_check=True).then_inc(sticks_done, 1)

            def values(layer, h, ready):
                p, r, a = h // 2, 64 * (h % 2), sc[3][h % 2]
                o = banks[4 + p % 2]
                pe.wait_ge(ready, h + 1)
                if r == 0 and 8 * layer + p >= 2:
                    pe.wait_ge(o_ready, 8 * layer + p - 1)
                pe.matmul(o[r:r + 64, 0:256], V[:, 0, h * DH:(h + 1) * DH], a[:, 0:256], start=True, stop=False,
                          skip_group_check=True)
                pe.matmul(o[r:r + 64, 128:256], V[:, 1, h * DH:(h + 1) * DH], a[:, 256:384], start=False, stop=True,
                          skip_group_check=True).then_inc(o_done, 1)

            wait_tiles(pe, TWO0 - 1)
            pe.wait_ge(consts, 3)
            for h in range(HEADS + 3):
                if h < HEADS:
                    scores0(h)
                if 1 <= h <= HEADS:
                    sticks(h - 1)
                if h < HEADS:
                    for kind, i in ada_at[h]:
                        ada(kind, i, 7)
                if h >= 3:
                    values(0, h - 3, a_ready)

            def out_projection(kind, layer):
                pe.wait_ge(o_ready, 8 * (layer + 1))
                for i in range(2):
                    wait_weights(pe, (kind, i))
                    w = weights((kind, i))
                    for j in range(4):
                        projection(lambda k: w[:, k, j * P:(j + 1) * P], lambda k: OT[:, k, :], KD)

            out_projection("wo0", 0)

            def moe(layer):
                pe.wait_ge(sq_ready, (2, 6)[layer])
                sum_squares(range(KD))
                pe.wait_ge(h_ready, (16, 37)[layer])
                pe.wait_ge(small_loaded, 160)
                for t in range(TT):
                    for k in range(KD):
                        mm = pe.matmul(banks[7][:, t * 32:t * 32 + NG + NE], hT[:, k, t * P:(t + 1) * P],
                                       wr[:, layer, k, :], start=(k == 0), stop=(k == KD - 1))
                mm.then_inc(logit_done, 1)
                for b in range(4):
                    mm = pe.matmul(banks[b][:, :], zeros[:, :], zeros[:, :].unsqueeze(1).broadcast_to([P, 4, P]),
                                   start=True, stop=False, skip_group_check=True)
                mm.then_inc(down_done, 1)
                pe.wait_ge(gu_read, 65 * layer + 1)
                with pe.Fori(0, NE // 2) as i:
                    for b in range(2):
                        pe.wait_ge(diag_ready, i * 2 + (NE * layer + b + 1))
                        for t in range(TT):
                            mm = pe.matmul(banks[6][:, t * P:(t + 1) * P], ones[:, :], diag[:, t, :],
                                           start=True, stop=True)
                        mm.then_inc(gate_done, 1)
                        for part in range(2):
                            pe.wait_ge(loaded[3 * b + part], i * 16 + 16 * (base[layer][3 * b + part] + 1))
                        for f in range(4):
                            pe.wait_ge(gu_read, i * 8 + (65 * layer + 4 * b + f))
                            for u in range(2):
                                for k in range(KD):
                                    mm = pe.matmul(banks[4 + f % 2][:, u * T:(u + 1) * T],
                                                   GU[b][k // 4][:, k % 4, u * FF + f * P:u * FF + (f + 1) * P],
                                                   hT[:, k, :], start=(k == 0), stop=(k == KD - 1))
                            mm.then_inc(gu_done, 1)
                        pe.wait_ge(loaded[3 * b + 2], i * 16 + 16 * (base[layer][3 * b + 2] + 1))
                        for f in range(4):
                            pe.wait_ge(hg_ready, i * 8 + (64 * layer + 4 * b + f + 1))
                            for d in range(KD):
                                mm = pe.matmul(banks[d // 2][:, (d % 2) * T:(d % 2 + 1) * T],
                                               DN[b][:, f, d * P:(d + 1) * P], hg[b][:, f, :],
                                               start=False, stop=False, skip_group_check=True)
                        mm.then_inc(down_done, 1)

            moe(0)

            pe.wait_ge(sq_ready, 3)
            sum_squares(range(KD))
            pe.wait_ge(h_ready, 24)
            for i in range(2):
                wait_weights(pe, ("win", i))
            win = [weights(("win", i)) for i in range(2)]
            for j in range(5):
                projection(lambda k: win[k // 4][:, k % 4, j * P:(j + 1) * P], lambda k: hT[:, k, :], KD)
            pe.wait_ge(packed, 2)
            projection(lambda k: k_rope_w[:, k, :], lambda k: hT[:, k, :], KD)
            pe.wait_ge(sq_ready, 5)
            sum_squares(range(3), at=0)
            pe.wait_ge(ms_ready, 4)
            sum_squares(range(3, 5), at=T)
            pe.wait_ge(h_ready, 29)
            pe.wait_ge(packed, 5)
            for p in range(8):
                projection(lambda k: q_nope_w[:, k, p * P:(p + 1) * P], lambda k: hT[:, k, :], 3)
            for g in range(4):
                projection(lambda k: q_rope_w[:, k, g * P:(g + 1) * P], lambda k: hT[:, k, :], 3)
            for g in range(5):
                wait_tiles(pe, TUP + 8 + g if g < 4 else TUP + 11)
                projection(lambda k: rot[:, :], lambda k: raw_rope[g], 1)
            wait_weights(pe, ("kvup", 0))
            pe.wait_ge(packed, 6)
            kvup = weights(("kvup", 0)).rearrange("p k (h d) -> p k h d", d=2 * DH)
            for p in range(8):
                projection(lambda k: k_nope_w[:, k, p * P:(p + 1) * P], lambda k: hT[:, 3 + k, :], 2)
            for t in range(TT):
                for half in range(2):
                    projection(lambda k: hT[:, 3 + k, t * P:(t + 1) * P],
                               lambda k: kvup[:, k, 8 * half:8 * half + 8, DH:2 * DH], 2, 512)

            def scores1(h):
                p, r, g, q = h // 2, 64 * (h % 2), h // 4, 32 * (h % 4)
                s = banks[h % 2]
                if h >= 2:
                    pe.wait_ge(masked_ready, 2 * (h - 1))
                pe.matmul(s[:, 0:P], QT[r:r + 64, p, 0:P], KT[r:r + 64, p, 0:P], start=True, stop=False,
                          skip_group_check=True)
                pe.matmul(s[:, P:384], QT[r:r + 64, p, P:T], KT[r:r + 64, p, :], start=False, stop=False,
                          skip_group_check=True)
                pe.matmul(s[:, 0:P], q_rope[g][q:q + 32, 0:P], k_rope[q:q + 32, 0:P], start=False, stop=False,
                          skip_group_check=True, tile_position=(q, 0))
                pe.matmul(s[:, P:384], q_rope[g][q:q + 32, P:T], k_rope[q:q + 32, :], start=False, stop=True,
                          skip_group_check=True, tile_position=(q, 0)).then_inc(s_done, 1)

            def turn(h):
                probs, pt = sc[1][h % 2], banks[2 + h % 2]
                pe.wait_ge(pn_ready, h + 1)
                if h >= 2:
                    pe.wait_ge(aT_ready, h - 1)
                for n in range(3):
                    tr = pe.transpose(pt[:, n * P:(n + 1) * P], probs[:, n * P:(n + 1) * P], ident[:, :])
                tr.then_inc(pt_done, 1)

            wait_tiles(pe, TWO1 - 1)
            pe.wait_ge(rope_ready, 5)
            for h in range(HEADS + 3):
                if h < HEADS:
                    scores1(h)
                if 2 <= h < HEADS + 2:
                    turn(h - 2)
                if h >= 3:
                    values(1, h - 3, aT_ready)
            out_projection("wo1", 1)
            moe(1)
            pe.wait_ge(sq_ready, 7)
            sum_squares(range(KD))
            pe.wait_ge(h_ready, 45)
            for b in range(4):
                t, half = b // 2, b % 2
                for k in range(4):
                    tr = pe.transpose(banks[b][:, k * P:(k + 1) * P], hT[:, 4 * half + k, t * P:(t + 1) * P],
                                      ident[:, :])
                tr.then_inc(y_turned, 1)

        def qkv_place(j):
            half, r = j // 10, j % 10
            if r < 4:
                return KT[:, 4 * half + r, :], T, 1.0
            if r < 8:
                return QT[:, 4 * half + r - 4, :], T, DH ** -0.5
            return V[:, r - 8, 512 * half:512 * half + 512], 512, 1.0

        def latent_place(j):
            if j < TUP:
                return lat[:, j - TLAT, :], T
            if j < TUP + 8:
                return QT[:, j - TUP, :], T
            if j < TROT:
                return raw_rope[j - TUP - 8], T
            if j < TKV + 8:
                return KT[:, j - TKV, :], T
            n = j - TKV - 8
            return V[:, n // 2, 512 * (n % 2):512 * (n % 2) + 512], 512

        @block.vector
        def _(dve):
            v = nc.vector
            links = [0]

            def link(ins):
                links[0] += 1
                ins.then_inc(dve_chain, 1)
                dve.wait_ge(dve_chain, links[0])

            dve.wait_ge(rows_turned, 1)
            v.tensor_copy(colA[:, 0:72], banks[6][:, 0:72])
            v.tensor_copy(colB[:, 0:77], banks[6][:, 128:205]).then_inc(cols_ready, 1)
            dve.wait_ge(cols_ready, 1)
            for b in range(4):
                dve.wait_ge(x_turned, b + 1)
                v.tensor_copy(xT[:, 2 * b:2 * b + 2, :], banks[b][:, :].rearrange("p (k t) -> p k t", k=2)) \
                    .then_inc(x_ready, 1)

            def mean_square(number, d, at=0, bank=6):
                dve.wait_ge(ss_done, number)
                v.tensor_scalar(rstd[:, at // T, :], banks[bank][:, at:at + T], 1.0 / d, EPS, ALU.mult,
                                ALU.add).then_inc(ms_ready, 1)

            def norm(number, gain, shift, bank=6):
                mean_square(number, D, 0, bank)
                dve.wait_ge(std_ready, number)
                link(v.reciprocal(rstd[:, 0, :], rstd[:, 0, :]))
                link(v.tensor_tensor(hT[:, :, :], xT[:, :, :], rstd[:, 0, :].unsqueeze(1).broadcast_to([P, KD, T]),
                                     ALU.mult))
                for k in range(KD):
                    if shift is None:
                        v.tensor_scalar(hT[:, k, :], hT[:, k, :], gain[:, k:k + 1], None,
                                        ALU.mult).then_inc(h_ready, 1)
                    else:
                        v.tensor_scalar(hT[:, k, :], hT[:, k, :], gain[:, k:k + 1], shift[:, k:k + 1], ALU.mult,
                                        ALU.add).then_inc(h_ready, 1)

            def set_gain(slot, layer, scale_at, g):
                link(v.scalar_tensor_tensor(out=gs[:, slot, :], in0=mod[:, layer, scale_at:scale_at + KD], scalar=1.0,
                                            in1=g, op0=ALU.add, op1=ALU.mult))

            dve.wait_ge(x_ready, 4)
            dve.wait_ge(mod_done, 4)
            link(v.tensor_tensor(mod[:, 0, 0:16], banks[6][:, 0:16], colA[:, 8:24], ALU.add))
            set_gain(0, 0, 8, colA[:, 56:64])
            norm(1, gs[:, 0, :], mod[:, 0, 0:8], bank=7)

            dve.wait_ge(small_loaded, 160)
            link(v.tensor_copy(ang, pos_i))
            link(v.tensor_scalar(ang, ang, freq[:, 0:1], None, ALU.mult))
            link(v.tensor_scalar(turns, ang, float(1.0 / (2 * np.pi)), None, ALU.mult))
            link(v.tensor_scalar(turns, turns, 1.5 * 2.0 ** 23, None, ALU.add))
            link(v.tensor_scalar(turns, turns, 1.5 * 2.0 ** 23, None, ALU.subtract))
            c1 = 6.28125
            c2 = float(np.floor((2 * np.pi - c1) * 2.0 ** 21) / 2.0 ** 21)
            c3 = float(2 * np.pi - c1 - c2)
            for part in (c1, c2, c3):
                link(v.scalar_tensor_tensor(out=ang, in0=turns, scalar=-part, in1=ang, op0=ALU.mult, op1=ALU.add))
            pi = float(np.nextafter(np.float32(np.pi), np.float32(0)))
            v.tensor_scalar(ang, ang, pi, -pi, ALU.min, ALU.max).then_inc(trig_in, 1)
            dve.wait_ge(trig_in, 1)
            link(v.scalar_tensor_tensor(out=turns, in0=ang, scalar=-1.0, in1=ang, op0=ALU.mult, op1=ALU.max))
            v.tensor_scalar(turns, turns, -1.0, float(np.pi / 2), ALU.mult, ALU.add).then_inc(trig_in, 1)

            for j in range(TWO0):
                if owner[j] == "v":
                    dst, n, scale = qkv_place(j)
                    dve.wait_ge(tile_done, j + 1)
                    v.tensor_scalar(dst, banks[j % 4][:, 0:n], scale, None, ALU.mult).then_inc(tile_kept["v"], 1)

            def log_a(h):
                dve.wait_ge(sticks_done, h + 1)
                if h >= 2:
                    dve.wait_ge(a_ready, h - 1)
                v.scalar_tensor_tensor(out=sc[4][h % 2][:, :], in0=banks[h % 4][:, 0:384], scalar=0.0,
                                       in1=bias_strict[:, :], op0=ALU.min, op1=ALU.add).then_inc(log_ready, 1)

            def softplus(h):
                dve.wait_ge(soft_ready, h + 1)
                if h >= 2:
                    dve.wait_ge(sticks_done, h - 1)
                v.scalar_tensor_tensor(out=sc[2][h % 2][:, :], in0=banks[h % 4][:, 0:384], scalar=0.0,
                                       in1=sc[1][h % 2][:, :], op0=ALU.max, op1=ALU.add).then_inc(sp_ready, 1)

            def keep_o(layer, p):
                dve.wait_ge(o_done, 16 * layer + 2 * p + 2)
                v.tensor_copy(OT[:, p, :], banks[4 + p % 2][:, 0:T]).then_inc(o_ready, 1)

            dve.wait_ge(consts, 3)
            dve.wait_ge(trig_ready, 2)
            for h in range(HEADS + 5):
                if 2 <= h < HEADS + 2:
                    log_a(h - 2)
                if 1 <= h <= HEADS:
                    softplus(h - 1)
                if h >= 5 and h % 2 == 1:
                    keep_o(0, (h - 5) // 2)
            dve.wait_ge(mod_done, 24)
            link(v.tensor_tensor(mod[:, 0, 16:48], banks[7][:, 16:48], colA[:, 24:56], ALU.add))
            link(v.tensor_tensor(mod[:, 1, :], banks[7][:, 48:96], colB[:, 0:48], ALU.add))
            set_gain(1, 0, 32, colA[:, 64:72])
            set_gain(2, 1, 8, colB[:, 48:56])
            set_gain(3, 1, 32, colB[:, 56:64])

            def residual_tiles(first, layer, ready):
                for d in range(KD):
                    j = first + d
                    dve.wait_ge(tile_done, j + 1)
                    v.scalar_tensor_tensor(out=xT[:, d, :], in0=banks[j % 4][:, 0:T],
                                           scalar=mod[:, layer, 16 + d:17 + d], in1=xT[:, d, :],
                                           op0=ALU.mult, op1=ALU.add).then_inc(tile_kept["v"], 1)
                dve.wait_ge(tile_kept["v"], nth[first + KD - 1])

            residual_tiles(TWO0, 0, 8)

            def first_of(hot, vals, top):
                eq, best = rt[:, 3, 0:4], rt[:, 4, 0:1]
                link(v.tensor_scalar(eq, vals, top, None, ALU.is_equal))
                link(v.tensor_tensor(eq, eq, prio[:, :], ALU.mult))
                link(v.reduce_max(best, eq, AX.X))
                link(v.tensor_scalar(hot, eq, best, None, ALU.is_equal))

            def moe(layer):
                norm((2, 6)[layer], gs[:, 1 + 2 * layer, :], mod[:, layer, 24:32])
                dve.wait_ge(logit_done, layer + 1)
                link(v.tensor_tensor(lg[:, :, :],
                                     banks[7][:, 0:64].rearrange("p (t n) -> p t n", t=2)[:, :, 0:NG + NE],
                                     br[:, layer, :].unsqueeze(1).broadcast_to([P, TT, NG + NE]), ALU.add))
                for t in range(TT):
                    g, e = lg[:, t, 0:NG], lg[:, t, NG:]
                    gmax, gneg, gsum, gw = (rt[:, 0, q:q + 1] for q in range(4))
                    group = rt[:, 2, 0:4]
                    link(v.reduce_max(gmax, g, AX.X))
                    v.tensor_scalar(gneg, gmax, -1.0, None, ALU.mult).then_inc(route_in, 1)
                    dve.wait_ge(route_out, 4 * layer + 2 * t + 1)
                    link(v.reciprocal(gw, gsum))
                    first_of(group, g, gmax)
                    picked = rt[:, 6, 0:16].rearrange("p (g j) -> p g j", g=NG)
                    link(v.tensor_tensor(picked, e.rearrange("p (g j) -> p g j", g=NG),
                                         group.unsqueeze(2).broadcast_to([P, NG, EPG]), ALU.mult))
                    ein = rt[:, 7, 0:4]
                    link(v.tensor_reduce(ein, picked.rearrange("p g j -> p j g"), AX.X, ALU.add))
                    m1, m2, dm, w1, w2, ex = (rt[:, 8, q:q + 1] for q in range(6))
                    hot1, hot2, rest = rt[:, 9, 0:4], rt[:, 10, 0:4], rt[:, 11, 0:4]
                    link(v.reduce_max(m1, ein, AX.X))
                    first_of(hot1, ein, m1)
                    link(v.scalar_tensor_tensor(out=rest, in0=hot1, scalar=NEG, in1=ein, op0=ALU.mult, op1=ALU.add))
                    link(v.reduce_max(m2, rest, AX.X))
                    first_of(hot2, rest, m2)
                    v.tensor_tensor(dm, m2, m1, ALU.subtract).then_inc(route_in, 1)
                    dve.wait_ge(route_out, 4 * layer + 2 * t + 2)
                    link(v.tensor_scalar(w1, ex, 1.0, None, ALU.add))
                    link(v.reciprocal(w1, w1))
                    link(v.tensor_tensor(w1, w1, gw, ALU.mult))
                    link(v.tensor_tensor(w2, w1, ex, ALU.mult))
                    link(v.tensor_scalar(hot1, hot1, w1, None, ALU.mult))
                    link(v.scalar_tensor_tensor(out=hot1, in0=hot2, scalar=w2, in1=hot1, op0=ALU.mult, op1=ALU.add))
                    ins = v.tensor_tensor(gates[:, t, :].rearrange("p (g j) -> p g j", g=NG),
                                          hot1.unsqueeze(1).broadcast_to([P, NG, EPG]),
                                          group.unsqueeze(2).broadcast_to([P, NG, EPG]), ALU.mult)
                    if t == 0:
                        link(ins)
                ins.then_inc(gu_read, 1)
                dve.wait_ge(gu_read, 65 * layer + 1)
                with dve.Fori(0, NE // 2) as i:
                    for b in range(2):
                        dve.wait_ge(gate_done, i * 2 + (NE * layer + b))
                        v.tensor_tensor(diag, ident[:, :].unsqueeze(1).broadcast_to([P, TT, P]),
                                        gates[:, :, bass.ds(i * 2 + b, 1)].broadcast_to([P, TT, P]),
                                        ALU.mult).then_inc(diag_ready, 1)
                        dve.wait_ge(gate_done, i * 2 + (NE * layer + b + 1))
                        v.tensor_copy(gate_row[b], banks[6][:, 0:T]).then_inc(gate_ready, 1)
                        dve.wait_ge(down_done, i * 2 + (17 * layer + b))
                        for f in range(4):
                            dve.wait_ge(silu_ready, i * 8 + (64 * layer + 4 * b + f + 1))
                            v.tensor_tensor(hg[b][:, f, :], silu[f % 2], banks[4 + f % 2][:, T:2 * T],
                                            ALU.mult).then_inc(gu_read, 1)
                dve.wait_ge(down_done, 17 * (layer + 1))
                for d in range(KD):
                    ins = v.scalar_tensor_tensor(out=xT[:, d, :], in0=banks[d // 2][:, (d % 2) * T:(d % 2 + 1) * T],
                                                 scalar=mod[:, layer, 40 + d:41 + d], in1=xT[:, d, :],
                                                 op0=ALU.mult, op1=ALU.add)
                ins.then_inc(x_ready, 1)
                dve.wait_ge(x_ready, 5 + layer)

            moe(0)
            norm(3, gs[:, 2, :], mod[:, 1, 0:8])

            def keep(lo, hi):
                for j in range(lo, hi):
                    if owner[j] == "v":
                        dst, n = latent_place(j)
                        dve.wait_ge(tile_done, j + 1)
                        v.tensor_copy(dst, banks[j % 4][:, 0:n]).then_inc(tile_kept["v"], 1)

            keep(TLAT, TUP)
            mean_square(4, QR)
            mean_square(5, KVR, T)
            dve.wait_ge(std_ready, 5)
            link(v.reciprocal(rstd[:, :, :], rstd[:, :, :]))
            wait_tiles(dve, TUP - 1)
            for k in range(5):
                v.scalar_tensor_tensor(out=hT[:, k, :], in0=lat[:, k, :], scalar=colB[:, 72 + k:73 + k],
                                       in1=rstd[:, 0 if k < 3 else 1, :], op0=ALU.mult,
                                       op1=ALU.mult).then_inc(h_ready, 1)
            keep(TUP, TROT)
            for g in range(5):
                j = TROT + g
                dve.wait_ge(tile_done, j + 1)
                dst = q_rope[g] if g < 4 else k_rope[:, :]
                v.tensor_tensor(sin_part, banks[j % 4][:, 0:T], sinT[:, :], ALU.mult).then_inc(tile_kept["v"], 1)
                dve.wait_ge(tile_kept["v"], nth[j])
                link(v.tensor_tensor(dst, raw_rope[g], cosT[:, :], ALU.mult))
                v.tensor_tensor(dst, dst, sin_part, ALU.add).then_inc(rope_ready, 1)
                dve.wait_ge(rope_ready, g + 1)
            keep(TKV, TWO1)
            spans = [(0, P), (P, 384)]

            def mask_max(h):
                dve.wait_ge(s_done, h + 1)
                if h >= 2:
                    dve.wait_ge(p_ready, 2 * (h - 1))
                for m, (a, b) in enumerate(spans):
                    v.tensor_tensor_reduce(out=sc[0][h % 2][:, a:b], in0=banks[h % 2][:, a:b],
                                           in1=bias_causal[:, a:b], scale=float(QK ** -0.5), scalar=NEG, op0=ALU.add,
                                           op1=ALU.max, accum_out=st[h % 2][:, m:m + 1]).then_inc(masked_ready, 1)
                dve.wait_ge(masked_ready, 2 * (h + 1))
                v.tensor_scalar(st[h % 2][:, 2:4], st[h % 2][:, 0:2], -1.0, None, ALU.mult).then_inc(neg_ready, 1)

            def normalise(h):
                dve.wait_ge(p_ready, 2 * (h + 1))
                link(v.reciprocal(st[h % 2][:, 6:8], st[h % 2][:, 4:6]))
                for m, (a, b) in enumerate(spans):
                    ins = v.tensor_scalar(sc[1][h % 2][:, a:b], sc[1][h % 2][:, a:b], st[h % 2][:, 6 + m:7 + m], None,
                                          ALU.mult)
                ins.then_inc(pn_ready, 1)

            for h in range(HEADS + 5):
                if h < HEADS:
                    mask_max(h)
                if 1 <= h <= HEADS:
                    normalise(h - 1)
                if h >= 5 and h % 2 == 1:
                    keep_o(1, (h - 5) // 2)
            residual_tiles(TWO1, 1, 16)
            moe(1)
            norm(7, colB[:, 64:72], None)
            for b in range(4):
                dve.wait_ge(y_turned, b + 1)
                t, half = b // 2, b % 2
                v.tensor_copy(V[:, t, 512 * half:512 * half + 512], banks[b][:, :]).then_inc(y_ready, 1)

        @block.scalar
        def _(act):
            s = nc.scalar
            links = [0]

            def link(ins):
                links[0] += 1
                ins.then_inc(act_chain, 1)
                act.wait_ge(act_chain, links[0])

            act.wait_ge(cols_ready, 1)
            s.activation(c_act[:, :], colA[:, 0:8], ACT.Silu).then_inc(c_ready, 1)

            def root(number, at=0):
                act.wait_ge(ms_ready, number)
                s.activation(rstd[:, at // T, :], rstd[:, at // T, :], ACT.Sqrt).then_inc(std_ready, 1)

            act.wait_ge(x_ready, 4)
            s.activation(sq[:, :, :], xT[:, :, :], ACT.Square).then_inc(sq_ready, 1)
            root(1)
            act.wait_ge(trig_in, 2)
            s.activation(sinT[:, :], ang, ACT.Sin).then_inc(trig_ready, 1)
            s.activation(cosT[:, :], turns, ACT.Sin).then_inc(trig_ready, 1)
            for j in range(TWO0):
                if owner[j] == "a":
                    dst, n, scale = qkv_place(j)
                    act.wait_ge(tile_done, j + 1)
                    s.activation(dst, banks[j % 4][:, 0:n], ACT.Copy, scale=scale).then_inc(tile_kept["a"], 1)

            for h in range(HEADS + 2):
                if h < HEADS:
                    e = sc[1][h % 2][:, :]
                    act.wait_ge(z_done, h + 1)
                    if h >= 2:
                        act.wait_ge(sp_ready, h - 1)
                    link(s.activation(e, banks[h % 4][:, 0:384], ACT.Abs))
                    link(s.activation(e, e, ACT.Exp, scale=-1.0))
                    s.activation(e, e, ACT.Ln, bias=1.0).then_inc(soft_ready, 1)
                if h >= 2:
                    g = h - 2
                    act.wait_ge(log_ready, g + 1)
                    if g >= 2:
                        act.wait_ge(o_done, g - 1)
                    s.activation(sc[3][g % 2][:, :], sc[4][g % 2][:, :], ACT.Exp).then_inc(a_ready, 1)

            def moe(layer):
                act.wait_ge(tile_kept["v"], nth[(TWO0, TWO1)[layer] + KD - 1])
                s.activation(sq[:, :, :], xT[:, :, :], ACT.Square).then_inc(sq_ready, 1)
                root((2, 6)[layer])
                for t in range(TT):
                    act.wait_ge(route_in, 4 * layer + 2 * t + 1)
                    s.activation(rt[:, 1, 0:4], lg[:, t, 0:NG], ACT.Exp, bias=rt[:, 0, 1:2],
                                 accum_out=rt[:, 0, 2:3]).then_inc(route_out, 1)
                    act.wait_ge(route_in, 4 * layer + 2 * t + 2)
                    s.activation(rt[:, 8, 5:6], rt[:, 8, 2:3], ACT.Exp).then_inc(route_out, 1)
                with act.Fori(0, NE // 2) as i:
                    for b in range(2):
                        for f in range(4):
                            act.wait_ge(gu_done, i * 8 + (64 * layer + 4 * b + f + 1))
                            act.wait_ge(gu_read, i * 8 + (65 * layer + 4 * b + f))
                            s.activation(silu[f % 2], banks[4 + f % 2][:, 0:T], ACT.Silu).then_inc(silu_ready, 1)

            moe(0)
            act.wait_ge(x_ready, 5)
            s.activation(sq[:, :, :], xT[:, :, :], ACT.Square).then_inc(sq_ready, 1)
            root(3)

            def keep(lo, hi):
                for j in range(lo, hi):
                    if owner[j] == "a":
                        dst, n = latent_place(j)
                        act.wait_ge(tile_done, j + 1)
                        s.activation(dst, banks[j % 4][:, 0:n], ACT.Copy).then_inc(tile_kept["a"], 1)

            keep(TLAT, TUP)
            wait_tiles(act, TUP - 1)
            s.activation(sq[:, 0:3, :], lat[:, 0:3, :], ACT.Square).then_inc(sq_ready, 1)
            s.activation(sq[:, 3:5, :], lat[:, 3:5, :], ACT.Square).then_inc(sq_ready, 1)
            root(4)
            root(5, T)
            keep(TUP, TROT)
            keep(TKV, TWO1)
            for h in range(HEADS + 2):
                if h < HEADS:
                    act.wait_ge(neg_ready, h + 1)
                    if h >= 2:
                        act.wait_ge(pt_done, h - 1)
                    for m, (a, b) in enumerate([(0, P), (P, 384)]):
                        s.activation(sc[1][h % 2][:, a:b], sc[0][h % 2][:, a:b], ACT.Exp,
                                     bias=st[h % 2][:, 2 + m:3 + m],
                                     accum_out=st[h % 2][:, 4 + m:5 + m]).then_inc(p_ready, 1)
                if h >= 2:
                    g = h - 2
                    act.wait_ge(pt_done, g + 1)
                    if g >= 2:
                        act.wait_ge(o_done, HEADS + g - 1)
                    s.activation(sc[3][g % 2][:, :], banks[2 + g % 2][:, 0:384], ACT.Copy).then_inc(aT_ready, 1)
            moe(1)
            act.wait_ge(x_ready, 6)
            s.activation(sq[:, :, :], xT[:, :, :], ACT.Square).then_inc(sq_ready, 1)
            root(7)


_INS = ["x", "c", "positions", "norm_mix_g", "norm_ffn_g", "ada_w", "ada_b", "sb_w_qkv", "sb_w_o",
        "mla_w_in", "mla_g_q", "mla_g_kv", "mla_w_q_up", "mla_w_kv_up", "mla_w_o",
        "moe_w_group", "moe_b_group", "moe_w_router", "moe_b_router", "moe_w_gate_up", "moe_w_down", "final_g"]


def kernel(**inputs):
    import numpy as _np
    import concourse.bacc as _bacc
    from concourse import mybir as _mybir
    from concourse.bass_utils import run_bass_kernel_spmd as _run

    nc = _bacc.Bacc("TRN2", target_bir_lowering=False, num_devices=1)
    arrays, args = {}, []
    for name in _INS:
        arrays[f"in_{name}"] = _np.ascontiguousarray(inputs[name])
    half = _np.arange(0, ROPE, 2, dtype=_np.float32) / _np.float32(ROPE)
    arrays["in_inv_freq"] = _np.tile(_np.float32(THETA) ** (-half), 2 * P // ROPE).astype(_np.float32)
    for name, a in arrays.items():
        args.append(nc.dram_tensor(name, a.shape, _mybir.dt.from_np(a.dtype), kind="ExternalInput").ap())
    args.append(nc.dram_tensor("out_0", (1, T, D), _mybir.dt.float32, kind="ExternalOutput").ap())
    build(nc, *args)
    r = _run(nc, [arrays], core_ids=[0])
    return r.results[0]["out_0"]
```

```python
from contextlib import ExitStack

import concourse.bass as bass
import numpy as np
from concourse import mybir

F32 = mybir.dt.float32
F32R = mybir.dt.float32r
I32 = mybir.dt.int32
ALU = mybir.AluOpType
ACT = mybir.ActivationFunctionType
AX = mybir.AxisListType

P = 128
D = 1024
T = 256
KD = D // P
TT = T // P
HEADS = 16
DH = 64
QR, KVR, ROPE = 384, 256, 32
QK = DH + ROPE
NE, NG, EPG = 16, 4, 4
FF = 512
MOD = 6 * D // P
EPS = 1e-6
THETA = 10000.0
NEG = -1.0e30
CAP = 64
FEW = CAP
SLOTS = 8
SLOT = 4096
TQKV = 0
TWO0 = 20
TLAT = TWO0 + 8
TUP = TLAT + 6
TROT = TUP + 12
TKV = TROT + 5
TWO1 = TKV + 12
TEND = TWO1 + 8


def build(nc, x, c, positions, norm_mix_g, norm_ffn_g, ada_w, ada_b, sb_w_qkv, sb_w_o,
          mla_w_in, mla_g_q, mla_g_kv, mla_w_q_up, mla_w_kv_up, mla_w_o,
          moe_w_group, moe_b_group, moe_w_router, moe_b_router, moe_w_gate_up, moe_w_down,
          final_g, inv_freq, out):
    owner = []
    for j in range(TEND):
        alone = TWO0 <= j < TLAT or TUP + 8 <= j < TKV or j >= TWO1
        owner.append("v" if alone or j % 2 == 0 else "a")
    nth = [owner[:j + 1].count(owner[j]) for j in range(TEND)]

    stream = []
    uses = [0] * SLOTS
    where = {}

    def chunk(name, slot, src, k, n):
        uses[slot] += 1
        where[name] = (slot, uses[slot], k, n)
        stream.append((name, slot, src, k, n))

    def cols(w, a, b):
        return w[:, a:b].rearrange("(k p) n -> p k n", p=P)

    qkv_order = [("k", 0), ("q", 0), ("v", 0), ("k", 1), ("q", 1), ("v", 1)]
    phases = [[("ada0", i) for i in range(4)],
              [("ada0", i) for i in range(4, 12)] + [("ada1", i) for i in range(4)],
              [("ada1", i) for i in range(4, 12)]]
    ada_no = {a: n for n, a in enumerate(sum(phases, []))}

    def ada_chunk(a, slot):
        chunk(a, slot, cols(ada_w[int(a[0][3])], 512 * a[1], 512 * a[1] + 512), KD, 512)

    order0 = []
    for n, part in enumerate(qkv_order):
        order0 += [part] + phases[1][2 * n:2 * n + 2]
    for n, (kind, i) in enumerate(phases[0] + order0):
        if kind in ("q", "k", "v"):
            at = D * "qkv".index(kind) + 512 * i
            chunk((kind, i), n % 6, cols(sb_w_qkv[0], at, at + 512), KD, 512)
        else:
            ada_chunk((kind, i), n % 6)
    for i in range(2):
        chunk(("wo0", i), 6 + i, cols(sb_w_o[0], 512 * i, 512 * i + 512), KD, 512)
    first = [len(stream), 0]
    base = [list(uses), 0]
    for s in range(6):
        uses[s] += NE // 2
    for i in range(2):
        chunk(("win", i), i, mla_w_in[0][512 * i:512 * i + 512].rearrange("(k p) n -> p k n", p=P), 4,
              QR + KVR + ROPE)
    chunk(("kvup", 0), 2, cols(mla_w_kv_up[0], 0, 2048), KVR // P, 2048)
    for i in range(2):
        chunk(("qup", i), 6 + i, cols(mla_w_q_up[0], 768 * i, 768 * i + 768), QR // P, 768)
    for n, a in enumerate(phases[2]):
        ada_chunk(a, 6 + n % 2)
    for i in range(2):
        chunk(("wo1", i), 6 + i, cols(mla_w_o[0], 512 * i, 512 * i + 512), KD, 512)
    first[1] = len(stream)
    base[1] = list(uses)

    with ExitStack() as ctx:
        def sb(name, shape, dt=F32):
            return ctx.enter_context(nc.sbuf_tensor(name, shape, dt))

        def sem(name):
            return ctx.enter_context(nc.semaphore(name))

        end = nc.sbuf_usable_end // 64 * 64
        side = [end - 2 * 4 * SLOT, end - 4 * SLOT]

        def at(name, shape, dt, offset):
            return nc.alloc_sbuf_tensor_at(name, shape, dt, offset=offset)

        ring = [sb(f"ring{s}", [P, SLOT]) for s in range(SLOTS - 2)]
        ring += [at(f"ring{6 + n}", [P, SLOT], F32, side[n]) for n in range(2)]
        xT = sb("xT", [P, KD, T])
        hT = sb("hT", [P, KD, T])
        big_at = nc.sbuf_base
        big = sb("big", [P, 4 * 8 * T])
        assert nc.sbuf_base == big_at + 4 * 4 * 8 * T
        QT, KT, OT = (big[:, n * 8 * T:(n + 1) * 8 * T].rearrange("p (k t) -> p k t", k=8) for n in (0, 1, 3))
        V = big[:, 2 * 8 * T:3 * 8 * T].rearrange("p (t n) -> p t n", t=TT)
        ident = sb("ident", [P, P])
        ones = sb("ones", [P, P])
        neg_ones = sb("neg_ones", [P, P])
        neg_tri = sb("neg_tri", [P, P])
        strict = sb("strict", [P, P])
        bias_strict = sb("bias_strict", [P, 384])
        bias_causal = sb("bias_causal", [P, 384])
        rot = sb("rot", [P, P])
        prio = sb("prio", [P, 4])
        colA = sb("colA", [P, 72])
        colB = sb("colB", [P, 77])
        c_pad = sb("c_pad", [P, KD, 64])
        row_sel = sb("row_sel", [P, 12])
        mod = sb("mod", [P, 2, MOD])
        gs = sb("gs", [P, 4, KD])
        freq = sb("freq", [P, 1])
        cosT = sb("cosT", [P, T])
        sinT = sb("sinT", [P, T])
        rstd = sb("rstd", [P, 2, T])
        scratch = sb("scratch", [P, 10 * 384])
        sc = [[scratch[:, (2 * i + b) * 384:(2 * i + b + 1) * 384] for b in range(2)] for i in range(5)]
        st = [sb(f"st{b}", [P, 8]) for b in range(2)]
        wr = sb("wr", [P, 2, KD, NG + NE])
        br = sb("br", [P, 2, NG + NE])
        lg = sb("lg", [P, TT, NG + NE])
        mask = sb("mask", [P, TT, NE])
        slot_no = sb("slot_no", [P, CAP])
        most = sb("most", [P, 1])
        most_i = sb("most_i", [P, 1], I32)
        slot_gate = sb("slot_gate", [P, NE // 2])
        gates = sb("gates", [P, TT, NE])
        k_rope = sb("k_rope", [P, T])

        assert nc.sbuf_base <= side[0]
        zeros = bias_causal[:, P:2 * P]

        rowsA, rowsB = sc[2][0][:, 0:P], sc[2][1][:, 0:P]
        ada_rows = scratch[:, 0:512]
        slot_i = sc[1][0][:, 0:CAP].bitcast(I32)
        x_nat = V
        sq = V.rearrange("p t (k n) -> p (t k) n", n=T)
        lat = OT
        q_rope = [hT[:, 5, :], hT[:, 6, :], hT[:, 7, :], bias_strict[:, 0:T]]
        pos_i = sc[4][0][:, 0:T].bitcast(I32)
        raw_rope = [OT[:, 0, :], OT[:, 1, :], OT[:, 2, :], OT[:, 3, :], OT[:, 5, :]]
        ang, turns, sin_part = sc[3][0][:, 0:T], sc[3][1][:, 0:T], OT[:, 6, :]
        hg = [QT[:, 0:4, :], QT[:, 4:8, :]]
        silu = [sc[0][b][:, 0:T] for b in range(2)]
        gate_row = [sc[1][b][:, 0:T] for b in range(2)]
        diag = sc[2][0][:, 0:T].rearrange("p (t n) -> p t n", t=TT)
        GU = [[ring[3 * b + i][:, :].rearrange("p (k n) -> p k n", k=4) for i in range(2)] for b in range(2)]
        q_nope_w = ring[3][:, 0:3 * D].rearrange("p (k n) -> p k n", k=3)
        q_rope_w = KT[:, 0:6, :].rearrange("p (k a) t -> p k (a t)", k=3)
        k_nope_w = ring[4][:, 0:2 * D].rearrange("p (k n) -> p k n", k=2)
        k_rope_w = ring[4][:, 2 * D:2 * D + KD * P].rearrange("p (k n) -> p k n", k=KD)
        tok = [at(f"tok{n}", [P, TT, D], F32R, side[0] + n * 4 * TT * D) for n in range(2)]
        Y = [at(f"Y{n}", [P, D], F32R, big_at + 4 * (2 * 8 * T + n * D)) for n in range(2)]
        pick = at("pick", [P, TT, NE * CAP], F32R, side[1])
        pick_T = at("pick_T", [P, NE // 2, T], F32R, side[1] + 4 * TT * NE * CAP)
        XG = big[:, 0:KD * 2 * CAP].rearrange("p (k s) -> p k s", k=KD)
        silu_pair, h_pair = OT[:, 0:2, :].rearrange("p a t -> p (a t)"), OT[:, 2:4, :].rearrange("p a t -> p (a t)")
        hT_pair = big[:, 3 * 8 * T + 4 * T:3 * 8 * T + 6 * T].rearrange("p (f s) -> p f s", f=4)
        DN = [ring[3 * b + 2][:, :].rearrange("p (k n) -> p k n", k=4) for b in range(2)]

        banks = [ctx.enter_context(nc.psum_tensor(f"bank{b}", [P, 512], F32)) for b in range(8)]

        consts = sem("consts")
        pool_chain = sem("pool_chain")
        packed = sem("packed")
        dve_chain = sem("dve_chain")
        act_chain = sem("act_chain")
        x_loaded = sem("x_loaded")
        rows_loaded = sem("rows_loaded")
        small_loaded = sem("small_loaded")
        loaded = [sem(f"loaded{s}") for s in range(SLOTS)]
        x_turned = sem("x_turned")
        x_ready = sem("x_ready")
        rows_turned = sem("rows_turned")
        cols_ready = sem("cols_ready")
        c_ready = sem("c_ready")
        ada_done = sem("ada_done")
        ada_kept = sem("ada_kept")
        mod_done = sem("mod_done")
        mod_ready = sem("mod_ready")
        sq_ready = sem("sq_ready")
        ss_done = sem("ss_done")
        ms_ready = sem("ms_ready")
        std_ready = sem("std_ready")
        scaled_ready = sem("scaled_ready")
        h_ready = sem("h_ready")
        tile_done = sem("tile_done")
        tile_kept = {"v": sem("tile_kept_vector"), "a": sem("tile_kept_scalar")}
        trig_in = sem("trig_in")
        trig_ready = sem("trig_ready")
        z_done = sem("z_done")
        soft_ready = sem("soft_ready")
        sp_ready = sem("sp_ready")
        spm_ready = sem("spm_ready")
        sticks_done = sem("sticks_done")
        log_ready = sem("log_ready")
        a_ready = sem("a_ready")
        o_done = sem("o_done")
        o_ready = sem("o_ready")
        s_done = sem("s_done")
        masked_ready = sem("masked_ready")
        neg_ready = sem("neg_ready")
        p_ready = sem("p_ready")
        pn_ready = sem("pn_ready")
        pt_done = sem("pt_done")
        aT_ready = sem("aT_ready")
        rope_ready = sem("rope_ready")
        logit_done = sem("logit_done")
        route_in = sem("route_in")
        route_out = sem("route_out")
        gu_done = sem("gu_done")
        down_done = sem("down_done")
        hn_turned = sem("hn_turned")
        hn_high = sem("hn_high")
        hn_ready = sem("hn_ready")
        mask_ready = sem("mask_ready")
        rank_done = sem("rank_done")
        most_ready = sem("most_ready")
        gates_ready = sem("gates_ready")
        acc_done = sem("acc_done")

        class PerLayer:
            def __init__(self, layer):
                def own(name):
                    return sem(f"{name}_{layer}")

                self.diag_ready = own("diag_ready")
                self.gate_done = own("gate_done")
                self.gate_ready = own("gate_ready")
                self.silu_ready = own("silu_ready")
                self.gu_read = own("gu_read")
                self.hg_ready = own("hg_ready")
                self.rank_ready = own("rank_ready")
                self.pick_ready = own("pick_ready")
                self.slot_gate_done = own("slot_gate_done")
                self.slot_gate_ready = own("slot_gate_ready")
                self.pick_turned = own("pick_turned")
                self.pick_T_ready = own("pick_T_ready")
                self.gathered = own("gathered")
                self.xg_kept = {"v": own("xg_kept_vector"), "a": own("xg_kept_scalar")}
                self.act_ready = own("act_ready")
                self.h_ready = own("h_ready")
                self.h_turned = own("h_turned")
                self.hT_ready = own("hT_ready")
                self.y_high = own("y_high")
                self.y_done = own("y_done")
                self.scattered = own("scattered")

        per_layer = [PerLayer(layer) for layer in range(2)]
        y_turned = sem("y_turned")
        y_ready = sem("y_ready")
        stored = sem("stored")

        used_up = {}
        for a, n in ada_no.items():
            used_up[a] = (ada_done, n + 1)
        for half in range(2):
            used_up[("k", half)] = (tile_done, 10 * half + 4)
            used_up[("q", half)] = (tile_done, 10 * half + 8)
            used_up[("v", half)] = (tile_done, 10 * half + 10)
            used_up[("wo0", half)] = (tile_done, TWO0 + 4 * half + 4)
            used_up[("win", half)] = (tile_done, TUP)
            used_up[("qup", half)] = (packed, 5)
            used_up[("wo1", half)] = (tile_done, TWO1 + 4 * half + 4)
            used_up[("win", half)] = (tile_done, TUP)
        used_up[("kvup", 0)] = (tile_done, TWO1)

        def weights(name):
            slot, _, k, n = where[name]
            return ring[slot][:, 0:k * n].rearrange("p (k n) -> p k n", k=k)

        def wait_weights(eng, name):
            slot, use, _, _ = where[name]
            eng.wait_ge(loaded[slot], 16 * use)

        def wait_tiles(eng, last):
            for kind in "va":
                count = owner[:last + 1].count(kind)
                if count:
                    eng.wait_ge(tile_kept[kind], count)

        block = ctx.enter_context(nc.Block())

        @block.sync
        def _(sp):
            sp.dma_start(x_nat[:, :, :], x[0].rearrange("(t p) d -> p t d", p=P)).then_inc(x_loaded, 16)
            before = [None] * SLOTS

            def load(entry):
                name, slot, src, k, n = entry
                if before[slot] is not None:
                    sp.wait_ge(*before[slot])
                sp.dma_start(ring[slot][:, 0:k * n].rearrange("p (k n) -> p k n", k=k), src).then_inc(loaded[slot], 16)
                before[slot] = used_up[name]

            def load_expert_part(layer, b, part, e):
                slot = 3 * b + part
                if part < 2:
                    src = moe_w_gate_up[layer][e, 512 * part:512 * part + 512, :]
                else:
                    src = moe_w_down[layer][e, :, :]
                sp.dma_start(ring[slot][:, :].rearrange("p (k n) -> p k n", k=4),
                             src.rearrange("e (k p) n -> p (e k) n", p=P)).then_inc(loaded[slot], 16)

            parts = [(0, 0), (1, 0), (0, 1), (1, 1), (0, 2), (1, 2)]

            def experts(layer):
                for b, part in parts:
                    sp.wait_ge(*before[3 * b + part])
                    load_expert_part(layer, b, part, bass.ds(b, 1))
                with sp.Fori(1, NE // 2) as i:
                    for b, part in parts:
                        if part < 2:
                            sp.wait_ge(gu_done, i * 8 + (64 * layer - 4 * (b == 0 and part == 0)))
                        else:
                            sp.wait_ge(down_done, i * 2 + (17 * layer + b))
                        load_expert_part(layer, b, part, bass.ds(i * 2 + b, 1))
                for b in range(2):
                    before[3 * b] = before[3 * b + 1] = (gu_done, 64 * (layer + 1))
                    before[3 * b + 2] = (down_done, 17 * layer + NE + b)
                before[3] = (tile_done, TUP + 8)
                before[4] = (tile_done, TKV + 8)
                before[6] = before[7] = (x_ready, 4 + 8 * (layer + 1))

            for entry in stream[:first[0]]:
                load(entry)
            experts(0)
            for entry in stream[first[0]:first[1]]:
                load(entry)
            experts(1)
            sp.wait_ge(y_ready, 4)
            sp.dma_start(out[0].rearrange("(t p) d -> p t d", p=P), V[:, :, :]).then_inc(stored, 16)
            sp.wait_ge(stored, 16)

        @block.gpsimd
        def _(pool):
            nc.gpsimd.memset(ident[:, :], 0.0).then_inc(pool_chain, 1)
            pool.wait_ge(pool_chain, 1)
            nc.gpsimd.affine_select(out=ident[:, :], in_=ident[:, :], compare_op=ALU.not_equal, fill=1.0, base=0,
                                    pattern=[[-1, P]], channel_multiplier=1).then_inc(consts, 1)
            nc.gpsimd.memset(ones[:, :], 1.0).then_inc(consts, 1)
            nc.gpsimd.memset(c_pad[:, :, :], 0.0).then_inc(consts, 1)
            nc.gpsimd.memset(row_sel[:, :], 0.0).then_inc(pool_chain, 1)
            for g in range(4):
                pool.wait_ge(pool_chain, 2 + g)
                ins = nc.gpsimd.affine_select(out=row_sel[:, :], in_=row_sel[:, :], compare_op=ALU.not_equal, fill=1.0,
                                              base=-32 * g, pattern=[[-1, 12]], channel_multiplier=1)
                ins.then_inc(pool_chain, 1) if g < 3 else ins.then_inc(consts, 1)
            pool.dma_start(pos_i, positions.broadcast_to([P, T])).then_inc(small_loaded, 16)
            pool.dma_start(freq[:, :], inv_freq.rearrange("(p o) -> p o", o=1)).then_inc(small_loaded, 16)
            for l in range(2):
                pool.dma_start(wr[:, l, :, 0:NG], moe_w_group[l].rearrange("(k p) n -> p k n", p=P)).then_inc(small_loaded, 16)
                pool.dma_start(wr[:, l, :, NG:], moe_w_router[l].rearrange("(k p) n -> p k n", p=P)).then_inc(small_loaded, 16)
                pool.dma_start(br[:, l, 0:NG], moe_b_group[l:l + 1].broadcast_to([P, NG])).then_inc(small_loaded, 16)
                pool.dma_start(br[:, l, NG:], moe_b_router[l:l + 1].broadcast_to([P, NE])).then_inc(small_loaded, 16)
            nc.gpsimd.iota(slot_i[:, :], pattern=[[1, CAP]], base=1, channel_multiplier=0)
            nc.gpsimd.memset(neg_ones[:, :], -1.0)
            for j in range(4):
                nc.gpsimd.memset(prio[:, j:j + 1], float(4 - j))
            nc.gpsimd.memset(neg_tri[:, :], -1.0)
            nc.gpsimd.memset(strict[:, :], 1.0)
            nc.gpsimd.memset(bias_strict[:, :], 0.0)
            nc.gpsimd.memset(bias_causal[:, :], 0.0)
            nc.gpsimd.memset(rot[:, :], 0.0).then_inc(pool_chain, 1)
            pool.wait_ge(pool_chain, 6)
            nc.gpsimd.tensor_copy(slot_no[:, :], slot_i[:, :])
            nc.gpsimd.affine_select(out=neg_tri[:, :], in_=neg_tri[:, :], compare_op=ALU.is_ge, fill=0.0, base=0,
                                    pattern=[[-1, P]], channel_multiplier=1)
            nc.gpsimd.affine_select(out=strict[:, :], in_=strict[:, :], compare_op=ALU.is_gt, fill=0.0, base=0,
                                    pattern=[[1, P]], channel_multiplier=-1)
            for part in (0, 256):
                nc.gpsimd.affine_select(out=bias_strict[:, part:part + P], in_=bias_strict[:, part:part + P],
                                        compare_op=ALU.is_gt, fill=NEG, base=0, pattern=[[1, P]],
                                        channel_multiplier=-1)
                nc.gpsimd.affine_select(out=bias_causal[:, part:part + P], in_=bias_causal[:, part:part + P],
                                        compare_op=ALU.is_ge, fill=NEG, base=0, pattern=[[-1, P]],
                                        channel_multiplier=1)
            halves = rot[:, :].rearrange("p (b h j) -> p b h j", b=4, h=2)
            nc.gpsimd.affine_select(out=halves[:, :, 0, :], in_=halves[:, :, 0, :], compare_op=ALU.not_equal,
                                    fill=-1.0, base=-16, pattern=[[-32, 4], [-1, 16]], channel_multiplier=1)
            nc.gpsimd.affine_select(out=halves[:, :, 1, :], in_=halves[:, :, 1, :], compare_op=ALU.not_equal,
                                    fill=1.0, base=0, pattern=[[-32, 4], [-1, 16]],
                                    channel_multiplier=1).then_inc(consts, 1)
            for h in range(HEADS):
                pool.wait_ge(sp_ready, h + 1)
                for at in (0, 256):
                    ins = nc.gpsimd.tensor_tensor(sc[2][h % 2][:, at:at + P], sc[2][h % 2][:, at:at + P],
                                                  strict[:, :], ALU.mult)
                ins.then_inc(spm_ready, 1)
            def gate_experts(layer):
                q = per_layer[layer]
                pool.wait_ge(most_ready, layer + 1)
                with pool.If(pool.value_load(most_i[0:1, 0:1], min_val=0, max_val=T) > FEW):
                    with pool.Fori(0, NE // 2) as i:
                        for b in range(2):
                            pool.wait_ge(q.gate_ready, i * 2 + (b + 1))
                            for f in range(4):
                                pool.wait_ge(q.gu_read, i * 8 + (4 * b + f + 3))
                                nc.gpsimd.tensor_tensor(hg[b][:, f, :], hg[b][:, f, :], gate_row[b],
                                                        ALU.mult).then_inc(q.hg_ready, 1)

            def pack_mixer1():
                pool.wait_ge(gu_done, 4 * NE)
                pool.wait_ge(down_done, 1 + NE)
                for i in range(2):
                    wait_weights(pool, ("win", i))
                    nc.gpsimd.tensor_copy(
                        k_rope_w[:, 4 * i:4 * i + 4, :].rearrange("p k (c r) -> p k c r", c=4),
                        weights(("win", i))[:, :, QR + KVR:].unsqueeze(2).broadcast_to([P, 4, 4, ROPE])).then_inc(packed, 1)
                wait_weights(pool, ("kvup", 0))
                nc.gpsimd.tensor_copy(k_nope_w.rearrange("p k (h d) -> p k h d", d=DH),
                                      weights(("kvup", 0)).rearrange("p k (h d) -> p k h d", d=2 * DH)[:, :, :, 0:DH]) \
                    .then_inc(packed, 1)
                for i in range(2):
                    wait_weights(pool, ("qup", i))
                    w = weights(("qup", i)).rearrange("p k (h d) -> p k h d", d=QK)
                    nc.gpsimd.tensor_copy(q_nope_w[:, :, 512 * i:512 * i + 512].rearrange("p k (h d) -> p k h d", d=DH),
                                          w[:, :, :, 0:DH])
                    ins = nc.gpsimd.tensor_copy(
                        q_rope_w[:, :, 256 * i:256 * i + 256].rearrange("p k (h d) -> p k h d", d=ROPE),
                        w[:, :, :, DH:QK])
                    ins.then_inc(packed, 1)

            gate_experts(0)
            pack_mixer1()
            gate_experts(1)

        @block.tensor
        def _(pe):
            tile_no = [0]

            def projection(lhs, rhs, ks, n=T):
                j = tile_no[0]
                if j >= 4:
                    pe.wait_ge(tile_kept[owner[j - 4]], nth[j - 4])
                tile_no[0] += 1
                for k in range(ks):
                    mm = pe.matmul(banks[j % 4][:, 0:n], lhs(k), rhs(k), start=(k == 0), stop=(k == ks - 1))
                mm.then_inc(tile_done, 1)

            def sum_squares(tiles, squares, at=0, bank=6):
                for n, k in enumerate(tiles):
                    pe.wait_ge(sq_ready, squares + n + 1)
                    mm = pe.matmul(banks[bank][:, at:at + T], ones[:, :], sq[:, k, :],
                                   start=(k == tiles[0]), stop=(k == tiles[-1]))
                mm.then_inc(ss_done, 1)

            def ada(a):
                phase = [a in phase for phase in phases].index(True)
                m = phases[phase].index(a)
                wait_weights(pe, a)
                if m == 0 and phase:
                    pe.wait_ge(ada_kept, phase)
                w = weights(a)
                for j in range(2):
                    for g in range(4):
                        k = 2 * g + j
                        mm = pe.matmul(banks[6][32 * g:32 * g + 32, :], c_pad[:, k, 31 - m:63 - m], w[:, k, :],
                                       start=(m == 0 and j == 0), stop=(a == phases[phase][-1] and j == 1),
                                       skip_group_check=True)
                mm.then_inc(ada_done, 1)

            def ada_columns(phase):
                n = len(phases[phase])
                pe.wait_ge(ada_kept, phase + 1)
                for j in range(4):
                    mm = pe.matmul(banks[7][:, j * n:(j + 1) * n], ada_rows[:, j * P:(j + 1) * P], row_sel[:, 0:n],
                                   start=True, stop=True)
                mm.then_inc(mod_done, 1)

            pe.wait_ge(consts, 2)
            pe.wait_ge(rows_loaded, 160)
            pe.transpose(banks[6][:, 0:72], rowsA[0:72, :], ident[0:72, 0:72])
            pe.transpose(banks[6][:, 128:205], rowsB[0:77, :], ident[0:77, 0:77]).then_inc(rows_turned, 1)
            pe.wait_ge(x_loaded, 16)
            for b in range(4):
                for k in range(2):
                    for t in range(TT):
                        tr = pe.transpose(banks[b][:, k * T + t * P:k * T + (t + 1) * P],
                                          x_nat[:, t, (2 * b + k) * P:(2 * b + k + 1) * P], ident[:, :])
                tr.then_inc(x_turned, 1)
            pe.wait_ge(cols_ready, 1)
            pe.wait_ge(c_ready, 1)
            sum_squares(range(KD), 0, bank=5)
            pe.wait_ge(consts, 4)
            for a in phases[0]:
                ada(a)
            ada_columns(0)

            pe.wait_ge(h_ready, KD)
            for n, (kind, half) in enumerate(qkv_order):
                wait_weights(pe, (kind, half))
                w = weights((kind, half))
                if kind == "v":
                    for t in range(TT):
                        projection(lambda k: hT[:, k, t * P:(t + 1) * P], lambda k: w[:, k, :], KD, 512)
                else:
                    for j in range(4):
                        projection(lambda k: w[:, k, j * P:(j + 1) * P], lambda k: hT[:, k, :], KD)
                for a in phases[1][2 * n:2 * n + 2]:
                    ada(a)

            def scores0(h):
                p, r = h // 2, 64 * (h % 2)
                z = banks[h % 4]
                if h >= 4:
                    pe.wait_ge(log_ready, h - 3)
                pe.matmul(z[:, 0:256], KT[r:r + 64, p, 0:P], QT[r:r + 64, p, :], start=True, stop=False,
                          skip_group_check=True)
                pe.matmul(z[:, 256:384], KT[r:r + 64, p, P:T], QT[r:r + 64, p, P:T], start=False, stop=False,
                          skip_group_check=True).then_inc(z_done, 1)

            def sticks(h):
                z, spm = banks[h % 4], sc[2][h % 2]
                pe.wait_ge(spm_ready, h + 1)
                pe.matmul(z[:, 0:256], neg_tri[:, :], spm[:, 0:256], start=False, stop=False, skip_group_check=True)
                pe.matmul(z[:, 128:256], neg_ones[:, :], spm[:, 256:384], start=False, stop=False,
                          skip_group_check=True)
                pe.matmul(z[:, 256:384], neg_tri[:, :], spm[:, 256:384], start=False, stop=True,
                          skip_group_check=True).then_inc(sticks_done, 1)

            def values(layer, h, ready):
                p, r, a = h // 2, 64 * (h % 2), sc[3][h % 2]
                o = banks[4 + p % 2]
                pe.wait_ge(ready, h + 1)
                if r == 0 and 8 * layer + p >= 2:
                    pe.wait_ge(o_ready, 8 * layer + p - 1)
                pe.matmul(o[r:r + 64, 0:256], V[:, 0, h * DH:(h + 1) * DH], a[:, 0:256], start=True, stop=False,
                          skip_group_check=True)
                pe.matmul(o[r:r + 64, 128:256], V[:, 1, h * DH:(h + 1) * DH], a[:, 256:384], start=False, stop=True,
                          skip_group_check=True).then_inc(o_done, 1)

            wait_tiles(pe, TWO0 - 1)
            pe.wait_ge(consts, 5)
            for h in range(HEADS + 3):
                if h < HEADS:
                    scores0(h)
                if h == 0:
                    ada_columns(1)
                if 1 <= h <= HEADS:
                    sticks(h - 1)
                if h >= 3:
                    values(0, h - 3, a_ready)

            def out_projection(kind, layer):
                pe.wait_ge(o_ready, 8 * (layer + 1))
                for i in range(2):
                    wait_weights(pe, (kind, i))
                    w = weights((kind, i))
                    for j in range(4):
                        projection(lambda k: w[:, k, j * P:(j + 1) * P], lambda k: OT[:, k, :], KD)

            out_projection("wo0", 0)

            def moe(layer):
                sum_squares(range(KD), (8, 29)[layer])
                pe.wait_ge(h_ready, (16, 37)[layer])
                pe.wait_ge(small_loaded, 160)
                for t in range(TT):
                    for k in range(KD):
                        mm = pe.matmul(banks[7][:, t * 32:t * 32 + NG + NE], hT[:, k, t * P:(t + 1) * P],
                                       wr[:, layer, k, :], start=(k == 0), stop=(k == KD - 1))
                mm.then_inc(logit_done, 1)
                for t in range(TT):
                    for half in range(2):
                        for k in range(4):
                            tr = pe.transpose(banks[2 * t + half][:, k * P:(k + 1) * P],
                                              hT[:, 4 * half + k, t * P:(t + 1) * P], ident[:, :])
                        tr.then_inc(hn_turned, 1)
                pe.wait_ge(mask_ready, layer + 1)
                for t in range(TT):
                    at = banks[6][:, t * NE:(t + 1) * NE]
                    if t:
                        pe.matmul(at, ones[:, :], mask[:, 0, :], start=True, stop=False)
                    pe.matmul(at, strict[:, :], mask[:, t, :], start=(t == 0), stop=True)
                pe.matmul(banks[6][:, 32:32 + NE], ones[:, :], mask[:, 0, :], start=True, stop=False)
                pe.matmul(banks[6][:, 32:32 + NE], ones[:, :], mask[:, 1, :], start=False,
                          stop=True).then_inc(rank_done, 1)
                pe.wait_ge(hn_ready, 4 * (layer + 1))
                pe.wait_ge(most_ready, layer + 1)
                few = pe.value_load(most_i[0:1, 0:1], min_val=0, max_val=T)
                with pe.If(few > FEW):
                    clear_accumulators()
                    dense_experts(layer)
                with pe.Else():
                    sparse_experts(layer)
                pe.drain().then_inc(acc_done, 1)

            def clear_accumulators():
                for b in range(4):
                    mm = pe.matmul(banks[b][:, :], zeros[:, :], zeros[:, :].unsqueeze(1).broadcast_to([P, 4, P]),
                                   start=True, stop=False, skip_group_check=True)
                mm.then_inc(down_done, 1)

            def dense_experts(layer):
                q = per_layer[layer]
                with pe.Fori(0, NE // 2) as i:
                    for b in range(2):
                        pe.wait_ge(q.diag_ready, i * 2 + (b + 1))
                        for t in range(TT):
                            mm = pe.matmul(banks[6][:, t * P:(t + 1) * P], ones[:, :], diag[:, t, :],
                                           start=True, stop=True)
                        mm.then_inc(q.gate_done, 1)
                        for part in range(2):
                            pe.wait_ge(loaded[3 * b + part], i * 16 + 16 * (base[layer][3 * b + part] + 1))
                        for f in range(4):
                            pe.wait_ge(q.gu_read, i * 8 + (4 * b + f + 1))
                            for u in range(2):
                                for k in range(KD):
                                    mm = pe.matmul(banks[4 + f % 2][:, u * T:(u + 1) * T],
                                                   GU[b][k // 4][:, k % 4, u * FF + f * P:u * FF + (f + 1) * P],
                                                   hT[:, k, :], start=(k == 0), stop=(k == KD - 1))
                            mm.then_inc(gu_done, 1)
                        pe.wait_ge(loaded[3 * b + 2], i * 16 + 16 * (base[layer][3 * b + 2] + 1))
                        for f in range(4):
                            pe.wait_ge(q.hg_ready, i * 8 + (4 * b + f + 1))
                            for d in range(KD):
                                mm = pe.matmul(banks[d // 2][:, (d % 2) * T:(d % 2 + 1) * T],
                                               DN[b][:, f, d * P:(d + 1) * P], hg[b][:, f, :],
                                               start=False, stop=False, skip_group_check=True)
                        mm.then_inc(down_done, 1)

            def gather(layer, i, half):
                q = per_layer[layer]
                for d in range(4):
                    for t in range(TT):
                        for part in range(2):
                            mm = pe.matmul(banks[5 - half][:, d * P:(d + 1) * P],
                                           tok[part][:, t, (4 * half + d) * P:(4 * half + d + 1) * P],
                                           pick[:, t, bass.ds(i * (2 * CAP), 2 * CAP)], start=(t + part == 0),
                                           stop=(t + part == 2))
                mm.then_inc(q.gathered, 1)

            def gate_up(layer, i):
                q = per_layer[layer]
                pe.wait_ge(q.xg_kept["v"], i + 1)
                pe.wait_ge(q.xg_kept["a"], i + 1)
                for k in range(KD):
                    if k % 4 == 0:
                        for b in range(2):
                            slot = 3 * b + k // 4
                            pe.wait_ge(loaded[slot], i * 16 + 16 * (base[layer][slot] + 1))
                    for u in range(2):
                        for b in range(2):
                            mm = pe.matmul(banks[4 + u][CAP * b:CAP * (b + 1), :], XG[:, k, CAP * b:CAP * (b + 1)],
                                           GU[b][k // 4][:, k % 4, u * FF:(u + 1) * FF],
                                           start=(k == 0), stop=(k == KD - 1))
                    mm.then_inc(gu_done, 1)

            def turn_h(layer, i):
                q = per_layer[layer]
                pe.wait_ge(q.h_ready, i + 1)
                for f in range(4):
                    tr = pe.transpose(banks[4][:, f * P:(f + 1) * P], h_pair[:, f * P:(f + 1) * P], ident[:, :])
                tr.then_inc(q.h_turned, 1)

            def down(layer, i, first):
                q = per_layer[layer]
                pe.wait_ge(q.hT_ready, i + 1)
                if not first:
                    pe.wait_ge(q.y_done, i)
                for b in range(2):
                    pe.wait_ge(loaded[3 * b + 2], i * 16 + 16 * (base[layer][3 * b + 2] + 1))
                for f in range(4):
                    for half in range(2):
                        for b in range(2):
                            mm = pe.matmul(banks[6 + half][CAP * b:CAP * (b + 1), :],
                                           hT_pair[:, f, CAP * b:CAP * (b + 1)],
                                           DN[b][:, f, 512 * half:512 * half + 512], start=(f == 0), stop=(f == 3))
                            if f == 3 and half == 1:
                                mm.then_inc(down_done, 1)

            def scatter(layer, i):
                q = per_layer[layer]
                pe.wait_ge(q.y_done, i + 1)
                for part in range(2):
                    for d in range(KD):
                        mm = pe.matmul(banks[d // 2][:, (d % 2) * T:(d % 2 + 1) * T], Y[part][:, d * P:(d + 1) * P],
                                       pick_T[:, bass.ds(i, 1), :].rearrange("p a t -> p (a t)"),
                                       start=False, stop=False, skip_group_check=True)
                mm.then_inc(q.scattered, 1)

            def sparse_experts(layer):
                q = per_layer[layer]
                pe.wait_ge(q.pick_ready, 1)
                pe.wait_ge(gates_ready, layer + 1)
                for p in range(NE // 2):
                    for t in range(TT):
                        mm = pe.matmul(banks[7][:, 2 * p:2 * p + 2], pick[:, t, p * P:(p + 1) * P].bitcast(F32),
                                       gates[:, t, 2 * p:2 * p + 2], start=(t == 0), stop=(t == 1))
                mm.then_inc(q.slot_gate_done, 1)
                for b in range(4):
                    for n in range(4):
                        p, t = 2 * b + n // 2, n % 2
                        tr = pe.transpose(banks[b][:, n * P:(n + 1) * P], pick[:, t, p * P:(p + 1) * P].bitcast(F32),
                                          ident[:, :])
                    tr.then_inc(q.pick_turned, 1)
                pe.wait_ge(q.slot_gate_ready, 1)
                gather(layer, 0, 0)
                gather(layer, 0, 1)
                pe.wait_ge(q.pick_T_ready, 4)
                clear_accumulators()

                def pair(i, first=False, last=False):
                    gate_up(layer, i)
                    if not first:
                        scatter(layer, i - 1)
                    turn_h(layer, i)
                    if not last:
                        gather(layer, i + 1, 0)
                        pe.wait_ge(q.hT_ready, i + 1)
                        gather(layer, i + 1, 1)
                    down(layer, i, first)

                pair(0, first=True)
                with pe.Fori(1, NE // 2 - 1) as i:
                    pair(i)
                pair(NE // 2 - 1, last=True)
                scatter(layer, NE // 2 - 1)

            moe(0)

            sum_squares(range(KD), 16)
            pe.wait_ge(h_ready, 24)
            for i in range(2):
                wait_weights(pe, ("win", i))
            win = [weights(("win", i)) for i in range(2)]
            for j in range(5):
                projection(lambda k: win[k // 4][:, k % 4, j * P:(j + 1) * P], lambda k: hT[:, k, :], KD)
            pe.wait_ge(packed, 2)
            projection(lambda k: k_rope_w[:, k, :], lambda k: hT[:, k, :], KD)
            sum_squares(range(3), 24)
            pe.wait_ge(ms_ready, 4)
            sum_squares(range(3, 5), 27, at=T)
            pe.wait_ge(h_ready, 29)
            pe.wait_ge(packed, 5)
            for p in range(8):
                projection(lambda k: q_nope_w[:, k, p * P:(p + 1) * P], lambda k: hT[:, k, :], 3)
            for g in range(4):
                projection(lambda k: q_rope_w[:, k, g * P:(g + 1) * P], lambda k: hT[:, k, :], 3)
            for g in range(5):
                wait_tiles(pe, TUP + 8 + g if g < 4 else TUP + 11)
                projection(lambda k: rot[:, :], lambda k: raw_rope[g], 1)
            wait_weights(pe, ("kvup", 0))
            kvup = weights(("kvup", 0)).rearrange("p k (h d) -> p k h d", d=2 * DH)
            for p in range(8):
                projection(lambda k: k_nope_w[:, k, p * P:(p + 1) * P], lambda k: hT[:, 3 + k, :], 2)
            for t in range(TT):
                for half in range(2):
                    projection(lambda k: hT[:, 3 + k, t * P:(t + 1) * P],
                               lambda k: kvup[:, k, 8 * half:8 * half + 8, DH:2 * DH], 2, 512)

            def scores1(h):
                p, r, g, q = h // 2, 64 * (h % 2), h // 4, 32 * (h % 4)
                s = banks[h % 2]
                if h >= 2:
                    pe.wait_ge(masked_ready, 2 * (h - 1))
                pe.matmul(s[:, 0:P], QT[r:r + 64, p, 0:P], KT[r:r + 64, p, 0:P], start=True, stop=False,
                          skip_group_check=True)
                pe.matmul(s[:, P:384], QT[r:r + 64, p, P:T], KT[r:r + 64, p, :], start=False, stop=False,
                          skip_group_check=True)
                pe.matmul(s[:, 0:P], q_rope[g][q:q + 32, 0:P], k_rope[q:q + 32, 0:P], start=False, stop=False,
                          skip_group_check=True, tile_position=(q, 0))
                pe.matmul(s[:, P:384], q_rope[g][q:q + 32, P:T], k_rope[q:q + 32, :], start=False, stop=True,
                          skip_group_check=True, tile_position=(q, 0)).then_inc(s_done, 1)

            def turn(h):
                probs, pt = sc[1][h % 2], banks[2 + h % 2]
                pe.wait_ge(pn_ready, h + 1)
                if h >= 2:
                    pe.wait_ge(aT_ready, h - 1)
                for n in range(3):
                    tr = pe.transpose(pt[:, n * P:(n + 1) * P], probs[:, n * P:(n + 1) * P], ident[:, :])
                tr.then_inc(pt_done, 1)

            wait_tiles(pe, TWO1 - 1)
            pe.wait_ge(rope_ready, 5)
            for h in range(HEADS + 3):
                if h < HEADS:
                    scores1(h)
                if 2 <= h < HEADS + 2:
                    turn(h - 2)
                if h >= 3:
                    values(1, h - 3, aT_ready)
                if h < HEADS and h % 2:
                    ada(phases[2][h // 2])
            ada_columns(2)
            out_projection("wo1", 1)
            moe(1)
            sum_squares(range(KD), 37)
            pe.wait_ge(h_ready, 45)
            for b in range(4):
                t, half = b // 2, b % 2
                for k in range(4):
                    tr = pe.transpose(banks[b][:, k * P:(k + 1) * P], hT[:, 4 * half + k, t * P:(t + 1) * P],
                                      ident[:, :])
                tr.then_inc(y_turned, 1)

        def qkv_place(j):
            half, r = j // 10, j % 10
            if r < 4:
                return KT[:, 4 * half + r, :], T, 1.0
            if r < 8:
                return QT[:, 4 * half + r - 4, :], T, DH ** -0.5
            return V[:, r - 8, 512 * half:512 * half + 512], 512, 1.0

        def latent_place(j):
            if j < TUP:
                return lat[:, j - TLAT, :], T
            if j < TUP + 8:
                return QT[:, j - TUP, :], T
            if j < TROT:
                return raw_rope[j - TUP - 8], T
            if j < TKV + 8:
                return KT[:, j - TKV, :], T
            n = j - TKV - 8
            return V[:, n // 2, 512 * (n % 2):512 * (n % 2) + 512], 512

        @block.vector
        def _(dve):
            v = nc.vector
            links = [0]

            def link(ins):
                links[0] += 1
                ins.then_inc(dve_chain, 1)
                dve.wait_ge(dve_chain, links[0])

            dve.wait_ge(rows_turned, 1)
            v.tensor_copy(colA[:, 0:72], banks[6][:, 0:72])
            v.tensor_copy(colB[:, 0:77], banks[6][:, 128:205]).then_inc(cols_ready, 1)
            dve.wait_ge(cols_ready, 1)
            for b in range(4):
                dve.wait_ge(x_turned, b + 1)
                v.tensor_copy(xT[:, 2 * b:2 * b + 2, :], banks[b][:, :].rearrange("p (k t) -> p k t", k=2)) \
                    .then_inc(x_ready, 1)

            def mean_square(number, d, at=0, bank=6):
                dve.wait_ge(ss_done, number)
                v.tensor_scalar(rstd[:, at // T, :], banks[bank][:, at:at + T], 1.0 / d, EPS, ALU.mult,
                                ALU.add).then_inc(ms_ready, 1)

            def norm(number, gain, shift, bank=6):
                mean_square(number, D, 0, bank)
                dve.wait_ge(std_ready, number)
                link(v.reciprocal(rstd[:, 0, :], rstd[:, 0, :]))
                for k in range(KD):
                    ins = v.scalar_tensor_tensor(out=hT[:, k, :], in0=xT[:, k, :], scalar=gain[:, k:k + 1],
                                                 in1=rstd[:, 0, :], op0=ALU.mult, op1=ALU.mult)
                    ins.then_inc(h_ready if shift is None else scaled_ready, 1)

            def take_columns(phase):
                n = len(phases[phase])
                dve.wait_ge(ada_done, ada_no[phases[phase][-1]] + 1)
                v.tensor_copy(ada_rows[:, :], banks[6][:, :]).then_inc(ada_kept, 1)
                dve.wait_ge(mod_done, phase + 1)
                got = banks[7][:, 0:4 * n].rearrange("p (j m) -> p m j", j=4)
                at = 0
                for layer in range(2):
                    mine = [i for kind, i in phases[phase] if kind == f"ada{layer}"]
                    if mine:
                        a, b = 4 * mine[0], 4 * mine[-1] + 4
                        bias = (colA[:, 8:56], colB[:, 0:48])[layer]
                        link(v.tensor_tensor(mod[:, layer, a:b].rearrange("p (m j) -> p m j", j=4),
                                             got[:, at:at + len(mine), :],
                                             bias[:, a:b].rearrange("p (m j) -> p m j", j=4), ALU.add))
                        at += len(mine)

            def set_gain(slot, layer, scale_at, g):
                link(v.scalar_tensor_tensor(out=gs[:, slot, :], in0=mod[:, layer, scale_at:scale_at + KD], scalar=1.0,
                                            in1=g, op0=ALU.add, op1=ALU.mult))

            def mod_signal():
                v.memset(most[:, :], 0.0).then_inc(mod_ready, 1)

            dve.wait_ge(x_ready, 4)
            take_columns(0)
            set_gain(0, 0, 8, colA[:, 56:64])
            mod_signal()
            norm(1, gs[:, 0, :], mod[:, 0, 0:8], bank=5)

            dve.wait_ge(small_loaded, 160)
            link(v.tensor_copy(ang, pos_i))
            link(v.tensor_scalar(ang, ang, freq[:, 0:1], None, ALU.mult))
            link(v.tensor_scalar(turns, ang, float(1.0 / (2 * np.pi)), None, ALU.mult))
            link(v.tensor_scalar(turns, turns, 1.5 * 2.0 ** 23, None, ALU.add))
            link(v.tensor_scalar(turns, turns, 1.5 * 2.0 ** 23, None, ALU.subtract))
            c1 = 6.28125
            c2 = float(np.floor((2 * np.pi - c1) * 2.0 ** 21) / 2.0 ** 21)
            c3 = float(2 * np.pi - c1 - c2)
            for part in (c1, c2, c3):
                link(v.scalar_tensor_tensor(out=ang, in0=turns, scalar=-part, in1=ang, op0=ALU.mult, op1=ALU.add))
            pi = float(np.nextafter(np.float32(np.pi), np.float32(0)))
            v.tensor_scalar(ang, ang, pi, -pi, ALU.min, ALU.max).then_inc(trig_in, 1)
            dve.wait_ge(trig_in, 1)
            link(v.scalar_tensor_tensor(out=turns, in0=ang, scalar=-1.0, in1=ang, op0=ALU.mult, op1=ALU.max))
            v.tensor_scalar(turns, turns, -1.0, float(np.pi / 2), ALU.mult, ALU.add).then_inc(trig_in, 1)

            for j in range(TWO0):
                if owner[j] == "v":
                    dst, n, scale = qkv_place(j)
                    dve.wait_ge(tile_done, j + 1)
                    v.tensor_scalar(dst, banks[j % 4][:, 0:n], scale, None, ALU.mult).then_inc(tile_kept["v"], 1)

            def log_a(h):
                dve.wait_ge(sticks_done, h + 1)
                if h >= 2:
                    dve.wait_ge(a_ready, h - 1)
                v.scalar_tensor_tensor(out=sc[4][h % 2][:, :], in0=banks[h % 4][:, 0:384], scalar=0.0,
                                       in1=bias_strict[:, :], op0=ALU.min, op1=ALU.add).then_inc(log_ready, 1)

            def softplus(h):
                dve.wait_ge(soft_ready, h + 1)
                if h >= 2:
                    dve.wait_ge(sticks_done, h - 1)
                v.scalar_tensor_tensor(out=sc[2][h % 2][:, :], in0=banks[h % 4][:, 0:384], scalar=0.0,
                                       in1=sc[1][h % 2][:, :], op0=ALU.max, op1=ALU.add).then_inc(sp_ready, 1)

            def keep_o(layer, p):
                dve.wait_ge(o_done, 16 * layer + 2 * p + 2)
                v.tensor_copy(OT[:, p, :], banks[4 + p % 2][:, 0:T]).then_inc(o_ready, 1)

            dve.wait_ge(consts, 5)
            take_columns(1)
            set_gain(1, 0, 32, colA[:, 64:72])
            set_gain(2, 1, 8, colB[:, 48:56])
            mod_signal()
            dve.wait_ge(trig_ready, 2)
            for h in range(HEADS + 5):
                if 2 <= h < HEADS + 2:
                    log_a(h - 2)
                if 1 <= h <= HEADS:
                    softplus(h - 1)
                if h >= 5 and h % 2 == 1:
                    keep_o(0, (h - 5) // 2)
            def residual_tiles(first, layer, ready):
                for d in range(KD):
                    j = first + d
                    dve.wait_ge(tile_done, j + 1)
                    v.scalar_tensor_tensor(out=xT[:, d, :], in0=banks[j % 4][:, 0:T],
                                           scalar=mod[:, layer, 16 + d:17 + d], in1=xT[:, d, :],
                                           op0=ALU.mult, op1=ALU.add).then_inc(tile_kept["v"], 1)
                dve.wait_ge(tile_kept["v"], nth[first + KD - 1])

            residual_tiles(TWO0, 0, 8)

            def field(n, *dims):
                at = sc[3 + n // 12][0][:, (n % 12) * 32:(n % 12) * 32 + 32].rearrange("p (t n) -> p t n", t=TT)
                return at[:, :, 0:dims[0]] if dims else at[:, :, 0]

            def spread(a, n):
                return a.unsqueeze(2).broadcast_to([P, TT, n])

            def first_of(hot, vals, top):
                eq, best = field(0, 4), field(1)
                link(v.tensor_tensor(eq, vals, spread(top, 4), ALU.is_equal))
                link(v.tensor_tensor(eq, eq, prio[:, :].unsqueeze(1).broadcast_to([P, TT, 4]), ALU.mult))
                link(v.tensor_reduce(best, eq, AX.X, ALU.max))
                link(v.tensor_tensor(hot, eq, spread(best, 4), ALU.is_equal))

            def by_group(a):
                return a.rearrange("p t (g j) -> p t g j", g=NG)

            def moe(layer):
                norm((2, 6)[layer], gs[:, 1 + 2 * layer, :], mod[:, layer, 24:32])
                dve.wait_ge(logit_done, layer + 1)
                link(v.tensor_tensor(lg[:, :, :],
                                     banks[7][:, 0:64].rearrange("p (t n) -> p t n", t=2)[:, :, 0:NG + NE],
                                     br[:, layer, :].unsqueeze(1).broadcast_to([P, TT, NG + NE]), ALU.add))
                g, e = lg[:, :, 0:NG], lg[:, :, NG:]
                gmax, group, picked, ein = field(2), field(3, 4), field(4, 16), field(5, 4)
                m1, m2, hot1, hot2, rest, both = field(6), field(7), field(8, 4), field(9, 4), field(10, 4), field(11, 4)
                gdiff, gexp, mdiff, mexp = field(12, 4), field(13, 4), field(14), field(15)
                gsum, w1, w2 = field(16), field(17), field(18)
                link(v.tensor_reduce(gmax, g, AX.X, ALU.max))
                v.tensor_tensor(gdiff, g, spread(gmax, NG), ALU.subtract).then_inc(route_in, 1)
                first_of(group, g, gmax)
                link(v.tensor_tensor(by_group(picked), by_group(e),
                                     group.unsqueeze(3).broadcast_to([P, TT, NG, EPG]), ALU.mult))
                link(v.tensor_reduce(ein, picked.rearrange("p t (g j) -> p t j g", g=NG), AX.X, ALU.add))
                link(v.tensor_reduce(m1, ein, AX.X, ALU.max))
                first_of(hot1, ein, m1)
                link(v.scalar_tensor_tensor(out=rest, in0=hot1, scalar=NEG, in1=ein, op0=ALU.mult, op1=ALU.add))
                link(v.tensor_reduce(m2, rest, AX.X, ALU.max))
                first_of(hot2, rest, m2)
                v.tensor_tensor(mdiff, m2, m1, ALU.subtract).then_inc(route_in, 1)
                link(v.tensor_tensor(both, hot1, hot2, ALU.add))
                v.tensor_tensor(by_group(mask[:, :, :]), both.unsqueeze(2).broadcast_to([P, TT, NG, EPG]),
                                group.unsqueeze(3).broadcast_to([P, TT, NG, EPG]), ALU.mult).then_inc(mask_ready, 1)
                for t in range(TT):
                    for half in range(2):
                        n = 2 * t + half
                        dve.wait_ge(hn_high, 4 * layer + n + 1)
                        v.tensor_tensor(tok[1][:, t, 512 * half:512 * half + 512], banks[n][:, :],
                                        tok[0][:, t, 512 * half:512 * half + 512].bitcast(F32),
                                        ALU.subtract).then_inc(hn_ready, 1)
                dve.wait_ge(rank_done, layer + 1)
                link(v.tensor_reduce(most[:, :], banks[6][:, 32:32 + NE], AX.X, ALU.max))
                v.tensor_copy(most_i[:, :], most[:, :]).then_inc(most_ready, 1)
                dve.wait_ge(route_out, 2 * layer + 2)
                link(v.tensor_reduce(gsum, gexp, AX.X, ALU.add))
                link(v.scalar_tensor_tensor(out=w1, in0=mexp, scalar=1.0, in1=gsum, op0=ALU.add, op1=ALU.mult))
                link(v.reciprocal(w1, w1))
                link(v.tensor_tensor(w2, w1, mexp, ALU.mult))
                link(v.tensor_tensor(hot1, hot1, spread(w1, 4), ALU.mult))
                link(v.tensor_tensor(hot2, hot2, spread(w2, 4), ALU.mult))
                link(v.tensor_tensor(hot1, hot1, hot2, ALU.add))
                v.tensor_tensor(by_group(gates[:, :, :]), hot1.unsqueeze(2).broadcast_to([P, TT, NG, EPG]),
                                group.unsqueeze(3).broadcast_to([P, TT, NG, EPG]), ALU.mult).then_inc(gates_ready, 1)
                dve.wait_ge(gates_ready, layer + 1)
                dve.wait_ge(most_ready, layer + 1)
                few = dve.value_load(most_i[0:1, 0:1], min_val=0, max_val=T)
                with dve.If(few > FEW):
                    dense_experts(layer)
                with dve.Else():
                    sparse_experts(layer)
                dve.wait_ge(acc_done, layer + 1)
                for d in range(KD):
                    v.scalar_tensor_tensor(out=xT[:, d, :], in0=banks[d // 2][:, (d % 2) * T:(d % 2 + 1) * T],
                                           scalar=mod[:, layer, 40 + d:41 + d], in1=xT[:, d, :],
                                           op0=ALU.mult, op1=ALU.add).then_inc(x_ready, 1)
                dve.wait_ge(x_ready, 4 + 8 * (layer + 1))

            def dense_experts(layer):
                q = per_layer[layer]
                for n in range(2):
                    v.memset(most[64 * n:64 * n + 64, :], 0.0).then_inc(q.gu_read, 1)
                with dve.Fori(0, NE // 2) as i:
                    for b in range(2):
                        v.tensor_tensor(diag, ident[:, :].unsqueeze(1).broadcast_to([P, TT, P]),
                                        gates[:, :, bass.ds(i * 2 + b, 1)].broadcast_to([P, TT, P]),
                                        ALU.mult).then_inc(q.diag_ready, 1)
                        dve.wait_ge(q.gate_done, i * 2 + (b + 1))
                        v.tensor_copy(gate_row[b], banks[6][:, 0:T]).then_inc(q.gate_ready, 1)
                        dve.wait_ge(down_done, i * 2 + (17 * layer + b + 1))
                        for f in range(4):
                            dve.wait_ge(q.silu_ready, i * 8 + (4 * b + f + 1))
                            v.tensor_tensor(hg[b][:, f, :], silu[f % 2], banks[4 + f % 2][:, T:2 * T],
                                            ALU.mult).then_inc(q.gu_read, 1)

            def sparse_experts(layer):
                q = per_layer[layer]
                rank = field(19, 16)
                v.scalar_tensor_tensor(out=rank, in0=banks[6][:, 0:32].rearrange("p (t n) -> p t n", t=TT),
                                       scalar=1.0, in1=mask[:, :, :], op0=ALU.add,
                                       op1=ALU.mult).then_inc(q.rank_ready, 1)
                dve.wait_ge(q.rank_ready, 1)
                for t in range(TT):
                    ins = v.tensor_tensor(pick[:, t, :].rearrange("p (e s) -> p e s", e=NE),
                                          rank[:, t, :].unsqueeze(2).broadcast_to([P, NE, CAP]),
                                          slot_no[:, :].unsqueeze(1).broadcast_to([P, NE, CAP]), ALU.is_equal)
                ins.then_inc(q.pick_ready, 1)
                dve.wait_ge(q.slot_gate_done, 1)
                for b in range(2):
                    r = slice(CAP * b, CAP * (b + 1))
                    ins = v.tensor_copy(slot_gate[r, :], banks[7][r, b:NE:2])
                ins.then_inc(q.slot_gate_ready, 1)
                for b in range(0, 4, 2):
                    dve.wait_ge(q.pick_turned, b + 1)
                    v.tensor_copy(pick_T[:, 2 * b:2 * b + 2, :], banks[b][:, :].rearrange("p (a t) -> p a t", a=2)) \
                        .then_inc(q.pick_T_ready, 1)
                def keep_gathered(i):
                    dve.wait_ge(q.gathered, i * 2 + 1)
                    v.tensor_copy(XG[:, 0:4, :], banks[5][:, :].rearrange("p (k s) -> p k s", k=4)) \
                        .then_inc(q.xg_kept["v"], 1)

                def pair(i, last=False):
                    dve.wait_ge(q.act_ready, i + 1)
                    v.tensor_tensor(h_pair, silu_pair, banks[5][:, :], ALU.mult).then_inc(q.h_ready, 1)
                    dve.wait_ge(q.h_turned, i + 1)
                    v.tensor_copy(hT_pair, banks[4][:, :].rearrange("p (f s) -> p f s", f=4)).then_inc(q.hT_ready, 1)
                    if not last:
                        keep_gathered(i + 1)
                    for half in range(2):
                        dve.wait_ge(q.y_high, i * 2 + (half + 1))
                        ins = v.scalar_tensor_tensor(
                            out=Y[1][:, 512 * half:512 * half + 512], in0=banks[6 + half][:, :],
                            scalar=slot_gate[:, bass.ds(i, 1)],
                            in1=Y[0][:, 512 * half:512 * half + 512].bitcast(F32), op0=ALU.mult, op1=ALU.subtract)
                    ins.then_inc(q.y_done, 1)

                keep_gathered(0)
                with dve.Fori(0, NE // 2 - 1) as i:
                    pair(i)
                pair(NE // 2 - 1, last=True)

            moe(0)
            norm(3, gs[:, 2, :], mod[:, 1, 0:8])

            def keep(lo, hi):
                for j in range(lo, hi):
                    if owner[j] == "v":
                        dst, n = latent_place(j)
                        dve.wait_ge(tile_done, j + 1)
                        v.tensor_copy(dst, banks[j % 4][:, 0:n]).then_inc(tile_kept["v"], 1)

            keep(TLAT, TUP)
            mean_square(4, QR)
            mean_square(5, KVR, T)
            dve.wait_ge(std_ready, 5)
            link(v.reciprocal(rstd[:, :, :], rstd[:, :, :]))
            wait_tiles(dve, TUP - 1)
            for k in range(5):
                v.scalar_tensor_tensor(out=hT[:, k, :], in0=lat[:, k, :], scalar=colB[:, 72 + k:73 + k],
                                       in1=rstd[:, 0 if k < 3 else 1, :], op0=ALU.mult,
                                       op1=ALU.mult).then_inc(h_ready, 1)
            keep(TUP, TROT)
            for g in range(5):
                j = TROT + g
                dve.wait_ge(tile_done, j + 1)
                dst = q_rope[g] if g < 4 else k_rope[:, :]
                v.tensor_tensor(sin_part, banks[j % 4][:, 0:T], sinT[:, :], ALU.mult).then_inc(tile_kept["v"], 1)
                dve.wait_ge(tile_kept["v"], nth[j])
                link(v.tensor_tensor(dst, raw_rope[g], cosT[:, :], ALU.mult))
                v.tensor_tensor(dst, dst, sin_part, ALU.add).then_inc(rope_ready, 1)
                dve.wait_ge(rope_ready, g + 1)
            keep(TKV, TWO1)
            spans = [(0, P), (P, 384)]

            def mask_max(h):
                dve.wait_ge(s_done, h + 1)
                if h >= 2:
                    dve.wait_ge(p_ready, 2 * (h - 1))
                for m, (a, b) in enumerate(spans):
                    v.tensor_tensor_reduce(out=sc[0][h % 2][:, a:b], in0=banks[h % 2][:, a:b],
                                           in1=bias_causal[:, a:b], scale=float(QK ** -0.5), scalar=NEG, op0=ALU.add,
                                           op1=ALU.max, accum_out=st[h % 2][:, m:m + 1]).then_inc(masked_ready, 1)
                dve.wait_ge(masked_ready, 2 * (h + 1))
                v.tensor_scalar(st[h % 2][:, 2:4], st[h % 2][:, 0:2], -1.0, None, ALU.mult).then_inc(neg_ready, 1)

            def normalise(h):
                dve.wait_ge(p_ready, 2 * (h + 1))
                link(v.reciprocal(st[h % 2][:, 6:8], st[h % 2][:, 4:6]))
                for m, (a, b) in enumerate(spans):
                    ins = v.tensor_scalar(sc[1][h % 2][:, a:b], sc[1][h % 2][:, a:b], st[h % 2][:, 6 + m:7 + m], None,
                                          ALU.mult)
                ins.then_inc(pn_ready, 1)

            for h in range(HEADS + 5):
                if h < HEADS:
                    mask_max(h)
                if 1 <= h <= HEADS:
                    normalise(h - 1)
                if h >= 5 and h % 2 == 1:
                    keep_o(1, (h - 5) // 2)
            take_columns(2)
            set_gain(3, 1, 32, colB[:, 56:64])
            mod_signal()
            residual_tiles(TWO1, 1, 16)
            moe(1)
            norm(7, colB[:, 64:72], None)
            for b in range(4):
                dve.wait_ge(y_turned, b + 1)
                t, half = b // 2, b % 2
                v.tensor_copy(V[:, t, 512 * half:512 * half + 512], banks[b][:, :]).then_inc(y_ready, 1)

        @block.scalar
        def _(act):
            s = nc.scalar
            links = [0]

            def link(ins):
                links[0] += 1
                ins.then_inc(act_chain, 1)
                act.wait_ge(act_chain, links[0])

            rows = [(rowsA, 0, c, 8), (rowsA, 8, ada_b[0:1], 48), (rowsA, 56, norm_mix_g[0:1], 8),
                    (rowsA, 64, norm_ffn_g[0:1], 8), (rowsB, 0, ada_b[1:2], 48), (rowsB, 48, norm_mix_g[1:2], 8),
                    (rowsB, 56, norm_ffn_g[1:2], 8), (rowsB, 72, mla_g_q, 3), (rowsB, 75, mla_g_kv, 2)]
            for tile_, at, src, r in rows:
                act.dma_start(tile_[at:at + r, :], src.rearrange("o (r p) -> (o r) p", p=P)).then_inc(rows_loaded, 16)
            act.dma_start(rowsB[64:72, :], final_g.rearrange("(r p) -> r p", p=P)).then_inc(rows_loaded, 16)
            act.preload_act_table_set("silu_and_others")
            act.wait_ge(cols_ready, 1)
            act.wait_ge(consts, 3)
            s.activation(c_pad[:, :, 31], colA[:, 0:8], ACT.Silu).then_inc(c_ready, 1)

            def squares(ready, counts):
                for k in range(KD):
                    act.wait_ge(ready, counts[k])
                    s.activation(sq[:, k, :], xT[:, k, :], ACT.Square).then_inc(sq_ready, 1)

            def add_shift(norm, shift, moded, after=None):
                act.wait_ge(mod_ready, moded)
                if after:
                    act.preload_act_table_set(after)
                for k in range(KD):
                    act.wait_ge(scaled_ready, KD * norm + k + 1)
                    s.activation(hT[:, k, :], hT[:, k, :], ACT.Identity, bias=shift[:, k:k + 1]).then_inc(h_ready, 1)

            def root(number, at=0):
                act.wait_ge(ms_ready, number)
                s.activation(rstd[:, at // T, :], rstd[:, at // T, :], ACT.Sqrt).then_inc(std_ready, 1)

            act.wait_ge(x_turned, 4)
            squares(x_ready, [k // 2 + 1 for k in range(KD)])
            act.preload_act_table_set("sqrt_and_others")
            root(1)
            add_shift(0, mod[:, 0, 0:8], 1, "silu_and_others")
            act.wait_ge(trig_in, 2)
            s.activation(sinT[:, :], ang, ACT.Sin).then_inc(trig_ready, 1)
            s.activation(cosT[:, :], turns, ACT.Sin).then_inc(trig_ready, 1)
            for j in range(TWO0):
                if owner[j] == "a":
                    dst, n, scale = qkv_place(j)
                    act.wait_ge(tile_done, j + 1)
                    s.activation(dst, banks[j % 4][:, 0:n], ACT.Copy, scale=scale).then_inc(tile_kept["a"], 1)

            act.preload_act_table_set("natural_log_exp_and_others")
            act.wait_ge(consts, 5)
            for h in range(HEADS + 2):
                if h < HEADS:
                    e = sc[1][h % 2][:, :]
                    act.wait_ge(z_done, h + 1)
                    if h >= 2:
                        act.wait_ge(sp_ready, h - 1)
                    link(s.activation(e, banks[h % 4][:, 0:384], ACT.Abs))
                    link(s.activation(e, e, ACT.Exp, scale=-1.0))
                    s.activation(e, e, ACT.Ln, bias=1.0).then_inc(soft_ready, 1)
                if h >= 2:
                    g = h - 2
                    act.wait_ge(log_ready, g + 1)
                    if g >= 2:
                        act.wait_ge(o_done, g - 1)
                    s.activation(sc[3][g % 2][:, :], sc[4][g % 2][:, :], ACT.Exp).then_inc(a_ready, 1)

            def moe(layer):
                first_tile = (TWO0, TWO1)[layer]
                act.preload_act_table_set("sqrt_and_others")
                squares(tile_kept["v"], [nth[first_tile + k] for k in range(KD)])
                root((2, 6)[layer])
                add_shift((1, 3)[layer], mod[:, layer, 24:32], (2, 3)[layer], "exp_and_others")
                act.wait_ge(route_in, 2 * layer + 1)
                s.activation(sc4_field(1), sc4_field(0), ACT.Exp).then_inc(route_out, 1)
                for n in range(4):
                    act.wait_ge(hn_turned, 4 * layer + n + 1)
                    s.activation(tok[0][:, n // 2, 512 * (n % 2):512 * (n % 2) + 512], banks[n][:, :],
                                 ACT.Copy).then_inc(hn_high, 1)
                act.wait_ge(route_in, 2 * layer + 2)
                s.activation(sc4_field(3)[:, :, 0], sc4_field(2)[:, :, 0], ACT.Exp).then_inc(route_out, 1)
                act.wait_ge(most_ready, layer + 1)
                few = act.value_load(most_i[0:1, 0:1], min_val=0, max_val=T)
                act.preload_act_table_set("silu_and_others")
                with act.If(few > FEW):
                    dense_experts(layer)
                with act.Else():
                    sparse_experts(layer)

            def sc4_field(n):
                at = sc[4][0][:, n * 32:n * 32 + 32].rearrange("p (t n) -> p t n", t=TT)
                return at[:, :, 0:4]

            def dense_experts(layer):
                q = per_layer[layer]
                with act.Fori(0, NE // 2) as i:
                    for b in range(2):
                        for f in range(4):
                            act.wait_ge(gu_done, i * 8 + (64 * layer + 4 * b + f + 1))
                            act.wait_ge(q.gu_read, i * 8 + (4 * b + f + 1))
                            s.activation(silu[f % 2], banks[4 + f % 2][:, 0:T], ACT.Silu).then_inc(q.silu_ready, 1)

            def sparse_experts(layer):
                q = per_layer[layer]
                for b in range(1, 4, 2):
                    act.wait_ge(q.pick_turned, b + 1)
                    s.activation(pick_T[:, 2 * b:2 * b + 2, :], banks[b][:, :].rearrange("p (a t) -> p a t", a=2),
                                 ACT.Copy).then_inc(q.pick_T_ready, 1)

                def keep_gathered(i):
                    act.wait_ge(q.gathered, i * 2 + 2)
                    s.activation(XG[:, 4:8, :], banks[4][:, :].rearrange("p (k s) -> p k s", k=4),
                                 ACT.Copy).then_inc(q.xg_kept["a"], 1)

                def pair(i, first=False, last=False):
                    act.wait_ge(gu_done, i * 8 + (64 * layer + 8))
                    s.activation(silu_pair, banks[4][:, :], ACT.Silu).then_inc(q.act_ready, 1)
                    if not last:
                        keep_gathered(i + 1)
                    act.wait_ge(down_done, i * 2 + (17 * layer + 3))
                    if not first:
                        act.wait_ge(q.scattered, i)
                    for half in range(2):
                        s.activation(Y[0][:, 512 * half:512 * half + 512], banks[6 + half][:, :], ACT.Copy,
                                     scale=slot_gate[:, bass.ds(i, 1)]).then_inc(q.y_high, 1)

                keep_gathered(0)
                pair(0, first=True)
                with act.Fori(1, NE // 2 - 1) as i:
                    pair(i)
                pair(NE // 2 - 1, last=True)

            moe(0)
            act.preload_act_table_set("sqrt_and_others")
            squares(x_ready, [4 + k + 1 for k in range(KD)])
            root(3)
            add_shift(2, mod[:, 1, 0:8], 2)

            def keep(lo, hi):
                for j in range(lo, hi):
                    if owner[j] == "a":
                        dst, n = latent_place(j)
                        act.wait_ge(tile_done, j + 1)
                        s.activation(dst, banks[j % 4][:, 0:n], ACT.Copy).then_inc(tile_kept["a"], 1)

            keep(TLAT, TUP)
            wait_tiles(act, TUP - 1)
            for k in range(5):
                s.activation(sq[:, k, :], lat[:, k, :], ACT.Square).then_inc(sq_ready, 1)
            root(4)
            root(5, T)
            act.preload_act_table_set("exp_and_others")
            keep(TUP, TROT)
            keep(TKV, TWO1)
            for h in range(HEADS + 2):
                if h < HEADS:
                    act.wait_ge(neg_ready, h + 1)
                    if h >= 2:
                        act.wait_ge(pt_done, h - 1)
                    for m, (a, b) in enumerate([(0, P), (P, 384)]):
                        s.activation(sc[1][h % 2][:, a:b], sc[0][h % 2][:, a:b], ACT.Exp,
                                     bias=st[h % 2][:, 2 + m:3 + m],
                                     accum_out=st[h % 2][:, 4 + m:5 + m]).then_inc(p_ready, 1)
                if h >= 2:
                    g = h - 2
                    act.wait_ge(pt_done, g + 1)
                    if g >= 2:
                        act.wait_ge(o_done, HEADS + g - 1)
                    s.activation(sc[3][g % 2][:, :], banks[2 + g % 2][:, 0:384], ACT.Copy).then_inc(aT_ready, 1)
            moe(1)
            act.preload_act_table_set("sqrt_and_others")
            squares(x_ready, [12 + k + 1 for k in range(KD)])
            root(7)


_INS = ["x", "c", "positions", "norm_mix_g", "norm_ffn_g", "ada_w", "ada_b", "sb_w_qkv", "sb_w_o",
        "mla_w_in", "mla_g_q", "mla_g_kv", "mla_w_q_up", "mla_w_kv_up", "mla_w_o",
        "moe_w_group", "moe_b_group", "moe_w_router", "moe_b_router", "moe_w_gate_up", "moe_w_down", "final_g"]


def kernel(**inputs):
    import numpy as _np
    import concourse.bacc as _bacc
    from concourse import mybir as _mybir
    from concourse.bass_utils import run_bass_kernel_spmd as _run

    nc = _bacc.Bacc("TRN2", target_bir_lowering=False, num_devices=1)
    arrays, args = {}, []
    for name in _INS:
        arrays[f"in_{name}"] = _np.ascontiguousarray(inputs[name])
    half = _np.arange(0, ROPE, 2, dtype=_np.float32) / _np.float32(ROPE)
    arrays["in_inv_freq"] = _np.tile(_np.float32(THETA) ** (-half), 2 * P // ROPE).astype(_np.float32)
    for name, a in arrays.items():
        args.append(nc.dram_tensor(name, a.shape, _mybir.dt.from_np(a.dtype), kind="ExternalInput").ap())
    args.append(nc.dram_tensor("out_0", (1, T, D), _mybir.dt.float32, kind="ExternalOutput").ap())
    build(nc, *args)
    r = _run(nc, [arrays], core_ids=[0])
    return r.results[0]["out_0"]
```

```python
from contextlib import ExitStack

import concourse.bass as bass
import numpy as np
from concourse import mybir

F32 = mybir.dt.float32
F32R = mybir.dt.float32r
I32 = mybir.dt.int32
ALU = mybir.AluOpType
ACT = mybir.ActivationFunctionType
AX = mybir.AxisListType

P = 128
D = 1024
T = 256
KD = D // P
TT = T // P
HEADS = 16
DH = 64
QR, KVR, ROPE = 384, 256, 32
QK = DH + ROPE
NE, NG, EPG = 16, 4, 4
FF = 512
MOD = 6 * D // P
EPS = 1e-6
THETA = 10000.0
NEG = -1.0e30
CAP = 64
FEW = CAP
SLOTS = 8
SLOT = 4096
TQKV = 0
TWO0 = 20
TLAT = TWO0 + 8
TUP = TLAT + 6
TROT = TUP + 12
TKV = TROT + 5
TWO1 = TKV + 12
TEND = TWO1 + 8


def build(nc, x, c, positions, norm_mix_g, norm_ffn_g, ada_w, ada_b, sb_w_qkv, sb_w_o,
          mla_w_in, mla_g_q, mla_g_kv, mla_w_q_up, mla_w_kv_up, mla_w_o,
          moe_w_group, moe_b_group, moe_w_router, moe_b_router, moe_w_gate_up, moe_w_down,
          final_g, inv_freq, out):
    owner = []
    for j in range(TEND):
        alone = TWO0 <= j < TLAT or TUP + 8 <= j < TKV or j >= TWO1
        owner.append("v" if alone or j % 2 == 0 else "a")
    nth = [owner[:j + 1].count(owner[j]) for j in range(TEND)]

    stream = []
    uses = [0] * SLOTS
    where = {}

    def chunk(name, slot, src, k, n):
        uses[slot] += 1
        where[name] = (slot, uses[slot], k, n)
        stream.append((name, slot, src, k, n))

    def cols(w, a, b):
        return w[:, a:b].rearrange("(k p) n -> p k n", p=P)

    qkv_order = [("k", 0), ("q", 0), ("v", 0), ("k", 1), ("q", 1), ("v", 1)]
    phases = [[("ada0", i) for i in range(4)],
              [("ada0", i) for i in range(4, 12)] + [("ada1", i) for i in range(4)],
              [("ada1", i) for i in range(4, 12)]]
    ada_no = {a: n for n, a in enumerate(sum(phases, []))}

    def ada_chunk(a, slot):
        chunk(a, slot, cols(ada_w[int(a[0][3])], 512 * a[1], 512 * a[1] + 512), KD, 512)

    parts = [(0, 0), (1, 0), (0, 1), (1, 1), (0, 2), (1, 2)]

    def first_expert(n):
        stream.append((("expert", n), 3 * parts[n][0] + parts[n][1], None, 0, 0))

    for n, a in enumerate(phases[0]):
        ada_chunk(a, n)
    slot_of = {("k", 0): 4, ("q", 0): 5, ("v", 0): 0, ("k", 1): 3, ("q", 1): 1, ("v", 1): 2}
    slot_of.update({a: (6, 7, 4, 5)[n % 4] for n, a in enumerate(phases[1])})
    late = phases[1]
    for name in ([("k", 0), ("q", 0), late[0], ("v", 0), late[1], ("k", 1), ("q", 1), ("v", 1)] + late[2:6] +
                 [0, 1, late[6], 2] + late[7:12] + [4]):
        if isinstance(name, int):
            first_expert(name)
        elif name[0] in ("q", "k", "v"):
            at = D * "qkv".index(name[0]) + 512 * name[1]
            chunk(name, slot_of[name], cols(sb_w_qkv[0], at, at + 512), KD, 512)
        else:
            ada_chunk(name, slot_of[name])
    for i in range(2):
        chunk(("wo0", i), 6 + i, cols(sb_w_o[0], 512 * i, 512 * i + 512), KD, 512)
    for n in (3, 5):
        first_expert(n)
    first = [len(stream), 0]
    base = [list(uses), 0]
    for s in range(6):
        uses[s] += NE // 2 - (s == 3)
    for i in range(2):
        chunk(("win", i), i, mla_w_in[0][512 * i:512 * i + 512].rearrange("(k p) n -> p k n", p=P), 4,
              QR + KVR + ROPE)
    chunk(("kvup", 0), 2, cols(mla_w_kv_up[0], 0, 2048), KVR // P, 2048)
    for i in range(2):
        chunk(("qup", i), 6 + i, cols(mla_w_q_up[0], 768 * i, 768 * i + 768), QR // P, 768)
    for n, a in enumerate(phases[2]):
        ada_chunk(a, 6 + n % 2)
    for i in range(2):
        chunk(("wo1", i), 6 + i, cols(mla_w_o[0], 512 * i, 512 * i + 512), KD, 512)
    for n in range(6):
        first_expert(n)
    first[1] = len(stream)
    base[1] = list(uses)

    with ExitStack() as ctx:
        def sb(name, shape, dt=F32):
            return ctx.enter_context(nc.sbuf_tensor(name, shape, dt))

        def sem(name):
            return ctx.enter_context(nc.semaphore(name))

        end = nc.sbuf_usable_end // 64 * 64
        side = [end - 2 * 4 * SLOT, end - 4 * SLOT]

        def at(name, shape, dt, offset):
            return nc.alloc_sbuf_tensor_at(name, shape, dt, offset=offset)

        ring = [sb(f"ring{s}", [P, SLOT]) for s in range(SLOTS - 2)]
        ring += [at(f"ring{6 + n}", [P, SLOT], F32, side[n]) for n in range(2)]
        xT = sb("xT", [P, KD, T])
        hT = sb("hT", [P, KD, T])
        big_at = nc.sbuf_base
        big = sb("big", [P, 4 * 8 * T])
        assert nc.sbuf_base == big_at + 4 * 4 * 8 * T
        QT, KT, OT = (big[:, n * 8 * T:(n + 1) * 8 * T].rearrange("p (k t) -> p k t", k=8) for n in (0, 1, 3))
        V = big[:, 2 * 8 * T:3 * 8 * T].rearrange("p (t n) -> p t n", t=TT)
        ident = sb("ident", [P, P])
        ones = sb("ones", [P, P])
        neg_ones = sb("neg_ones", [P, P])
        neg_tri = sb("neg_tri", [P, P])
        strict = sb("strict", [P, P])
        bias_strict = sb("bias_strict", [P, 384])
        bias_causal = sb("bias_causal", [P, 384])
        rot = sb("rot", [P, P])
        prio = sb("prio", [P, 4])
        colA = sb("colA", [P, KD + 2 * MOD])
        colB = sb("colB", [P, 5 * KD + 5])
        c_pad = sb("c_pad", [P, KD, 64])
        row_sel = sb("row_sel", [P, 12])
        mod = sb("mod", [P, 2, MOD])
        gs = sb("gs", [P, 4, KD])
        freq = sb("freq", [P, 1])
        cosT = sb("cosT", [P, T])
        sinT = sb("sinT", [P, T])
        rstd = sb("rstd", [P, 2, T])
        scratch = sb("scratch", [P, 10 * 384])
        sc = [[scratch[:, (2 * i + b) * 384:(2 * i + b + 1) * 384] for b in range(2)] for i in range(5)]
        st = [sb(f"st{b}", [P, 8]) for b in range(2)]
        wr = sb("wr", [P, 2, KD, NG + NE])
        br = sb("br", [P, 2, NG + NE])
        lg = sb("lg", [P, TT, NG + NE])
        mask = sb("mask", [P, TT, NE])
        slot_no = sb("slot_no", [P, CAP])
        most = sb("most", [P, 1])
        most_i = sb("most_i", [P, 1], I32)
        slot_gate = sb("slot_gate", [P, NE // 2])
        gates = sb("gates", [P, TT, NE])
        k_rope = sb("k_rope", [P, T])

        assert nc.sbuf_base <= side[0]
        zeros = bias_causal[:, P:2 * P]

        rowsA, rowsB = sc[2][0][:, 0:P], sc[2][1][:, 0:P]
        ada_rows = scratch[:, 0:512]
        slot_i = sc[1][0][:, 0:CAP].bitcast(I32)
        x_nat = V
        sq = V.rearrange("p t (k n) -> p (t k) n", n=T)
        lat = OT
        q_rope = [hT[:, 5, :], hT[:, 6, :], hT[:, 7, :], bias_strict[:, 0:T]]
        pos_i = sc[4][0][:, 0:T].bitcast(I32)
        raw_rope = [OT[:, 0, :], OT[:, 1, :], OT[:, 2, :], OT[:, 3, :], OT[:, 5, :]]
        ang, turns, sin_part = sc[3][0][:, 0:T], sc[3][1][:, 0:T], OT[:, 6, :]
        hg = [V[:, b, :].rearrange("p (f t) -> p f t", f=4) for b in range(2)]
        silu = [sc[0][b][:, 0:T] for b in range(2)]
        gate_row = [sc[1][b][:, 0:T] for b in range(2)]
        diag = sc[2][0][:, 0:T].rearrange("p (t n) -> p t n", t=TT)
        spare = big[:, 0:SLOT]
        GU = [[ring[3 * b + i][:, :].rearrange("p (k n) -> p k n", k=4) for i in range(2)] for b in range(2)]
        q_nope_w = ring[3][:, 0:3 * D].rearrange("p (k n) -> p k n", k=3)
        q_rope_w = KT[:, 0:6, :].rearrange("p (k a) t -> p k (a t)", k=3)
        k_nope_w = ring[4][:, 0:2 * D].rearrange("p (k n) -> p k n", k=2)
        k_rope_w = ring[4][:, 2 * D:2 * D + KD * P].rearrange("p (k n) -> p k n", k=KD)
        tok = [at(f"tok{n}", [P, TT, D], F32R, side[0] + n * 4 * TT * D) for n in range(2)]
        Y = [at(f"Y{n}", [P, D], F32R, big_at + 4 * (2 * 8 * T + n * D)) for n in range(2)]
        pick = at("pick", [P, TT, NE * CAP], F32R, side[1])
        pick_T = at("pick_T", [P, NE // 2, T], F32R, side[1] + 4 * TT * NE * CAP)
        XG = scratch[:, 512:512 + KD * 2 * CAP].rearrange("p (k s) -> p k s", k=KD)
        silu_pair, h_pair = OT[:, 0:2, :].rearrange("p a t -> p (a t)"), OT[:, 2:4, :].rearrange("p a t -> p (a t)")
        hT_pair = big[:, 3 * 8 * T + 4 * T:3 * 8 * T + 6 * T].rearrange("p (f s) -> p f s", f=4)
        DN = [ring[3 * b + 2][:, :].rearrange("p (k n) -> p k n", k=4) for b in range(2)]

        banks = [ctx.enter_context(nc.psum_tensor(f"bank{b}", [P, 512], F32)) for b in range(8)]

        consts = sem("consts")
        pool_chain = sem("pool_chain")
        packed = sem("packed")
        dve_chain = sem("dve_chain")
        act_chain = sem("act_chain")
        x_loaded = sem("x_loaded")
        rows_loaded = sem("rows_loaded")
        small_loaded = sem("small_loaded")
        loaded = [sem(f"loaded{s}") for s in range(SLOTS)]
        spare_loaded = sem("spare_loaded")
        half_loaded = {part: [sem(f"half_loaded{part}_{b}") for b in range(2)] for part in (1, 2)}
        x_turned = sem("x_turned")
        x_ready = sem("x_ready")
        rows_turned = sem("rows_turned")
        cols_ready = sem("cols_ready")
        c_ready = sem("c_ready")
        ada_done = sem("ada_done")
        ada_kept = sem("ada_kept")
        mod_done = sem("mod_done")
        mod_ready = sem("mod_ready")
        sq_ready = sem("sq_ready")
        ss_done = sem("ss_done")
        ms_ready = sem("ms_ready")
        std_ready = sem("std_ready")
        scaled_ready = sem("scaled_ready")
        h_ready = sem("h_ready")
        tile_done = sem("tile_done")
        tile_kept = {"v": sem("tile_kept_vector"), "a": sem("tile_kept_scalar")}
        trig_in = sem("trig_in")
        trig_ready = sem("trig_ready")
        z_done = sem("z_done")
        soft_ready = sem("soft_ready")
        sp_ready = sem("sp_ready")
        spm_ready = sem("spm_ready")
        sticks_done = sem("sticks_done")
        log_ready = sem("log_ready")
        a_ready = sem("a_ready")
        o_done = sem("o_done")
        o_ready = sem("o_ready")
        s_done = sem("s_done")
        masked_ready = sem("masked_ready")
        neg_ready = sem("neg_ready")
        p_ready = sem("p_ready")
        pn_ready = sem("pn_ready")
        pt_done = sem("pt_done")
        aT_ready = sem("aT_ready")
        rope_ready = sem("rope_ready")
        logit_done = sem("logit_done")
        route_in = sem("route_in")
        route_out = sem("route_out")
        gu_done = sem("gu_done")
        down_done = sem("down_done")
        hn_turned = sem("hn_turned")
        hn_high = sem("hn_high")
        hn_ready = sem("hn_ready")
        mask_ready = sem("mask_ready")
        rank_done = sem("rank_done")
        most_ready = sem("most_ready")
        gates_ready = sem("gates_ready")
        acc_done = sem("acc_done")
        rank_ready = sem("rank_ready")
        pick_ready = sem("pick_ready")

        class PerLayer:
            def __init__(self, layer):
                def own(name):
                    return sem(f"{name}_{layer}")

                self.diag_ready = own("diag_ready")
                self.gate_done = own("gate_done")
                self.gate_ready = own("gate_ready")
                self.silu_ready = own("silu_ready")
                self.gu_read = own("gu_read")
                self.hg_ready = own("hg_ready")
                self.slot_gate_done = own("slot_gate_done")
                self.slot_gate_ready = own("slot_gate_ready")
                self.pick_turned = own("pick_turned")
                self.pick_T_kept = {"v": own("pick_T_kept_vector"), "a": own("pick_T_kept_scalar")}
                self.gathered = own("gathered")
                self.xg_kept = {"v": own("xg_kept_vector"), "a": own("xg_kept_scalar")}
                self.act_ready = own("act_ready")
                self.h_ready = own("h_ready")
                self.h_turned = own("h_turned")
                self.hT_ready = own("hT_ready")
                self.y_high = own("y_high")
                self.y_done = own("y_done")
                self.scattered = own("scattered")

        per_layer = [PerLayer(layer) for layer in range(2)]
        gained_ready = sem("gained_ready")
        scale_ready = sem("scale_ready")
        y_turned = sem("y_turned")
        y_ready = sem("y_ready")
        stored = sem("stored")

        used_up = {}
        for a, n in ada_no.items():
            used_up[a] = (ada_done, n + 1)
        for half in range(2):
            used_up[("k", half)] = (tile_done, 10 * half + 4)
            used_up[("q", half)] = (tile_done, 10 * half + 8)
            used_up[("v", half)] = (tile_done, 10 * half + 10)
            used_up[("wo0", half)] = (tile_done, TWO0 + 4 * half + 4)
            used_up[("win", half)] = (tile_done, TUP)
            used_up[("qup", half)] = (packed, 5)
            used_up[("wo1", half)] = (tile_done, TWO1 + 4 * half + 4)
        used_up[("kvup", 0)] = (tile_done, TWO1)

        def gate_up_weights(i, b, part):
            if isinstance(i, int) and (i, b, part) == (1, 1, 0):
                return spare.rearrange("p (k n) -> p k n", k=4)
            return GU[b][part]

        def wait_expert(eng, layer, i, b, part):
            slot = 3 * b + part
            before = base[layer][slot]
            if slot == 3:
                if isinstance(i, int) and i == 1:
                    eng.wait_ge(spare_loaded, 16 * (layer + 1))
                    return
                if not isinstance(i, int) or i > 1:
                    before -= 1
            eng.wait_ge(loaded[slot], i * 16 + 16 * (before + 1))

        def weights_of(layer, h):
            return sc[(3, (0, 4)[layer])[h // 2 % 2]][h % 2]

        def weights(name):
            slot, _, k, n = where[name]
            return ring[slot][:, 0:k * n].rearrange("p (k n) -> p k n", k=k)

        def wait_weights(eng, name):
            slot, use, _, _ = where[name]
            eng.wait_ge(loaded[slot], 16 * use)

        def wait_tiles(eng, last):
            for kind in "va":
                count = owner[:last + 1].count(kind)
                if count:
                    eng.wait_ge(tile_kept[kind], count)

        block = ctx.enter_context(nc.Block())

        @block.sync
        def _(sp):
            rows = [(rowsA, 0, c), (rowsA, KD, ada_b), (rowsB, 0, norm_mix_g), (rowsB, 2 * KD, norm_ffn_g),
                    (rowsB, 4 * KD, final_g.rearrange("(o n) -> o n", o=1)), (rowsB, 5 * KD, mla_g_q),
                    (rowsB, 5 * KD + 3, mla_g_kv)]
            for tile_, at, src in rows:
                r = src.shape[0] * src.shape[1] // P
                sp.dma_start(tile_[at:at + r, :], src.rearrange("o (r p) -> (o r) p", p=P)).then_inc(rows_loaded, 16)
            sp.dma_start(x_nat[:, :, :], x[0].rearrange("(t p) d -> p t d", p=P)).then_inc(x_loaded, 16)
            before = [None] * SLOTS

            def load(entry):
                name, slot, src, k, n = entry
                if before[slot] is not None:
                    sp.wait_ge(*before[slot])
                sp.dma_start(ring[slot][:, 0:k * n].rearrange("p (k n) -> p k n", k=k), src).then_inc(loaded[slot], 16)
                before[slot] = used_up[name]

            def load_expert_part(layer, b, part, e):
                slot = 3 * b + part
                if part < 2:
                    src = moe_w_gate_up[layer][e, 512 * part:512 * part + 512, :]
                else:
                    src = moe_w_down[layer][e, :, :]
                sp.dma_start(ring[slot][:, :].rearrange("p (k n) -> p k n", k=4),
                             src.rearrange("e (k p) n -> p (e k) n", p=P)).then_inc(loaded[slot], 16)

            def first_pair(layer, n):
                b, part = parts[n]
                sp.wait_ge(*before[3 * b + part])
                load_expert_part(layer, b, part, bass.ds(b, 1))

            def experts(layer):
                sp.wait_ge(z_done if layer == 0 else s_done, HEADS)
                sp.dma_start(spare.rearrange("p (k n) -> p k n", k=4),
                             moe_w_gate_up[layer][3, 0:512, :].rearrange("(k p) n -> p k n", p=P)).then_inc(spare_loaded, 16)
                for b, part in parts[:1] + parts[2:]:
                    if part < 2:
                        sp.wait_ge(gu_done, 64 * layer + (8 if part else 4))
                    else:
                        sp.wait_ge(down_done, NE * layer + b + 1)
                    load_expert_part(layer, b, part, bass.ds(2 + b, 1))

                def pair_loads(i, chunks):
                    for b, part in chunks:
                        if part < 2:
                            sp.wait_ge(gu_done, i * 8 + (64 * layer - 4 * (b == 0 and part == 0)))
                        else:
                            sp.wait_ge(down_done, i * 2 + (NE * layer + b - 1))
                        load_expert_part(layer, b, part, bass.ds(i * 2 + b, 1))

                with sp.Fori(2, NE // 2 - 1) as i:
                    pair_loads(i, parts)
                pair_loads(NE // 2 - 1, parts[:2])
                for part in (1, 2):
                    for half in range(2):
                        for b in range(2):
                            if half == 0 and part == 1:
                                sp.wait_ge(gu_done, 64 * (layer + 1) - 8)
                            elif half == 0:
                                sp.wait_ge(down_done, NE * (layer + 1) - 3 + b)
                            row = 2 * P * half + (512 if part == 1 else 0)
                            src = (moe_w_gate_up, moe_w_down)[part - 1][layer][NE - 2 + b, row:row + 2 * P, :]
                            place = (GU[b][1], DN[b])[part - 1][:, 2 * half:2 * half + 2, :]
                            done = (half_loaded[part][b], loaded[3 * b + part])[half]
                            sp.dma_start(place, src.rearrange("(k p) n -> p k n", p=P)).then_inc(done, 16)
                for b in range(2):
                    before[3 * b] = before[3 * b + 1] = (gu_done, 64 * (layer + 1))
                    before[3 * b + 2] = (down_done, NE * layer + NE - 1 + b)
                before[3] = (tile_done, TUP + 8)
                before[4] = (tile_done, TKV + 8)
                before[6] = before[7] = (x_ready, 4 + 8 * (layer + 1))

            for layer in range(2):
                for entry in stream[first[layer - 1] if layer else 0:first[layer]]:
                    if entry[0][0] == "expert":
                        first_pair(layer, entry[0][1])
                    else:
                        load(entry)
                experts(layer)
            sp.wait_ge(y_ready, 4)
            sp.dma_start(out[0].rearrange("(t p) d -> p t d", p=P), V[:, :, :]).then_inc(stored, 16)
            sp.wait_ge(stored, 16)

        @block.gpsimd
        def _(pool):
            nc.gpsimd.memset(ident[:, :], 0.0).then_inc(pool_chain, 1)
            pool.wait_ge(pool_chain, 1)
            nc.gpsimd.affine_select(out=ident[:, :], in_=ident[:, :], compare_op=ALU.not_equal, fill=1.0, base=0,
                                    pattern=[[-1, P]], channel_multiplier=1).then_inc(consts, 1)
            nc.gpsimd.memset(ones[:, :], 1.0).then_inc(consts, 1)
            nc.gpsimd.memset(c_pad[:, :, :], 0.0).then_inc(consts, 1)
            nc.gpsimd.memset(row_sel[:, :], 0.0).then_inc(pool_chain, 1)
            for g in range(4):
                pool.wait_ge(pool_chain, 2 + g)
                ins = nc.gpsimd.affine_select(out=row_sel[:, :], in_=row_sel[:, :], compare_op=ALU.not_equal, fill=1.0,
                                              base=-32 * g, pattern=[[-1, 12]], channel_multiplier=1)
                ins.then_inc(pool_chain, 1) if g < 3 else ins.then_inc(consts, 1)
            pool.dma_start(pos_i, positions.broadcast_to([P, T])).then_inc(small_loaded, 16)
            pool.dma_start(freq[:, :], inv_freq.rearrange("(p o) -> p o", o=1)).then_inc(small_loaded, 16)
            for l in range(2):
                pool.dma_start(wr[:, l, :, 0:NG], moe_w_group[l].rearrange("(k p) n -> p k n", p=P)).then_inc(small_loaded, 16)
                pool.dma_start(wr[:, l, :, NG:], moe_w_router[l].rearrange("(k p) n -> p k n", p=P)).then_inc(small_loaded, 16)
                pool.dma_start(br[:, l, 0:NG], moe_b_group[l:l + 1].broadcast_to([P, NG])).then_inc(small_loaded, 16)
                pool.dma_start(br[:, l, NG:], moe_b_router[l:l + 1].broadcast_to([P, NE])).then_inc(small_loaded, 16)
            nc.gpsimd.iota(slot_i[:, :], pattern=[[1, CAP]], base=1, channel_multiplier=0)
            nc.gpsimd.memset(neg_ones[:, :], -1.0)
            for j in range(4):
                nc.gpsimd.memset(prio[:, j:j + 1], float(4 - j))
            nc.gpsimd.memset(neg_tri[:, :], -1.0)
            nc.gpsimd.memset(strict[:, :], 1.0)
            nc.gpsimd.memset(bias_strict[:, :], 0.0)
            nc.gpsimd.memset(bias_causal[:, :], 0.0)
            nc.gpsimd.memset(rot[:, :], 0.0).then_inc(pool_chain, 1)
            pool.wait_ge(pool_chain, 6)
            nc.gpsimd.tensor_copy(slot_no[:, :], slot_i[:, :])
            nc.gpsimd.affine_select(out=neg_tri[:, :], in_=neg_tri[:, :], compare_op=ALU.is_ge, fill=0.0, base=0,
                                    pattern=[[-1, P]], channel_multiplier=1)
            nc.gpsimd.affine_select(out=strict[:, :], in_=strict[:, :], compare_op=ALU.is_gt, fill=0.0, base=0,
                                    pattern=[[1, P]], channel_multiplier=-1)
            for part in (0, 256):
                nc.gpsimd.affine_select(out=bias_strict[:, part:part + P], in_=bias_strict[:, part:part + P],
                                        compare_op=ALU.is_gt, fill=NEG, base=0, pattern=[[1, P]],
                                        channel_multiplier=-1)
                nc.gpsimd.affine_select(out=bias_causal[:, part:part + P], in_=bias_causal[:, part:part + P],
                                        compare_op=ALU.is_ge, fill=NEG, base=0, pattern=[[-1, P]],
                                        channel_multiplier=1)
            halves = rot[:, :].rearrange("p (b h j) -> p b h j", b=4, h=2)
            nc.gpsimd.affine_select(out=halves[:, :, 0, :], in_=halves[:, :, 0, :], compare_op=ALU.not_equal,
                                    fill=-1.0, base=-16, pattern=[[-32, 4], [-1, 16]], channel_multiplier=1)
            nc.gpsimd.affine_select(out=halves[:, :, 1, :], in_=halves[:, :, 1, :], compare_op=ALU.not_equal,
                                    fill=1.0, base=0, pattern=[[-32, 4], [-1, 16]],
                                    channel_multiplier=1).then_inc(consts, 1)
            for h in range(HEADS):
                pool.wait_ge(sp_ready, h + 1)
                for at in (0, 256):
                    ins = nc.gpsimd.tensor_tensor(sc[2][h % 2][:, at:at + P], sc[2][h % 2][:, at:at + P],
                                                  strict[:, :], ALU.mult)
                ins.then_inc(spm_ready, 1)
            def gate_experts(layer):
                q = per_layer[layer]
                pool.wait_ge(most_ready, layer + 1)
                with pool.If(pool.value_load(most_i[0:1, 0:1], min_val=0, max_val=T) > FEW):
                    with pool.Fori(0, NE // 2) as i:
                        for b in range(2):
                            pool.wait_ge(q.gate_ready, i * 2 + (b + 1))
                            for f in range(4):
                                pool.wait_ge(q.gu_read, i * 8 + (4 * b + f + 3))
                                nc.gpsimd.tensor_tensor(hg[b][:, f, :], hg[b][:, f, :], gate_row[b],
                                                        ALU.mult).then_inc(q.hg_ready, 1)

            def pack_mixer1():
                pool.wait_ge(gu_done, 4 * NE)
                pool.wait_ge(down_done, NE)
                for i in range(2):
                    wait_weights(pool, ("win", i))
                    nc.gpsimd.tensor_copy(
                        k_rope_w[:, 4 * i:4 * i + 4, :].rearrange("p k (c r) -> p k c r", c=4),
                        weights(("win", i))[:, :, QR + KVR:].unsqueeze(2).broadcast_to([P, 4, 4, ROPE])).then_inc(packed, 1)
                wait_weights(pool, ("kvup", 0))
                nc.gpsimd.tensor_copy(k_nope_w.rearrange("p k (h d) -> p k h d", d=DH),
                                      weights(("kvup", 0)).rearrange("p k (h d) -> p k h d", d=2 * DH)[:, :, :, 0:DH]) \
                    .then_inc(packed, 1)
                for i in range(2):
                    wait_weights(pool, ("qup", i))
                    w = weights(("qup", i)).rearrange("p k (h d) -> p k h d", d=QK)
                    nc.gpsimd.tensor_copy(q_nope_w[:, :, 512 * i:512 * i + 512].rearrange("p k (h d) -> p k h d", d=DH),
                                          w[:, :, :, 0:DH])
                    ins = nc.gpsimd.tensor_copy(
                        q_rope_w[:, :, 256 * i:256 * i + 256].rearrange("p k (h d) -> p k h d", d=ROPE),
                        w[:, :, :, DH:QK])
                    ins.then_inc(packed, 1)

            gate_experts(0)
            pack_mixer1()
            gate_experts(1)

        @block.tensor
        def _(pe):
            tile_no = [0]

            def projection(lhs, rhs, ks, n=T, h_before=None):
                j = tile_no[0]
                if j >= 4:
                    pe.wait_ge(tile_kept[owner[j - 4]], nth[j - 4])
                tile_no[0] += 1
                for k in range(ks):
                    if h_before is not None:
                        pe.wait_ge(h_ready, h_before + k + 1)
                    mm = pe.matmul(banks[j % 4][:, 0:n], lhs(k), rhs(k), start=(k == 0), stop=(k == ks - 1))
                mm.then_inc(tile_done, 1)

            def sum_squares(tiles, squares, at=0, bank=6, ends=(0, KD - 1)):
                for n, k in enumerate(tiles):
                    pe.wait_ge(sq_ready, squares + n + 1)
                    mm = pe.matmul(banks[bank][:, at:at + T], ones[:, :], sq[:, k, :],
                                   start=(k == ends[0]), stop=(k == ends[1]), skip_group_check=True)
                if tiles[-1] == ends[1]:
                    mm.then_inc(ss_done, 1)

            def ada(a):
                phase = [a in phase for phase in phases].index(True)
                m = phases[phase].index(a)
                wait_weights(pe, a)
                if m == 0 and phase:
                    pe.wait_ge(ada_kept, phase)
                w = weights(a)
                for j in range(2):
                    for g in range(4):
                        k = 2 * g + j
                        mm = pe.matmul(banks[6][32 * g:32 * g + 32, :], c_pad[:, k, 31 - m:63 - m], w[:, k, :],
                                       start=(m == 0 and j == 0), stop=(a == phases[phase][-1] and j == 1),
                                       skip_group_check=True)
                mm.then_inc(ada_done, 1)

            def ada_columns(phase):
                n = len(phases[phase])
                pe.wait_ge(ada_kept, phase + 1)
                for j in range(4):
                    mm = pe.matmul(banks[7][:, j * n:(j + 1) * n], ada_rows[:, j * P:(j + 1) * P], row_sel[:, 0:n],
                                   start=True, stop=True)
                mm.then_inc(mod_done, 1)

            pe.wait_ge(consts, 2)
            pe.wait_ge(rows_loaded, 7 * 16)
            nA, nB = KD + 2 * MOD, 5 * KD + 5
            pe.transpose(banks[6][:, 0:nA], rowsA[0:nA, :], ident[0:nA, 0:nA])
            pe.transpose(banks[6][:, P:P + nB], rowsB[0:nB, :], ident[0:nB, 0:nB]).then_inc(rows_turned, 1)
            pe.wait_ge(x_loaded, 16)
            for b in range(4):
                for k in range(2):
                    for t in range(TT):
                        tr = pe.transpose(banks[b][:, k * T + t * P:k * T + (t + 1) * P],
                                          x_nat[:, t, (2 * b + k) * P:(2 * b + k + 1) * P], ident[:, :])
                tr.then_inc(x_turned, 1)
            pe.wait_ge(cols_ready, 1)
            pe.wait_ge(c_ready, 1)
            sum_squares(range(KD), 0, bank=5)
            pe.wait_ge(consts, 4)
            for a in phases[0]:
                ada(a)
            ada_columns(0)

            for n, (kind, half) in enumerate(qkv_order):
                wait_weights(pe, (kind, half))
                w = weights((kind, half))
                if kind == "v":
                    for t in range(TT):
                        projection(lambda k: hT[:, k, t * P:(t + 1) * P], lambda k: w[:, k, :], KD, 512)
                else:
                    for j in range(4):
                        projection(lambda k: w[:, k, j * P:(j + 1) * P], lambda k: hT[:, k, :], KD,
                                   h_before=0 if n == 0 and j == 0 else None)
                if n:
                    ada(phases[1][n - 1])

            def scores0(h):
                p, r = h // 2, 64 * (h % 2)
                z = banks[h % 4]
                if h >= 4:
                    pe.wait_ge(log_ready, h - 3)
                pe.matmul(z[:, 0:256], KT[r:r + 64, p, 0:P], QT[r:r + 64, p, :], start=True, stop=False,
                          skip_group_check=True)
                pe.matmul(z[:, 256:384], KT[r:r + 64, p, P:T], QT[r:r + 64, p, P:T], start=False, stop=False,
                          skip_group_check=True).then_inc(z_done, 1)

            def sticks(h):
                z, spm = banks[h % 4], sc[2][h % 2]
                pe.wait_ge(spm_ready, h + 1)
                pe.matmul(z[:, 0:256], neg_tri[:, :], spm[:, 0:256], start=False, stop=False, skip_group_check=True)
                pe.matmul(z[:, 128:256], neg_ones[:, :], spm[:, 256:384], start=False, stop=False,
                          skip_group_check=True)
                pe.matmul(z[:, 256:384], neg_tri[:, :], spm[:, 256:384], start=False, stop=True,
                          skip_group_check=True).then_inc(sticks_done, 1)

            def values(layer, p, ready):
                o = banks[4 + p % 2]
                pe.wait_ge(ready, 2 * p + 2)
                if 8 * layer + p >= 2:
                    pe.wait_ge(o_ready, 8 * layer + p - 1)
                for t in range(TT):
                    for h in (2 * p, 2 * p + 1):
                        r, a = 64 * (h % 2), weights_of(layer, h)
                        mm = pe.matmul(o[r:r + 64, t * P:T], V[:, t, h * DH:(h + 1) * DH],
                                       (a[:, 0:T], a[:, T:T + P])[t], start=(t == 0), stop=(t == 1),
                                       skip_group_check=True)
                        if t:
                            mm.then_inc(o_done, 1)

            wait_tiles(pe, TWO0 - 1)
            pe.wait_ge(consts, 5)
            ada_at = (0, 2, 4, 6, 8, 10, 12)
            for h in range(HEADS + 4):
                if h < HEADS:
                    scores0(h)
                if 2 <= h < HEADS + 2:
                    sticks(h - 2)
                if h >= 5 and h % 2 == 1:
                    values(0, (h - 5) // 2, a_ready)
                if h in ada_at:
                    ada(phases[1][5 + ada_at.index(h)])
            ada_columns(1)

            def out_projection(kind, layer, squares):
                pe.wait_ge(o_ready, 8 * (layer + 1))
                for i in range(2):
                    wait_weights(pe, (kind, i))
                    w = weights((kind, i))
                    for j in range(4):
                        projection(lambda k: w[:, k, j * P:(j + 1) * P], lambda k: OT[:, k, :], KD)
                        if 4 * i + j >= 2:
                            sum_squares([4 * i + j - 2], squares + 4 * i + j - 2)
                sum_squares([KD - 2, KD - 1], squares + KD - 2)

            out_projection("wo0", 0, 8)

            def moe(layer):
                pe.wait_ge(small_loaded, 160)
                for k in range(KD):
                    pe.wait_ge(h_ready, (8, 29)[layer] + k + 1)
                    for t in range(TT):
                        mm = pe.matmul(banks[7][:, t * 32:t * 32 + NG + NE], hT[:, k, t * P:(t + 1) * P],
                                       wr[:, layer, k, :], start=(k == 0 and t == 0), stop=(k == KD - 1),
                                       skip_group_check=True)
                mm.then_inc(logit_done, 1)
                for k in range(KD):
                    for t in range(TT):
                        tr = pe.transpose(banks[2 * t + k // 4][:, k % 4 * P:(k % 4 + 1) * P],
                                          hT[:, k, t * P:(t + 1) * P], ident[:, :])
                        if k % 4 == 3:
                            tr.then_inc(hn_turned, 1)
                pe.wait_ge(mask_ready, layer + 1)
                for t in range(TT):
                    at = banks[6][:, t * NE:(t + 1) * NE]
                    if t:
                        pe.matmul(at, ones[:, :], mask[:, 0, :], start=True, stop=False)
                    pe.matmul(at, strict[:, :], mask[:, t, :], start=(t == 0), stop=True)
                pe.matmul(banks[6][:, 32:32 + NE], ones[:, :], mask[:, 0, :], start=True, stop=False)
                pe.matmul(banks[6][:, 32:32 + NE], ones[:, :], mask[:, 1, :], start=False,
                          stop=True).then_inc(rank_done, 1)
                pe.wait_ge(most_ready, layer + 1)
                few = pe.value_load(most_i[0:1, 0:1], min_val=0, max_val=T)
                with pe.If(few > FEW):
                    pe.wait_ge(hn_ready, 4 * (layer + 1))
                    clear_accumulators()
                    dense_experts(layer)
                with pe.Else():
                    sparse_experts(layer)
                pe.drain().then_inc(acc_done, 1)

            def clear_accumulators():
                for b in range(4):
                    pe.matmul(banks[b][:, :], zeros[:, :], zeros[:, :].unsqueeze(1).broadcast_to([P, 4, P]),
                              start=True, stop=False, skip_group_check=True)

            def dense_experts(layer):
                q = per_layer[layer]
                def pair(i, last=False):
                    for b in range(2):
                        pe.wait_ge(q.diag_ready, i * 2 + (b + 1))
                        for t in range(TT):
                            mm = pe.matmul(banks[6][:, t * P:(t + 1) * P], ones[:, :], diag[:, t, :],
                                           start=True, stop=True)
                        mm.then_inc(q.gate_done, 1)
                        for part in range(2):
                            wait_expert(pe, layer, i, b, part)
                        if last:
                            pe.wait_ge(half_loaded[1][b], 16 * (layer + 1))
                        for f in range(4):
                            pe.wait_ge(q.gu_read, i * 8 + (4 * b + f + 1))
                            for u in range(2):
                                for k in range(KD):
                                    mm = pe.matmul(banks[4 + f % 2][:, u * T:(u + 1) * T],
                                                   gate_up_weights(i, b, k // 4)[:, k % 4,
                                                                                   u * FF + f * P:u * FF + (f + 1) * P],
                                                   hT[:, k, :], start=(k == 0), stop=(k == KD - 1))
                            mm.then_inc(gu_done, 1)
                        wait_expert(pe, layer, i, b, 2)
                        if last:
                            pe.wait_ge(half_loaded[2][b], 16 * (layer + 1))
                        for f in range(4):
                            pe.wait_ge(q.hg_ready, i * 8 + (4 * b + f + 1))
                            for d in range(KD):
                                mm = pe.matmul(banks[d // 2][:, (d % 2) * T:(d % 2 + 1) * T],
                                               DN[b][:, f, d * P:(d + 1) * P], hg[b][:, f, :],
                                               start=False, stop=False, skip_group_check=True)
                        mm.then_inc(down_done, 1)

                pair(0)
                pair(1)
                with pe.Fori(2, NE // 2 - 1) as i:
                    pair(i)
                pair(NE // 2 - 1, last=True)

            def gather(layer, i, half):
                q = per_layer[layer]
                for d in range(4):
                    for t in range(TT):
                        for part in range(2):
                            mm = pe.matmul(banks[5 - half][:, d * P:(d + 1) * P],
                                           tok[part][:, t, (4 * half + d) * P:(4 * half + d + 1) * P],
                                           pick[:, t, bass.ds(i * (2 * CAP), 2 * CAP)], start=(t + part == 0),
                                           stop=(t + part == 2))
                mm.then_inc(q.gathered, 1)

            def gate_up(layer, i, last=False):
                q = per_layer[layer]
                pe.wait_ge(q.xg_kept["v"], i + 1)
                pe.wait_ge(q.xg_kept["a"], i + 1)
                for k in range(KD):
                    for b in range(2):
                        if last and k == 4:
                            pe.wait_ge(half_loaded[1][b], 16 * (layer + 1))
                        elif k == 0 or k == (6 if last else 4):
                            wait_expert(pe, layer, i, b, k // 4)
                    for u in range(2):
                        for b in range(2):
                            mm = pe.matmul(banks[4 + u][CAP * b:CAP * (b + 1), :], XG[:, k, CAP * b:CAP * (b + 1)],
                                           gate_up_weights(i, b, k // 4)[:, k % 4, u * FF:(u + 1) * FF],
                                           start=(k == 0), stop=(k == KD - 1))
                    mm.then_inc(gu_done, 1)

            def turn_h(layer, i):
                q = per_layer[layer]
                pe.wait_ge(q.h_ready, i + 1)
                for f in range(4):
                    tr = pe.transpose(banks[4][:, f * P:(f + 1) * P], h_pair[:, f * P:(f + 1) * P], ident[:, :])
                tr.then_inc(q.h_turned, 1)

            def down(layer, i, first, last=False):
                q = per_layer[layer]
                pe.wait_ge(q.hT_ready, i + 1)
                if not first:
                    pe.wait_ge(q.y_done, i)
                for b in range(2):
                    if last:
                        pe.wait_ge(half_loaded[2][b], 16 * (layer + 1))
                    else:
                        wait_expert(pe, layer, i, b, 2)
                for f in range(4):
                    if last and f == 2:
                        for b in range(2):
                            wait_expert(pe, layer, i, b, 2)
                    for half in range(2):
                        for b in range(2):
                            mm = pe.matmul(banks[6 + half][CAP * b:CAP * (b + 1), :],
                                           hT_pair[:, f, CAP * b:CAP * (b + 1)],
                                           DN[b][:, f, 512 * half:512 * half + 512], start=(f == 0), stop=(f == 3))
                            if f == 3 and half == 1:
                                mm.then_inc(down_done, 1)

            def scatter(layer, i):
                first = isinstance(i, int) and i == 0
                if first:
                    pe.wait_ge(per_layer[layer].pick_T_kept["v"], 2)
                    pe.wait_ge(per_layer[layer].pick_T_kept["a"], 2)
                q = per_layer[layer]
                pe.wait_ge(q.y_done, i + 1)
                for part in range(2):
                    for d in range(KD):
                        mm = pe.matmul(banks[d // 2][:, (d % 2) * T:(d % 2 + 1) * T], Y[part][:, d * P:(d + 1) * P],
                                       pick_T[:, bass.ds(i, 1), :].rearrange("p a t -> p (a t)"),
                                       start=(first and part == 0 and d % 2 == 0), stop=False, skip_group_check=True)
                mm.then_inc(q.scattered, 1)

            def sparse_experts(layer):
                q = per_layer[layer]
                pe.wait_ge(pick_ready, layer + 1)
                pe.wait_ge(hn_ready, 4 * layer + 2)
                gather(layer, 0, 0)
                pe.wait_ge(hn_ready, 4 * (layer + 1))
                gather(layer, 0, 1)

                def slot_gates(pairs):
                    pe.wait_ge(gates_ready, layer + 1)
                    for p in pairs:
                        for t in range(TT):
                            mm = pe.matmul(banks[3][:, 2 * p:2 * p + 2], pick[:, t, p * P:(p + 1) * P].bitcast(F32),
                                           gates[:, t, 2 * p:2 * p + 2], start=(t == 0), stop=(t == 1))
                    if pairs[-1] == NE // 2 - 1:
                        mm.then_inc(q.slot_gate_done, 1)

                def turn_pick(b):
                    for n in range(4):
                        p, t = 2 * b + n // 2, n % 2
                        tr = pe.transpose(banks[b][:, n * P:(n + 1) * P],
                                          pick[:, t, p * P:(p + 1) * P].bitcast(F32), ident[:, :])
                    tr.then_inc(q.pick_turned, 1)

                def pair(i, first=False, last=False):
                    gate_up(layer, i, last)
                    if first:
                        slot_gates(range(NE // 4))
                    else:
                        scatter(layer, i - 1)
                    turn_h(layer, i)
                    if not last:
                        gather(layer, i + 1, 0)
                    if first:
                        down(layer, i, first)
                        slot_gates(range(NE // 4, NE // 2))
                    if not last:
                        pe.wait_ge(q.hT_ready, i + 1)
                        gather(layer, i + 1, 1)
                    if first:
                        for b in range(4):
                            if b == 3:
                                pe.wait_ge(q.slot_gate_ready, 1)
                            turn_pick(b)
                    else:
                        down(layer, i, first, last)

                pair(0, first=True)
                pair(1)
                with pe.Fori(2, NE // 2 - 1) as i:
                    pair(i)
                pair(NE // 2 - 1, last=True)
                scatter(layer, NE // 2 - 1)

            moe(0)

            sum_squares(range(KD), 16)
            for i in range(2):
                wait_weights(pe, ("win", i))
            win = [weights(("win", i)) for i in range(2)]
            for j in range(5):
                projection(lambda k: win[k // 4][:, k % 4, j * P:(j + 1) * P], lambda k: hT[:, k, :], KD,
                           h_before=16 if j == 0 else None)
            sum_squares(range(3), 24, ends=(0, 2))
            pe.wait_ge(packed, 2)
            projection(lambda k: k_rope_w[:, k, :], lambda k: hT[:, k, :], KD)
            sum_squares(range(3, 5), 27, bank=7, ends=(3, 4))
            pe.wait_ge(packed, 5)
            for p in range(8):
                projection(lambda k: q_nope_w[:, k, p * P:(p + 1) * P], lambda k: hT[:, k, :], 3,
                           h_before=24 if p == 0 else None)
            for g in range(4):
                projection(lambda k: q_rope_w[:, k, g * P:(g + 1) * P], lambda k: hT[:, k, :], 3)
            for g in range(5):
                wait_tiles(pe, TUP + 8 + g if g < 4 else TUP + 11)
                projection(lambda k: rot[:, :], lambda k: raw_rope[g], 1)
            wait_weights(pe, ("kvup", 0))
            pe.wait_ge(h_ready, 29)
            kvup = weights(("kvup", 0)).rearrange("p k (h d) -> p k h d", d=2 * DH)
            for p in range(8):
                projection(lambda k: k_nope_w[:, k, p * P:(p + 1) * P], lambda k: hT[:, 3 + k, :], 2)
            for t in range(TT):
                for half in range(2):
                    projection(lambda k: hT[:, 3 + k, t * P:(t + 1) * P],
                               lambda k: kvup[:, k, 8 * half:8 * half + 8, DH:2 * DH], 2, 512)

            def scores1(h):
                p, r, g, q = h // 2, 64 * (h % 2), h // 4, 32 * (h % 4)
                s = banks[h % 2]
                if h >= 2:
                    pe.wait_ge(masked_ready, 2 * (h - 1))
                pe.matmul(s[:, 0:P], QT[r:r + 64, p, 0:P], KT[r:r + 64, p, 0:P], start=True, stop=False,
                          skip_group_check=True)
                pe.matmul(s[:, P:384], QT[r:r + 64, p, P:T], KT[r:r + 64, p, :], start=False, stop=False,
                          skip_group_check=True)
                pe.matmul(s[:, 0:P], q_rope[g][q:q + 32, 0:P], k_rope[q:q + 32, 0:P], start=False, stop=False,
                          skip_group_check=True, tile_position=(q, 0))
                pe.matmul(s[:, P:384], q_rope[g][q:q + 32, P:T], k_rope[q:q + 32, :], start=False, stop=True,
                          skip_group_check=True, tile_position=(q, 0)).then_inc(s_done, 1)

            def turn(h):
                probs, pt = sc[1][h % 2], banks[2 + h % 2]
                pe.wait_ge(pn_ready, h + 1)
                if h >= 2:
                    pe.wait_ge(aT_ready, h - 1)
                for n in range(3):
                    tr = pe.transpose(pt[:, n * P:(n + 1) * P], probs[:, n * P:(n + 1) * P], ident[:, :])
                tr.then_inc(pt_done, 1)

            wait_tiles(pe, TWO1 - 1)
            pe.wait_ge(rope_ready, 5)
            ada_at = (1, 3, 5, 7, 9, 11, 13, 15)
            for h in range(HEADS + 3):
                if h < HEADS:
                    scores1(h)
                if 2 <= h < HEADS + 2:
                    turn(h - 2)
                if h >= 4 and h % 2 == 0:
                    values(1, (h - 4) // 2, aT_ready)
                if h in ada_at:
                    ada(phases[2][ada_at.index(h)])
            ada_columns(2)
            out_projection("wo1", 1, 29)
            moe(1)
            pe.wait_ge(x_ready, 20)
            for k in range(KD):
                pe.wait_ge(gained_ready, k + 1)
                for t in range(TT):
                    tr = pe.transpose(banks[2 * t + k // 4][:, k % 4 * P:(k % 4 + 1) * P],
                                      hT[:, k, t * P:(t + 1) * P], ident[:, :])
                pe.wait_ge(sq_ready, 37 + k + 1)
                for t in range(TT):
                    mm = pe.matmul(banks[6][:, t:t + 1], sq[:, k, t * P:(t + 1) * P], ones[:, 0:1],
                                   start=(k == 0 and t == 0), stop=(k == KD - 1), skip_group_check=True)
            mm.then_inc(y_turned, 1)

        def qkv_place(j):
            half, r = j // 10, j % 10
            if r < 4:
                return KT[:, 4 * half + r, :], T, 1.0
            if r < 8:
                return QT[:, 4 * half + r - 4, :], T, DH ** -0.5
            return V[:, r - 8, 512 * half:512 * half + 512], 512, 1.0

        def latent_place(j):
            if j < TUP:
                return lat[:, j - TLAT, :], T
            if j < TUP + 8:
                return QT[:, j - TUP, :], T
            if j < TROT:
                return raw_rope[j - TUP - 8], T
            if j < TKV + 8:
                return KT[:, j - TKV, :], T
            n = j - TKV - 8
            return V[:, n // 2, 512 * (n % 2):512 * (n % 2) + 512], 512

        @block.vector
        def _(dve):
            v = nc.vector
            links = [0]

            def link(ins):
                links[0] += 1
                ins.then_inc(dve_chain, 1)
                dve.wait_ge(dve_chain, links[0])

            dve.wait_ge(rows_turned, 1)
            v.tensor_copy(colA[:, :], banks[6][:, 0:KD + 2 * MOD])
            v.tensor_copy(colB[:, :], banks[6][:, P:P + 5 * KD + 5]).then_inc(cols_ready, 1)
            dve.wait_ge(cols_ready, 1)
            for b in range(4):
                dve.wait_ge(x_turned, b + 1)
                v.tensor_copy(xT[:, 2 * b:2 * b + 2, :], banks[b][:, :].rearrange("p (k t) -> p k t", k=2)) \
                    .then_inc(x_ready, 1)

            def mean_square(number, d, at=0, bank=6):
                dve.wait_ge(ss_done, number)
                v.tensor_scalar(rstd[:, at // T, :], banks[bank][:, 0:T], 1.0 / d, EPS, ALU.mult,
                                ALU.add).then_inc(ms_ready, 1)

            def norm(number, bank=6):
                mean_square(number, D, 0, bank)
                dve.wait_ge(std_ready, number)
                link(v.reciprocal(rstd[:, 0, :], rstd[:, 0, :]))
                for k in range(KD):
                    v.tensor_tensor(hT[:, k, :], xT[:, k, :], rstd[:, 0, :], ALU.mult).then_inc(scaled_ready, 1)

            def take_columns(phase):
                n = len(phases[phase])
                dve.wait_ge(ada_done, ada_no[phases[phase][-1]] + 1)
                v.tensor_copy(ada_rows[:, :], banks[6][:, :]).then_inc(ada_kept, 1)
                dve.wait_ge(mod_done, phase + 1)
                got = banks[7][:, 0:4 * n].rearrange("p (j m) -> p m j", j=4)
                at = 0
                for layer in range(2):
                    mine = [i for kind, i in phases[phase] if kind == f"ada{layer}"]
                    if mine:
                        a, b = 4 * mine[0], 4 * mine[-1] + 4
                        bias = colA[:, KD + MOD * layer:KD + MOD * (layer + 1)]
                        link(v.tensor_tensor(mod[:, layer, a:b].rearrange("p (m j) -> p m j", j=4),
                                             got[:, at:at + len(mine), :],
                                             bias[:, a:b].rearrange("p (m j) -> p m j", j=4), ALU.add))
                        at += len(mine)

            def set_gain(slot, layer, scale_at, g):
                link(v.scalar_tensor_tensor(out=gs[:, slot, :], in0=mod[:, layer, scale_at:scale_at + KD], scalar=1.0,
                                            in1=g, op0=ALU.add, op1=ALU.mult))

            def mod_signal():
                v.memset(most[:, :], 0.0).then_inc(mod_ready, 1)

            dve.wait_ge(x_ready, 4)
            norm(1, bank=5)
            take_columns(0)
            set_gain(0, 0, 8, colB[:, 0:8])
            mod_signal()

            dve.wait_ge(small_loaded, 160)
            link(v.tensor_copy(ang, pos_i))
            link(v.tensor_scalar(ang, ang, freq[:, 0:1], None, ALU.mult))
            link(v.tensor_scalar(turns, ang, float(1.0 / (2 * np.pi)), None, ALU.mult))
            link(v.tensor_scalar(turns, turns, 1.5 * 2.0 ** 23, None, ALU.add))
            link(v.tensor_scalar(turns, turns, 1.5 * 2.0 ** 23, None, ALU.subtract))
            c1 = 6.28125
            c2 = float(np.floor((2 * np.pi - c1) * 2.0 ** 21) / 2.0 ** 21)
            c3 = float(2 * np.pi - c1 - c2)
            for part in (c1, c2, c3):
                link(v.scalar_tensor_tensor(out=ang, in0=turns, scalar=-part, in1=ang, op0=ALU.mult, op1=ALU.add))
            pi = float(np.nextafter(np.float32(np.pi), np.float32(0)))
            v.tensor_scalar(ang, ang, pi, -pi, ALU.min, ALU.max).then_inc(trig_in, 1)
            dve.wait_ge(trig_in, 1)
            link(v.scalar_tensor_tensor(out=turns, in0=ang, scalar=-1.0, in1=ang, op0=ALU.mult, op1=ALU.max))
            v.tensor_scalar(turns, turns, -1.0, float(np.pi / 2), ALU.mult, ALU.add).then_inc(trig_in, 1)

            for j in range(TWO0):
                if owner[j] == "v":
                    dst, n, scale = qkv_place(j)
                    dve.wait_ge(tile_done, j + 1)
                    v.tensor_scalar(dst, banks[j % 4][:, 0:n], scale, None, ALU.mult).then_inc(tile_kept["v"], 1)

            def log_a(h):
                dve.wait_ge(sticks_done, h + 1)
                if h >= 2:
                    dve.wait_ge(a_ready, h - 1)
                v.scalar_tensor_tensor(out=sc[4][h % 2][:, :], in0=banks[h % 4][:, 0:384], scalar=0.0,
                                       in1=bias_strict[:, :], op0=ALU.min, op1=ALU.add).then_inc(log_ready, 1)

            def softplus(h):
                dve.wait_ge(soft_ready, h + 1)
                if h >= 2:
                    dve.wait_ge(sticks_done, h - 1)
                v.scalar_tensor_tensor(out=sc[2][h % 2][:, :], in0=banks[h % 4][:, 0:384], scalar=0.0,
                                       in1=sc[1][h % 2][:, :], op0=ALU.max, op1=ALU.add).then_inc(sp_ready, 1)

            def keep_o(layer, p):
                dve.wait_ge(o_done, 16 * layer + 2 * p + 2)
                v.tensor_copy(OT[:, p, :], banks[4 + p % 2][:, 0:T]).then_inc(o_ready, 1)

            dve.wait_ge(consts, 5)
            dve.wait_ge(trig_ready, 2)
            for h in range(HEADS + 5):
                if 3 <= h < HEADS + 3:
                    log_a(h - 3)
                if 1 <= h <= HEADS:
                    softplus(h - 1)
                if h >= 6 and h % 2 == 0:
                    keep_o(0, (h - 6) // 2)
            take_columns(1)
            set_gain(1, 0, 32, colB[:, 16:24])
            set_gain(2, 1, 8, colB[:, 8:16])
            mod_signal()

            def residual_tiles(first, layer, ready):
                for d in range(KD):
                    j = first + d
                    dve.wait_ge(tile_done, j + 1)
                    v.scalar_tensor_tensor(out=xT[:, d, :], in0=banks[j % 4][:, 0:T],
                                           scalar=mod[:, layer, 16 + d:17 + d], in1=xT[:, d, :],
                                           op0=ALU.mult, op1=ALU.add).then_inc(tile_kept["v"], 1)
                dve.wait_ge(tile_kept["v"], nth[first + KD - 1])

            residual_tiles(TWO0, 0, 8)

            def field(n, *dims):
                at = sc[3 + n // 12][0][:, (n % 12) * 32:(n % 12) * 32 + 32].rearrange("p (t n) -> p t n", t=TT)
                return at[:, :, 0:dims[0]] if dims else at[:, :, 0]

            def spread(a, n):
                return a.unsqueeze(2).broadcast_to([P, TT, n])

            def first_of(hot, vals, top):
                eq, best = field(0, 4), field(1)
                link(v.tensor_tensor(eq, vals, spread(top, 4), ALU.is_equal))
                link(v.tensor_tensor(eq, eq, prio[:, :].unsqueeze(1).broadcast_to([P, TT, 4]), ALU.mult))
                link(v.tensor_reduce(best, eq, AX.X, ALU.max))
                link(v.tensor_tensor(hot, eq, spread(best, 4), ALU.is_equal))

            def by_group(a):
                return a.rearrange("p t (g j) -> p t g j", g=NG)

            def moe(layer):
                norm((2, 6)[layer])
                dve.wait_ge(logit_done, layer + 1)
                link(v.tensor_tensor(lg[:, :, :],
                                     banks[7][:, 0:64].rearrange("p (t n) -> p t n", t=2)[:, :, 0:NG + NE],
                                     br[:, layer, :].unsqueeze(1).broadcast_to([P, TT, NG + NE]), ALU.add))
                g, e = lg[:, :, 0:NG], lg[:, :, NG:]
                gmax, group, picked, ein = field(2), field(3, 4), field(4, 16), field(5, 4)
                m1, m2, hot1, hot2, rest, both = field(6), field(7), field(8, 4), field(9, 4), field(10, 4), field(11, 4)
                gdiff, gexp, mdiff, mexp = field(12, 4), field(13, 4), field(14), field(15)
                gsum, w1, w2 = field(16), field(17), field(18)
                link(v.tensor_reduce(gmax, g, AX.X, ALU.max))
                v.tensor_tensor(gdiff, g, spread(gmax, NG), ALU.subtract).then_inc(route_in, 1)
                first_of(group, g, gmax)
                link(v.tensor_tensor(by_group(picked), by_group(e),
                                     group.unsqueeze(3).broadcast_to([P, TT, NG, EPG]), ALU.mult))
                link(v.tensor_reduce(ein, picked.rearrange("p t (g j) -> p t j g", g=NG), AX.X, ALU.add))
                link(v.tensor_reduce(m1, ein, AX.X, ALU.max))
                first_of(hot1, ein, m1)
                link(v.scalar_tensor_tensor(out=rest, in0=hot1, scalar=NEG, in1=ein, op0=ALU.mult, op1=ALU.add))
                link(v.tensor_reduce(m2, rest, AX.X, ALU.max))
                first_of(hot2, rest, m2)
                v.tensor_tensor(mdiff, m2, m1, ALU.subtract).then_inc(route_in, 1)
                link(v.tensor_tensor(both, hot1, hot2, ALU.add))
                v.tensor_tensor(by_group(mask[:, :, :]), both.unsqueeze(2).broadcast_to([P, TT, NG, EPG]),
                                group.unsqueeze(3).broadcast_to([P, TT, NG, EPG]), ALU.mult).then_inc(mask_ready, 1)
                def low_part(n):
                    half, t = n // 2, n % 2
                    dve.wait_ge(hn_high, 4 * layer + n + 1)
                    v.tensor_tensor(tok[1][:, t, 512 * half:512 * half + 512], banks[2 * t + half][:, :],
                                    tok[0][:, t, 512 * half:512 * half + 512].bitcast(F32),
                                    ALU.subtract).then_inc(hn_ready, 1)

                low_part(0)
                low_part(1)
                dve.wait_ge(rank_done, layer + 1)
                link(v.tensor_reduce(most[:, :], banks[6][:, 32:32 + NE], AX.X, ALU.max))
                v.tensor_copy(most_i[:, :], most[:, :]).then_inc(most_ready, 1)
                rank = field(19, 16)
                v.scalar_tensor_tensor(out=rank, in0=banks[6][:, 0:32].rearrange("p (t n) -> p t n", t=TT),
                                       scalar=1.0, in1=mask[:, :, :], op0=ALU.add, op1=ALU.mult).then_inc(rank_ready, 1)
                dve.wait_ge(rank_ready, layer + 1)
                for t in range(TT):
                    ins = v.tensor_tensor(pick[:, t, :].rearrange("p (e s) -> p e s", e=NE),
                                          rank[:, t, :].unsqueeze(2).broadcast_to([P, NE, CAP]),
                                          slot_no[:, :].unsqueeze(1).broadcast_to([P, NE, CAP]), ALU.is_equal)
                ins.then_inc(pick_ready, 1)
                low_part(2)
                low_part(3)
                dve.wait_ge(route_out, 2 * layer + 2)
                link(v.tensor_reduce(gsum, gexp, AX.X, ALU.add))
                link(v.scalar_tensor_tensor(out=w1, in0=mexp, scalar=1.0, in1=gsum, op0=ALU.add, op1=ALU.mult))
                link(v.reciprocal(w1, w1))
                link(v.tensor_tensor(w2, w1, mexp, ALU.mult))
                link(v.tensor_tensor(hot1, hot1, spread(w1, 4), ALU.mult))
                link(v.tensor_tensor(hot2, hot2, spread(w2, 4), ALU.mult))
                link(v.tensor_tensor(hot1, hot1, hot2, ALU.add))
                v.tensor_tensor(by_group(gates[:, :, :]), hot1.unsqueeze(2).broadcast_to([P, TT, NG, EPG]),
                                group.unsqueeze(3).broadcast_to([P, TT, NG, EPG]), ALU.mult).then_inc(gates_ready, 1)
                dve.wait_ge(gates_ready, layer + 1)
                dve.wait_ge(most_ready, layer + 1)
                few = dve.value_load(most_i[0:1, 0:1], min_val=0, max_val=T)
                with dve.If(few > FEW):
                    dense_experts(layer)
                with dve.Else():
                    sparse_experts(layer)
                dve.wait_ge(acc_done, layer + 1)
                for d in range(KD):
                    v.scalar_tensor_tensor(out=xT[:, d, :], in0=banks[d // 2][:, (d % 2) * T:(d % 2 + 1) * T],
                                           scalar=mod[:, layer, 40 + d:41 + d], in1=xT[:, d, :],
                                           op0=ALU.mult, op1=ALU.add).then_inc(x_ready, 1)
                dve.wait_ge(x_ready, 4 + 8 * (layer + 1))

            def dense_experts(layer):
                q = per_layer[layer]
                for n in range(2):
                    v.memset(most[64 * n:64 * n + 64, :], 0.0).then_inc(q.gu_read, 1)
                with dve.Fori(0, NE // 2) as i:
                    for b in range(2):
                        v.tensor_tensor(diag, ident[:, :].unsqueeze(1).broadcast_to([P, TT, P]),
                                        gates[:, :, bass.ds(i * 2 + b, 1)].broadcast_to([P, TT, P]),
                                        ALU.mult).then_inc(q.diag_ready, 1)
                        dve.wait_ge(q.gate_done, i * 2 + (b + 1))
                        v.tensor_copy(gate_row[b], banks[6][:, 0:T]).then_inc(q.gate_ready, 1)
                        for f in range(4):
                            dve.wait_ge(q.silu_ready, i * 8 + (4 * b + f + 1))
                            v.tensor_tensor(hg[b][:, f, :], silu[f % 2], banks[4 + f % 2][:, T:2 * T],
                                            ALU.mult).then_inc(q.gu_read, 1)

            def sparse_experts(layer):
                q = per_layer[layer]
                def keep_pick(b):
                    dve.wait_ge(q.pick_turned, b + 1)
                    v.tensor_copy(pick_T[:, 2 * b:2 * b + 2, :], banks[b][:, :].rearrange("p (a t) -> p a t", a=2)) \
                        .then_inc(q.pick_T_kept["v"], 1)

                def keep_gathered(i):
                    dve.wait_ge(q.gathered, i * 2 + 1)
                    v.tensor_copy(XG[:, 0:4, :], banks[5][:, :].rearrange("p (k s) -> p k s", k=4)) \
                        .then_inc(q.xg_kept["v"], 1)

                def pair(i, first=False, last=False):
                    dve.wait_ge(q.act_ready, i + 1)
                    v.tensor_tensor(h_pair, silu_pair, banks[5][:, :], ALU.mult).then_inc(q.h_ready, 1)
                    dve.wait_ge(q.h_turned, i + 1)
                    v.tensor_copy(hT_pair, banks[4][:, :].rearrange("p (f s) -> p f s", f=4)).then_inc(q.hT_ready, 1)
                    if not last:
                        keep_gathered(i + 1)
                    if first:
                        dve.wait_ge(q.slot_gate_done, 1)
                        for b in range(2):
                            rows = slice(CAP * b, CAP * (b + 1))
                            ins = v.tensor_copy(slot_gate[rows, :], banks[3][rows, b:NE:2])
                        ins.then_inc(q.slot_gate_ready, 1)
                    for half in range(2):
                        dve.wait_ge(q.y_high, i * 2 + (half + 1))
                        ins = v.scalar_tensor_tensor(
                            out=Y[1][:, 512 * half:512 * half + 512], in0=banks[6 + half][:, :],
                            scalar=slot_gate[:, bass.ds(i, 1)],
                            in1=Y[0][:, 512 * half:512 * half + 512].bitcast(F32), op0=ALU.mult, op1=ALU.subtract)
                    ins.then_inc(q.y_done, 1)
                    if first:
                        keep_pick(0)
                        keep_pick(2)

                keep_gathered(0)
                pair(0, first=True)
                with dve.Fori(1, NE // 2 - 1) as i:
                    pair(i)
                pair(NE // 2 - 1, last=True)

            moe(0)
            norm(3)

            def keep(lo, hi):
                for j in range(lo, hi):
                    if owner[j] == "v":
                        dst, n = latent_place(j)
                        dve.wait_ge(tile_done, j + 1)
                        v.tensor_copy(dst, banks[j % 4][:, 0:n]).then_inc(tile_kept["v"], 1)

            keep(TLAT, TUP)
            mean_square(4, QR)
            dve.wait_ge(std_ready, 4)
            link(v.reciprocal(rstd[:, 0, :], rstd[:, 0, :]))
            dve.wait_ge(tile_done, TUP)
            for k in range(5):
                if k == 3:
                    mean_square(5, KVR, T, bank=7)
                    dve.wait_ge(std_ready, 5)
                    link(v.reciprocal(rstd[:, 1, :], rstd[:, 1, :]))
                v.scalar_tensor_tensor(out=hT[:, k, :], in0=lat[:, k, :], scalar=colB[:, 40 + k:41 + k],
                                       in1=rstd[:, 0 if k < 3 else 1, :], op0=ALU.mult,
                                       op1=ALU.mult).then_inc(h_ready, 1)
            keep(TUP, TROT)
            for g in range(5):
                j = TROT + g
                dve.wait_ge(tile_done, j + 1)
                dst = q_rope[g] if g < 4 else k_rope[:, :]
                v.tensor_tensor(sin_part, banks[j % 4][:, 0:T], sinT[:, :], ALU.mult).then_inc(tile_kept["v"], 1)
                dve.wait_ge(tile_kept["v"], nth[j])
                link(v.tensor_tensor(dst, raw_rope[g], cosT[:, :], ALU.mult))
                v.tensor_tensor(dst, dst, sin_part, ALU.add).then_inc(rope_ready, 1)
                dve.wait_ge(rope_ready, g + 1)
            keep(TKV, TWO1)
            spans = [(0, P), (P, 384)]

            def mask_max(h):
                dve.wait_ge(s_done, h + 1)
                if h >= 2:
                    dve.wait_ge(p_ready, 2 * (h - 1))
                for m, (a, b) in enumerate(spans):
                    v.tensor_tensor_reduce(out=sc[0][h % 2][:, a:b], in0=banks[h % 2][:, a:b],
                                           in1=bias_causal[:, a:b], scale=float(QK ** -0.5), scalar=NEG, op0=ALU.add,
                                           op1=ALU.max, accum_out=st[h % 2][:, m:m + 1]).then_inc(masked_ready, 1)
                dve.wait_ge(masked_ready, 2 * (h + 1))
                v.tensor_scalar(st[h % 2][:, 2:4], st[h % 2][:, 0:2], -1.0, None, ALU.mult).then_inc(neg_ready, 1)

            def normalise(h):
                dve.wait_ge(p_ready, 2 * (h + 1))
                link(v.reciprocal(st[h % 2][:, 6:8], st[h % 2][:, 4:6]))
                for m, (a, b) in enumerate(spans):
                    ins = v.tensor_scalar(sc[1][h % 2][:, a:b], sc[1][h % 2][:, a:b], st[h % 2][:, 6 + m:7 + m], None,
                                          ALU.mult)
                ins.then_inc(pn_ready, 1)

            for h in range(HEADS + 5):
                if h < HEADS:
                    mask_max(h)
                if 1 <= h <= HEADS:
                    normalise(h - 1)
                if h >= 5 and h % 2 == 1:
                    keep_o(1, (h - 5) // 2)
            take_columns(2)
            set_gain(3, 1, 32, colB[:, 24:32])
            mod_signal()
            residual_tiles(TWO1, 1, 16)
            moe(1)
            for k in range(KD):
                v.tensor_scalar(hT[:, k, :], xT[:, k, :], colB[:, 32 + k:33 + k], None,
                                ALU.mult).then_inc(gained_ready, 1)
            dve.wait_ge(y_turned, 1)
            v.tensor_scalar(rstd[:, 0, 0:TT], banks[6][:, 0:TT], 1.0 / D, EPS, ALU.mult, ALU.add).then_inc(ms_ready, 1)
            dve.wait_ge(std_ready, 7)
            v.reciprocal(rstd[:, 1, 0:TT], rstd[:, 0, 0:TT]).then_inc(scale_ready, 1)
            dve.wait_ge(scale_ready, 1)
            for half in range(2):
                v.tensor_scalar(V[:, 0, 512 * half:512 * half + 512], banks[half][:, :], rstd[:, 1, 0:1], None,
                                ALU.mult).then_inc(y_ready, 1)

        @block.scalar
        def _(act):
            s = nc.scalar
            links = [0]

            def link(ins):
                links[0] += 1
                ins.then_inc(act_chain, 1)
                act.wait_ge(act_chain, links[0])

            act.preload_act_table_set("silu_and_others")
            act.wait_ge(cols_ready, 1)
            act.wait_ge(consts, 3)
            s.activation(c_pad[:, :, 31], colA[:, 0:8], ACT.Silu).then_inc(c_ready, 1)

            def squares(ready, counts):
                for k in range(KD):
                    act.wait_ge(ready, counts[k])
                    s.activation(sq[:, k, :], xT[:, k, :], ACT.Square).then_inc(sq_ready, 1)

            def modulate(norm, gain, shift, moded, after=None):
                if after:
                    act.preload_act_table_set(after)
                act.wait_ge(mod_ready, moded)
                for k in range(KD):
                    act.wait_ge(scaled_ready, KD * norm + k + 1)
                    s.activation(hT[:, k, :], hT[:, k, :], ACT.Identity, scale=gain[:, k:k + 1],
                                 bias=shift[:, k:k + 1]).then_inc(h_ready, 1)

            def root(number, at=0):
                act.wait_ge(ms_ready, number)
                s.activation(rstd[:, at // T, :], rstd[:, at // T, :], ACT.Sqrt).then_inc(std_ready, 1)

            act.wait_ge(x_turned, 4)
            squares(x_ready, [k // 2 + 1 for k in range(KD)])
            act.preload_act_table_set("sqrt_and_others")
            root(1)
            modulate(0, gs[:, 0, :], mod[:, 0, 0:8], 1, "silu_and_others")
            act.wait_ge(trig_in, 2)
            s.activation(sinT[:, :], ang, ACT.Sin).then_inc(trig_ready, 1)
            s.activation(cosT[:, :], turns, ACT.Sin).then_inc(trig_ready, 1)
            for j in range(TWO0):
                if owner[j] == "a":
                    dst, n, scale = qkv_place(j)
                    act.wait_ge(tile_done, j + 1)
                    s.activation(dst, banks[j % 4][:, 0:n], ACT.Copy, scale=scale).then_inc(tile_kept["a"], 1)

            act.preload_act_table_set("natural_log_exp_and_others")
            act.wait_ge(consts, 5)
            for h in range(HEADS + 3):
                if h < HEADS:
                    e = sc[1][h % 2][:, :]
                    act.wait_ge(z_done, h + 1)
                    if h >= 2:
                        act.wait_ge(sp_ready, h - 1)
                    link(s.activation(e, banks[h % 4][:, 0:384], ACT.Abs))
                    link(s.activation(e, e, ACT.Exp, scale=-1.0))
                    s.activation(e, e, ACT.Ln, bias=1.0).then_inc(soft_ready, 1)
                if h >= 3:
                    g = h - 3
                    act.wait_ge(log_ready, g + 1)
                    if g >= 4:
                        act.wait_ge(o_done, g - 3)
                    s.activation(weights_of(0, g), sc[4][g % 2][:, :], ACT.Exp).then_inc(a_ready, 1)

            def moe(layer):
                first_tile = (TWO0, TWO1)[layer]
                act.preload_act_table_set("sqrt_and_others")
                squares(tile_kept["v"], [nth[first_tile + k] for k in range(KD)])
                root((2, 6)[layer])
                modulate((1, 3)[layer], gs[:, 1 + 2 * layer, :], mod[:, layer, 24:32], (2, 3)[layer], "exp_and_others")
                act.wait_ge(route_in, 2 * layer + 1)
                s.activation(sc4_field(1), sc4_field(0), ACT.Exp).then_inc(route_out, 1)
                for n in range(4):
                    half, t = n // 2, n % 2
                    act.wait_ge(hn_turned, 4 * layer + n + 1)
                    s.activation(tok[0][:, t, 512 * half:512 * half + 512], banks[2 * t + half][:, :],
                                 ACT.Copy).then_inc(hn_high, 1)
                act.wait_ge(route_in, 2 * layer + 2)
                s.activation(sc4_field(3)[:, :, 0], sc4_field(2)[:, :, 0], ACT.Exp).then_inc(route_out, 1)
                act.wait_ge(most_ready, layer + 1)
                few = act.value_load(most_i[0:1, 0:1], min_val=0, max_val=T)
                act.preload_act_table_set("silu_and_others")
                with act.If(few > FEW):
                    dense_experts(layer)
                with act.Else():
                    sparse_experts(layer)

            def sc4_field(n):
                at = sc[4][0][:, n * 32:n * 32 + 32].rearrange("p (t n) -> p t n", t=TT)
                return at[:, :, 0:4]

            def dense_experts(layer):
                q = per_layer[layer]
                with act.Fori(0, NE // 2) as i:
                    for b in range(2):
                        for f in range(4):
                            act.wait_ge(gu_done, i * 8 + (64 * layer + 4 * b + f + 1))
                            act.wait_ge(q.gu_read, i * 8 + (4 * b + f + 1))
                            s.activation(silu[f % 2], banks[4 + f % 2][:, 0:T], ACT.Silu).then_inc(q.silu_ready, 1)

            def sparse_experts(layer):
                q = per_layer[layer]

                def keep_pick(b):
                    act.wait_ge(q.pick_turned, b + 1)
                    s.activation(pick_T[:, 2 * b:2 * b + 2, :], banks[b][:, :].rearrange("p (a t) -> p a t", a=2),
                                 ACT.Copy).then_inc(q.pick_T_kept["a"], 1)

                def keep_gathered(i):
                    act.wait_ge(q.gathered, i * 2 + 2)
                    s.activation(XG[:, 4:8, :], banks[4][:, :].rearrange("p (k s) -> p k s", k=4),
                                 ACT.Copy).then_inc(q.xg_kept["a"], 1)

                def pair(i, first=False, last=False):
                    act.wait_ge(gu_done, i * 8 + (64 * layer + 8))
                    s.activation(silu_pair, banks[4][:, :], ACT.Silu).then_inc(q.act_ready, 1)
                    if not last:
                        keep_gathered(i + 1)
                    act.wait_ge(down_done, i * 2 + (NE * layer + 2))
                    if first:
                        act.wait_ge(q.slot_gate_ready, 1)
                    else:
                        act.wait_ge(q.scattered, i)
                    for half in range(2):
                        s.activation(Y[0][:, 512 * half:512 * half + 512], banks[6 + half][:, :], ACT.Copy,
                                     scale=slot_gate[:, bass.ds(i, 1)]).then_inc(q.y_high, 1)
                    if first:
                        keep_pick(1)
                        keep_pick(3)

                keep_gathered(0)
                pair(0, first=True)
                with act.Fori(1, NE // 2 - 1) as i:
                    pair(i)
                pair(NE // 2 - 1, last=True)

            moe(0)
            act.preload_act_table_set("sqrt_and_others")
            squares(x_ready, [4 + k + 1 for k in range(KD)])
            root(3)
            modulate(2, gs[:, 2, :], mod[:, 1, 0:8], 2)

            def keep(lo, hi):
                for j in range(lo, hi):
                    if owner[j] == "a":
                        dst, n = latent_place(j)
                        act.wait_ge(tile_done, j + 1)
                        s.activation(dst, banks[j % 4][:, 0:n], ACT.Copy).then_inc(tile_kept["a"], 1)

            keep(TLAT, TUP - 1)
            for k in range(5):
                if k == 3:
                    root(4)
                    keep(TUP - 1, TUP)
                act.wait_ge(tile_kept[owner[TLAT + k]], nth[TLAT + k])
                s.activation(sq[:, k, :], lat[:, k, :], ACT.Square).then_inc(sq_ready, 1)
            root(5, T)
            act.preload_act_table_set("exp_and_others")
            keep(TUP, TROT)
            keep(TKV, TWO1)
            for h in range(HEADS + 2):
                if h < HEADS:
                    act.wait_ge(neg_ready, h + 1)
                    if h >= 2:
                        act.wait_ge(pt_done, h - 1)
                    for m, (a, b) in enumerate([(0, P), (P, 384)]):
                        s.activation(sc[1][h % 2][:, a:b], sc[0][h % 2][:, a:b], ACT.Exp,
                                     bias=st[h % 2][:, 2 + m:3 + m],
                                     accum_out=st[h % 2][:, 4 + m:5 + m]).then_inc(p_ready, 1)
                if h >= 2:
                    g = h - 2
                    act.wait_ge(pt_done, g + 1)
                    if g >= 4:
                        act.wait_ge(o_done, HEADS + g - 3)
                    s.activation(weights_of(1, g), banks[2 + g % 2][:, 0:384], ACT.Copy).then_inc(aT_ready, 1)
            moe(1)
            act.preload_act_table_set("sqrt_and_others")
            squares(x_ready, [12 + k + 1 for k in range(KD)])
            act.wait_ge(ms_ready, 7)
            s.activation(rstd[:, 0, 0:TT], rstd[:, 0, 0:TT], ACT.Sqrt).then_inc(std_ready, 1)
            act.wait_ge(scale_ready, 1)
            for half in range(2):
                s.activation(V[:, 1, 512 * half:512 * half + 512], banks[2 + half][:, :], ACT.Copy,
                             scale=rstd[:, 1, 1:2]).then_inc(y_ready, 1)


_INS = ["x", "c", "positions", "norm_mix_g", "norm_ffn_g", "ada_w", "ada_b", "sb_w_qkv", "sb_w_o",
        "mla_w_in", "mla_g_q", "mla_g_kv", "mla_w_q_up", "mla_w_kv_up", "mla_w_o",
        "moe_w_group", "moe_b_group", "moe_w_router", "moe_b_router", "moe_w_gate_up", "moe_w_down", "final_g"]


def kernel(**inputs):
    import numpy as _np
    import concourse.bacc as _bacc
    from concourse import mybir as _mybir
    from concourse.bass_utils import run_bass_kernel_spmd as _run

    nc = _bacc.Bacc("TRN2", target_bir_lowering=False, num_devices=1)
    arrays, args = {}, []
    for name in _INS:
        arrays[f"in_{name}"] = _np.ascontiguousarray(inputs[name])
    half = _np.arange(0, ROPE, 2, dtype=_np.float32) / _np.float32(ROPE)
    arrays["in_inv_freq"] = _np.tile(_np.float32(THETA) ** (-half), 2 * P // ROPE).astype(_np.float32)
    for name, a in arrays.items():
        args.append(nc.dram_tensor(name, a.shape, _mybir.dt.from_np(a.dtype), kind="ExternalInput").ap())
    args.append(nc.dram_tensor("out_0", (1, T, D), _mybir.dt.float32, kind="ExternalOutput").ap())
    build(nc, *args)
    r = _run(nc, [arrays], core_ids=[0])
    return r.results[0]["out_0"]
```
